# Optimizing a Trainium2 kernel written in Bass

```python
import jax, jax.numpy as jnp
from jax import lax
import numpy as np

D_MODEL = 1024
BATCH = 1
SEQ = 1024
DEPTH = 1

CHUNK = 64
EPS = 1e-6
GLA_HEADS = 4
GLA_DK = D_MODEL // 8
GLA_DV = D_MODEL // 4
GLA_GATE_RANK = 16
GLA_TAU = 16.0
RET_HEADS = 4
RET_DK = D_MODEL // 4
RET_DV = D_MODEL // 2
ROPE_BASE = 10000.0
D_FF = 2816
CONV_W = 3

GLA_QK = GLA_HEADS * GLA_DK
GLA_V = GLA_HEADS * GLA_DV
RET_QK = RET_HEADS * RET_DK
RET_V = RET_HEADS * RET_DV
IN_SPLITS = (GLA_QK, GLA_QK, GLA_V, GLA_V, GLA_GATE_RANK, RET_QK, RET_QK, RET_V, RET_V, D_MODEL, D_MODEL)
IN_COLS = GLA_QK * 2 + GLA_V * 2 + GLA_GATE_RANK + RET_QK * 2 + RET_V * 2 + D_MODEL * 2

kernel_name = "hybrid_gla_retnet_convffn_block"

def rmsnorm(x, w):
    xf = x.astype(jnp.float32)
    y = xf * lax.rsqrt(jnp.mean(xf * xf, axis=-1, keepdims=True) + EPS)
    return (y * w.astype(jnp.float32)).astype(x.dtype)

def head_layernorm(o):
    mu = jnp.mean(o, axis=-1, keepdims=True)
    var = jnp.mean(jnp.square(o - mu), axis=-1, keepdims=True)
    return (o - mu) * lax.rsqrt(var + EPS)

def to_chunks(t, heads):
    b, s, _ = t.shape
    t = t.reshape(b, s // CHUNK, CHUNK, heads, -1)
    return t.transpose(1, 0, 3, 2, 4)

def from_chunks(t):
    n, b, h, c, d = t.shape
    return t.transpose(1, 0, 3, 2, 4).reshape(b, n * c, h * d)

def rope(x, positions):
    d = x.shape[-1]
    inv_freq = ROPE_BASE ** (-jnp.arange(0, d, 2, dtype=jnp.float32) / d)
    ang = positions.astype(jnp.float32)[..., None] * inv_freq
    cos = jnp.cos(ang)[:, :, None, :]
    sin = jnp.sin(ang)[:, :, None, :]
    x1, x2 = x[..., : d // 2], x[..., d // 2:]
    return jnp.concatenate([x1 * cos - x2 * sin, x1 * sin + x2 * cos], axis=-1)

def gla_mixer(q, k, v, log_a):
    b = q.shape[0]
    qc = to_chunks(q * (GLA_DK ** -0.5), GLA_HEADS)
    kc = to_chunks(k, GLA_HEADS)
    vc = to_chunks(v, GLA_HEADS)
    gc = to_chunks(log_a, GLA_HEADS)

    def step(state, inp):
        qi, ki, vi, gi = inp
        G = jnp.cumsum(gi, axis=2)
        decay = jnp.exp(-jnp.abs(G[:, :, :, None, :] - G[:, :, None, :, :]))
        scores = jnp.einsum('bhnd,bhmd,bhnmd->bhnm', qi, ki, decay)
        o = jnp.einsum('bhnm,bhme->bhne', scores, vi) + \
            jnp.einsum('bhnd,bhde->bhne', qi * jnp.exp(G), state)
        G_last = G[:, :, -1:, :]
        k_dec = ki * jnp.exp(G_last - G)
        state = jnp.exp(G_last[:, :, 0, :])[..., None] * state + \
            jnp.einsum('bhmd,bhme->bhde', k_dec, vi)
        return state, o

    s0 = jnp.zeros((b, GLA_HEADS, GLA_DK, GLA_DV), jnp.float32)
    _, oc = lax.scan(step, s0, (qc, kc, vc, gc))
    return oc

def retention_mixer(q, k, v):
    b, s = q.shape[0], q.shape[1]
    qc = to_chunks(q.reshape(b, s, -1), RET_HEADS)
    kc = to_chunks(k.reshape(b, s, -1) * (RET_DK ** -0.5), RET_HEADS)
    vc = to_chunks(v, RET_HEADS)
    log_gamma = jnp.log(1.0 - jnp.exp2(-5.0 - jnp.arange(RET_HEADS, dtype=jnp.float32)))
    idx = jnp.arange(CHUNK, dtype=jnp.float32)
    intra_decay = jnp.exp(log_gamma[:, None, None] * jnp.abs(idx[:, None] - idx[None, :]))
    q_decay = jnp.exp(log_gamma[:, None] * (idx + 1.0))[..., None]
    k_decay = jnp.exp(log_gamma[:, None] * (CHUNK - 1.0 - idx))[..., None]
    chunk_decay = jnp.exp(log_gamma * CHUNK)[:, None, None]

    def step(state, inp):
        qi, ki, vi = inp
        scores = jnp.einsum('bhnd,bhmd->bhnm', qi, ki) * intra_decay
        o = jnp.einsum('bhnm,bhme->bhne', scores, vi) + \
            jnp.einsum('bhnd,bhde->bhne', qi * q_decay, state)
        state = chunk_decay * state + jnp.einsum('bhmd,bhme->bhde', ki * k_decay, vi)
        return state, o

    s0 = jnp.zeros((b, RET_HEADS, RET_DK, RET_DV), jnp.float32)
    _, oc = lax.scan(step, s0, (qc, kc, vc))
    return oc

def causal_dwconv(u, w, bias):
    y = lax.conv_general_dilated(
        u, w[:, None, :].astype(u.dtype), window_strides=(1,),
        padding=((CONV_W - 1, 0),), dimension_numbers=('NWC', 'WIO', 'NWC'),
        feature_group_count=u.shape[-1])
    return y + bias.astype(u.dtype)

def setup_inputs(seed: int = 0) -> dict:
    key = jax.random.key(seed)
    ks = jax.random.split(key, 20)
    f32 = jnp.float32
    nrm = lambda k, shape, scale: jax.random.normal(k, shape, f32) * scale
    x = jax.random.normal(ks[0], (BATCH, SEQ, D_MODEL), f32)
    offset = jax.random.randint(ks[1], (BATCH, 1), 0, 4096, dtype=jnp.int32)
    positions = offset + jnp.arange(SEQ, dtype=jnp.int32)[None, :]
    return {
        "x": x,
        "positions": positions,
        "ln_pre_mix": 1.0 + nrm(ks[2], (DEPTH, D_MODEL), 0.02),
        "w_in": nrm(ks[3], (DEPTH, D_MODEL, IN_COLS), D_MODEL ** -0.5),
        "w_gla_decay": nrm(ks[4], (DEPTH, GLA_GATE_RANK, GLA_QK), GLA_GATE_RANK ** -0.5),
        "b_gla_decay": nrm(ks[5], (DEPTH, GLA_QK), 0.1),
        "w_gla_out": nrm(ks[6], (DEPTH, GLA_V, D_MODEL), GLA_V ** -0.5),
        "w_ret_out": nrm(ks[7], (DEPTH, RET_V, D_MODEL), RET_V ** -0.5),
        "w_mix_out": nrm(ks[8], (DEPTH, D_MODEL, D_MODEL), D_MODEL ** -0.5),
        "ln_post_mix": 1.0 + nrm(ks[9], (DEPTH, D_MODEL), 0.02),
        "ln_pre_ffn": 1.0 + nrm(ks[10], (DEPTH, D_MODEL), 0.02),
        "w_ffn_up": nrm(ks[11], (DEPTH, D_MODEL, 2 * D_FF), D_MODEL ** -0.5),
        "conv_w": nrm(ks[12], (DEPTH, CONV_W, 2 * D_FF), CONV_W ** -0.5),
        "conv_b": nrm(ks[13], (DEPTH, 2 * D_FF), 0.02),
        "w_ffn_down": nrm(ks[14], (DEPTH, D_FF, D_MODEL), D_FF ** -0.5),
        "ln_post_ffn": 1.0 + nrm(ks[15], (DEPTH, D_MODEL), 0.02),
    }

def reference(x, positions, ln_pre_mix, w_in, w_gla_decay, b_gla_decay, w_gla_out, w_ret_out,
              w_mix_out, ln_post_mix, ln_pre_ffn, w_ffn_up, conv_w, conv_b, w_ffn_down, ln_post_ffn):
    f32 = jnp.float32
    b, s, _ = x.shape
    split_at = [int(v) for v in np.cumsum(IN_SPLITS)[:-1]]
    for layer in range(DEPTH):
        h = rmsnorm(x, ln_pre_mix[layer])
        p = h @ w_in[layer]
        (g_q, g_k, g_v, g_r, g_lr, r_q, r_k, r_v, r_g, a_gla, a_ret) = jnp.split(p, split_at, axis=-1)

        log_a = jax.nn.log_sigmoid((g_lr @ w_gla_decay[layer] + b_gla_decay[layer]).astype(f32)) / GLA_TAU
        o_gla = gla_mixer(g_q.astype(f32), g_k.astype(f32), g_v.astype(f32), log_a)
        o_gla = from_chunks(head_layernorm(o_gla)) * jax.nn.silu(g_r.astype(f32))
        y_gla = o_gla.astype(x.dtype) @ w_gla_out[layer]

        rq = rope(r_q.astype(f32).reshape(b, s, RET_HEADS, RET_DK), positions)
        rk = rope(r_k.astype(f32).reshape(b, s, RET_HEADS, RET_DK), positions)
        o_ret = retention_mixer(rq, rk, r_v.astype(f32))
        o_ret = from_chunks(head_layernorm(o_ret)) * jax.nn.silu(r_g.astype(f32))
        y_ret = o_ret.astype(x.dtype) @ w_ret_out[layer]

        merged = jax.nn.sigmoid(a_gla) * y_gla + jax.nn.sigmoid(a_ret) * y_ret
        x = x + rmsnorm(merged @ w_mix_out[layer], ln_post_mix[layer])

        h = rmsnorm(x, ln_pre_ffn[layer])
        u = causal_dwconv(h @ w_ffn_up[layer], conv_w[layer], conv_b[layer])
        u_val, u_gate = jnp.split(u, 2, axis=-1)
        f = jax.nn.gelu(u_gate, approximate=True) * u_val
        x = x + rmsnorm(f @ w_ffn_down[layer], ln_post_ffn[layer])
    return x


_drawn_inputs = setup_inputs


def setup_inputs(seed=0):
    import zlib

    import numpy as np

    out = dict(_drawn_inputs(seed))
    spreads = {}
    factors = {'ln_post_mix': 3.467, 'ln_pre_ffn': 3.505, 'conv_b': 3.504, 'ln_post_ffn': 4.964}
    for name, (base, spread) in spreads.items():
        noise = np.random.default_rng([zlib.crc32(name.encode()), seed]).standard_normal(out[name].shape)
        drawn = base * np.exp(spread * noise) if base else spread * noise
        out[name] = __import__('jax').numpy.asarray(drawn.astype(out[name].dtype))
    for name, factor in factors.items():
        out[name] = (out[name] * factor).astype(out[name].dtype)
    return out
```

```python
import math
from contextlib import ExitStack

import numpy as np

import concourse.bass as bass
from concourse import mybir

F32 = mybir.dt.float32
F32R = mybir.dt.float32r
I32 = mybir.dt.int32
ALU = mybir.AluOpType
ACT = mybir.ActivationFunctionType
AX = mybir.AxisListType

P = 128
D = 1024
SEQ = 1024
KT = D // P
NT = SEQ // P
HALF = 512
CHUNK = 64
EPS = 1e-6
HEADS = 4
GLA_DK, GLA_DV, GLA_RANK, GLA_TAU = D // 8, D // 4, 16, 16.0
RET_DK, RET_DV = D // 4, D // 2
D_FF = 2816
FT = D_FF // P
GLA_QK, GLA_V, RET_QK, RET_V = HEADS * GLA_DK, HEADS * GLA_DV, HEADS * RET_DK, HEADS * RET_DV
GLA_KT, RET_KT = GLA_V // P, RET_V // P

_SPLITS = (GLA_QK, GLA_QK, GLA_V, GLA_V, GLA_RANK, RET_QK, RET_QK, RET_V, RET_V, D, D)
_OFF = [0]
for _s in _SPLITS:
    _OFF.append(_OFF[-1] + _s)
O_GQ, O_GK, O_GV, O_GR, O_LR, O_RQ, O_RK, O_RV, O_RG, O_AG, O_AR = _OFF[:11]


def projection_columns():
    cols = []
    for h in range(HEADS):
        cols += [O_GQ + h * P, O_GK + h * P, O_GV + h * 2 * P, O_GV + h * 2 * P + P]
    for h in range(HEADS):
        cols += [O_RQ + h * 2 * P, O_RQ + h * 2 * P + P, O_RK + h * 2 * P, O_RK + h * 2 * P + P]
        cols += [O_RV + (4 * h + j) * P for j in range(4)]
    cols += [O_GR + j * P for j in range(GLA_KT)]
    cols += [O_RG + j * P for j in range(RET_KT)]
    cols += [O_AG + j * P for j in range(KT)]
    cols += [O_AR + j * P for j in range(KT)]
    return cols


N_PROJ = len(projection_columns())
ROW_GLA, ROW_RET = 0, 4 * HEADS
ROW_GR = ROW_RET + 8 * HEADS
ROW_RG = ROW_GR + GLA_KT
ROW_AG = ROW_RG + RET_KT
ROW_AR = ROW_AG + KT
SL_LR = 0
SL_PROJ = 1
SL_YGLA = SL_PROJ + N_PROJ
SL_YRET = SL_YGLA + KT
SL_MIX = SL_YRET + 2 * 2 * KT
SL_UP = SL_MIX + 2 * KT
SL_DOWN = SL_UP + 2 * FT
N_SLABS = SL_DOWN + 2 * FT
RING = 4

LEVELS = [128 >> i for i in range(7)]
NL = len(LEVELS)
E_BLOCKS = NL + 2


def interval_table():
    m, n = np.meshgrid(np.arange(P), np.arange(P), indexing="ij")
    t = np.zeros((P, E_BLOCKS, P), np.float32)
    t[:, 0] = m > n
    for i, b in enumerate(LEVELS):
        mid = (n // b) * b + b // 2
        t[:, 1 + i] = np.where(n >= mid, (m >= mid) & (m <= n), (m > n) & (m < mid))
    t[:, NL + 1] = m <= n
    return (t / GLA_TAU).astype(np.float32).reshape(P, E_BLOCKS * P)


def level_masks():
    m, n = np.meshgrid(np.arange(P), np.arange(P), indexing="ij")
    t = np.zeros((P, NL + 1, P), np.float32)
    for i, b in enumerate(LEVELS):
        same = (m // b) == (n // b)
        mid = (n // b) * b + b // 2
        t[:, i] = same & ((m >= mid) != (n >= mid)) & (m // CHUNK <= n // CHUNK)
    t[:, NL] = m == n
    return (t * GLA_DK ** -0.5).astype(np.float32).reshape(P, (NL + 1) * P)


def retention_tables():
    g = 1.0 - 2.0 ** (-5.0 - np.arange(HEADS))
    m, n = np.meshgrid(np.arange(P), np.arange(P), indexing="ij")
    scale = RET_DK ** -0.5
    dec = np.stack([g[h] ** np.abs(n - m) * (m // CHUNK <= n // CHUNK) * scale for h in range(HEADS)], 1)
    qd = np.stack([g[h] ** (n + 1.0) for h in range(HEADS)], 1)
    kd = np.stack([g[h] ** (P - 1.0 - np.arange(P)) * scale for h in range(HEADS)], 1)
    return (dec.reshape(P, -1).astype(np.float32), qd.reshape(P, -1).astype(np.float32),
            kd.astype(np.float32))


def two_pi_parts(bits=7, count=7):
    parts, rest = [], 2.0 * math.pi
    for _ in range(count):
        e = math.floor(math.log2(rest)) - (bits - 1)
        part = math.floor(rest / 2.0 ** e) * 2.0 ** e
        parts.append(part)
        rest -= part
    return parts


SEMS = """
const_in const2_in x_in0 x_in1 x_in2 x_in3 sq_done rms_std rms_rstd x_scaled x_transposed
act_hi_done act_lo_done raw_in0 raw_in1 raw_in2 raw_in3 hi_split slab_ready mm_half
lr_in lr_out lr_ones z_out z_copied z_abs z_exp z_ln log_a loga_stored
pos_in pos_f turns0 turns1 angle angle_red sin_half cos_sq rope_done rope_stored
proj_evac st0 st1 st2 st3
g_in0 g_in1 g_gate_in g_tab_in g_tab g_la_hi g_la_lo g_vT g_v g_E g_exp g_qlev g_qG g_dec g_klev g_kend
g_S g_mask g_P g_kT g_kd g_o g_u g_state g_bn g_mv g_lnv g_rstd g_on g_onT g_og g_hi g_lo
r_tab_in r_in0 r_in1 r_in2 r_in3 r_xc r_xs r_rope r_qd r_kT r_kd r_vT r_v r_S r_P r_o r_u r_state
r_bn r_mv r_lnv r_rstd r_on r_onT r_og r_hi r_lo state_zero
y_in0 y_in1 y_in2 y_in3 y_mul y_evac yst0 yst1 yst2 yst3
d_in0 d_in1 d_in2 d_in3 d_ln_in d_hi d_lo d_act_evac d_dve_evac d_sq d_std d_rstd d_scaled d_res d_x_in
d_stored zero_set u_lin u_tap1 u_tap0 u_gelu u_f phase_done
""".split()


def build(nc, x, positions, w_stream, w_dec, b_dec, ln_post_mix, ln_post_ffn, ln_cols_in, conv_in,
          ident_in, interval_in, masks_in, ret_dec_in, ret_q_in, ret_k_in, inv_freq_in, eps_in, out):
    ctx = ExitStack()
    with ctx:
        sem = {name: ctx.enter_context(nc.semaphore(name)) for name in SEMS}

        def dram(name, shape):
            return nc.dram_tensor(name, list(shape), F32, kind="Internal").ap()

        proj_d = dram("proj_scratch", (N_PROJ, P, SEQ))
        loga_d = dram("loga_scratch", (NT, P, GLA_QK))
        gla_d = dram("gated_gla_scratch", (KT, P, SEQ))
        merged_d = dram("merged_scratch", (KT, P, SEQ))
        x1_d = dram("x1_scratch", (SEQ, D))
        f_d = dram("ffn_scratch", (FT, P, SEQ))
        rope_d = dram("rope_scratch", (2, P, SEQ))

        def sb(stack, name, shape, dt=F32):
            return stack.enter_context(nc.sbuf_tensor(name, list(shape), dt))

        act_hi = sb(ctx, "act_hi", (P, KT * SEQ), F32R)
        act_lo = sb(ctx, "act_lo", (P, KT * SEQ), F32R)
        w_raw = sb(ctx, "w_raw", (P, RING, D))
        w_hi = sb(ctx, "w_hi", (P, RING, D), F32R)
        w_lo = sb(ctx, "w_lo", (P, RING, D), F32R)
        ident = sb(ctx, "ident", (P, P))
        ln_col = sb(ctx, "ln_col", (P, 2, KT))
        conv_col = sb(ctx, "conv_col", (P, 2 * FT * 4))
        eps_col = sb(ctx, "eps_col", (P, 1))
        zero_col = sb(ctx, "zero_col", (P, 1))
        stat = sb(ctx, "stat", (P, 64))
        psum = ctx.enter_context(nc.psum_tensor("psum", [P, 8, HALF], F32))
        bank = psum[:, :, :].rearrange("p b n -> p (b n)")
        act_k = act_hi[:, :].rearrange("p (k n) -> p k n", k=KT)
        act_lo_k = act_lo[:, :].rearrange("p (k n) -> p k n", k=KT)
        act_r = act_hi[:, :].rearrange("p (k n) -> p k n", k=RET_KT)
        act_lo_r = act_lo[:, :].rearrange("p (k n) -> p k n", k=RET_KT)

        with ExitStack() as s:
            x_tok = sb(s, "x_tok", (P, NT, D))
            sq_junk = sb(s, "sq_junk", (P, D))
        with ExitStack() as s:
            stage = sb(s, "stage", (P, RING, SEQ))
            z_sb = sb(s, "z_sb", (P, NT, GLA_QK))
            z_a = sb(s, "z_a", (P, 2, GLA_QK))
            z_e = sb(s, "z_e", (P, 2, GLA_QK))
            lr_aug = sb(s, "lr_aug", (GLA_RANK + 1, SEQ))
            wdec_aug = sb(s, "wdec_aug", (GLA_RANK + 1, GLA_QK))
            pos_i = sb(s, "pos_i", (P, SEQ), I32)
            ang = sb(s, "ang", (P, 2, SEQ))
            turn = sb(s, "turn", (P, SEQ))
            rope_out = sb(s, "rope_out", (P, 2, SEQ))
            invf = sb(s, "invf", (P, 1))
        with ExitStack() as s:
            g_x = sb(s, "g_x", (P, 2, 4 * HEADS, P))
            g_la = sb(s, "g_la", (P, 2, GLA_QK))
            g_gate = sb(s, "g_gate", (P, GLA_KT, P))
            la_hi = sb(s, "la_hi", (P, GLA_QK), F32R)
            la_lo = sb(s, "la_lo", (P, GLA_QK), F32R)
            interval = sb(s, "interval", (P, E_BLOCKS * P), F32R)
            masks = sb(s, "masks", (P, (NL + 1) * P))
            e_t = sb(s, "e_t", (P, 2, E_BLOCKS * P))
            q_lev = sb(s, "q_lev", (P, 2, NL, P))
            k_lev = sb(s, "k_lev", (P, 2, NL, P))
            q_g = sb(s, "q_g", (P, HEADS, P))
            k_end = sb(s, "k_end", (P, HEADS, P))
            g_vt = sb(s, "g_vt", (P, GLA_V))
            g_kdt = sb(s, "g_kdt", (P, GLA_QK))
            s_masked = sb(s, "s_masked", (P, (NL + 1) * P))
            p_t = sb(s, "p_t", (P, HEADS, P))
            g_st = sb(s, "g_st", (P, HEADS, GLA_DV))
            g_deccol = sb(s, "g_deccol", (P, HEADS))
            g_onb = sb(s, "g_onb", (P, GLA_V))
            g_ogb = sb(s, "g_ogb", (P, GLA_V))
            g_bst = sb(s, "g_bst", (P, HEADS, 8))
            g_mvb = sb(s, "g_mvb", (P, HEADS, 2))
            g_rsb = sb(s, "g_rsb", (P, 2, HEADS))
        with ExitStack() as s:
            r_st = sb(s, "r_st", (P, HEADS, 2, RET_DV))
            ret_dec = sb(s, "ret_dec", (P, HEADS, P))
            ret_q = sb(s, "ret_q", (P, HEADS, P))
            ret_k = sb(s, "ret_k", (P, HEADS))
            cossin = sb(s, "cossin", (P, 2, SEQ))
            with ExitStack() as s2:
                r_x = sb(s2, "r_x", (P, HEADS, 12, P))
                r_xcb = sb(s2, "r_xcb", (P, 2, 4, P))
                r_xsb = sb(s2, "r_xsb", (P, 2, 4, P))
                r_qk = sb(s2, "r_qk", (P, 2, 4, P))
                r_qdb = sb(s2, "r_qdb", (P, 2, 2, P))
                r_kdt = sb(s2, "r_kdt", (P, 2, RET_DK))
                r_vt = sb(s2, "r_vt", (P, 2, RET_DV))
                r_pt = sb(s2, "r_pt", (P, 2, P))
                r_onb = sb(s2, "r_onb", (P, 2, RET_DV))
                r_ogb = sb(s2, "r_ogb", (P, 2, RET_DV))
                r_bst = sb(s2, "r_bst", (P, 2, 8))
                r_mvb = sb(s2, "r_mvb", (P, 2, 2))
                r_rsb = sb(s2, "r_rsb", (P, 2, 2))
            with ExitStack() as s2:
                y_in = sb(s2, "y_in", (P, RING, SEQ))
                y_out = sb(s2, "y_out", (P, RING, SEQ))
                y_tmp = sb(s2, "y_tmp", (P, 2, HALF))
        with ExitStack() as s:
            d_raw = sb(s, "d_raw", (P, RING, HALF))
            d_hib = sb(s, "d_hib", (P, RING, HALF), F32R)
            d_lob = sb(s, "d_lob", (P, RING, HALF), F32R)
            d_out = sb(s, "d_out", (P, 4, D))
            d_x = sb(s, "d_x", (P, 4, D))
            d_ln = sb(s, "d_ln", (P, D))
            d_junk = sb(s, "d_junk", (P, D))
        with ExitStack() as s:
            u_conv = sb(s, "u_conv", (P, RING, SEQ))
            u_fb = sb(s, "u_fb", (P, RING, SEQ))

        def repeat(eng, lo, count, body, unroll=RING, peel=1):
            def group(g):
                for j in range(unroll):
                    body(g * unroll + j, g * unroll + (lo + j), g + (lo + j) // unroll,
                         (lo + j) % unroll, isinstance(g, int) and g == 0)
            groups = count // unroll
            first = min(peel, groups)
            for g in range(first):
                group(g)
            if groups - first >= 2:
                with eng.Fori(first, groups) as g:
                    group(g)
            elif groups - first == 1:
                group(first)
            for k in range(groups * unroll, count):
                body(k, lo + k, (lo + k) // unroll, (lo + k) % unroll, groups == 0)

        raw_in = [sem[f"raw_in{j}"] for j in range(RING)]
        stored = [sem[f"st{j}"] for j in range(RING)]
        x_in = [sem[f"x_in{j}"] for j in range(4)]
        g_in = [sem["g_in0"], sem["g_in1"]]
        r_in = [sem[f"r_in{j}"] for j in range(RING)]
        y_ins = [sem[f"y_in{j}"] for j in range(RING)]
        y_st = [sem[f"yst{j}"] for j in range(RING)]
        d_in = [sem[f"d_in{j}"] for j in range(RING)]

        def product3(o, s_hi, s_lo, m_hi, m_lo, start, stop):
            nc.tensor.matmul(o, s_hi, m_hi, start=start, stop=False)
            nc.tensor.matmul(o, s_hi, m_lo, start=False, stop=False)
            return nc.tensor.matmul(o, s_lo, m_hi, start=False, stop=stop)

        def end_phase(eng):
            eng.drain().then_inc(sem["phase_done"], 1)

        def begin_phase(eng, n):
            if n:
                eng.wait_ge(sem["phase_done"], 4 * n)

        def load_slab(sp, n, j):
            sp.dma_start(w_raw[:, j, :], w_stream[n, :, :]).then_inc(raw_in[j], 16)

        def stream_prologue(sp):
            for n in range(RING):
                load_slab(sp, n, n)
            for n in range(RING):
                sp.wait_ge(sem["slab_ready"], n + 1)
                load_slab(sp, n + RING, n)

        def stream_step(sp, n, j):
            sp.wait_ge(sem["slab_ready"], n + RING + 1)
            load_slab(sp, n + 2 * RING, j)

        def split_slabs(pool, lo, hi):
            def body(k, n, grp, j, early):
                pool.wait_ge(raw_in[j], 16 * grp + 16)
                if not (early and lo == 0):
                    pool.wait_ge(sem["mm_half"], 2 * n - 2 * RING + 2)
                nc.gpsimd.tensor_tensor(w_hi[:, j, :], w_raw[:, j, :],
                                        zero_col[:, :].to_broadcast((P, D)), ALU.add).then_inc(sem["hi_split"], 1)
                pool.wait_ge(sem["hi_split"], n + 1)
                nc.gpsimd.tensor_tensor(w_lo[:, j, :], w_raw[:, j, :], w_hi[:, j, :].bitcast(F32),
                                        ALU.subtract).then_inc(sem["slab_ready"], 1)
            repeat(pool, lo, hi - lo, body)

        def norm_sp(sp, src):
            for c in range(4):
                sp.dma_start(x_tok[:, 2 * c:2 * c + 2, :],
                             src[c * 256:c * 256 + 256, :].rearrange("(t p) d -> p t d", p=P)
                             ).then_inc(x_in[c], 16)

        def norm_act(act, rnd):
            for t in range(NT):
                if t % 2 == 0:
                    act.wait_ge(x_in[t // 2], 16 * rnd + 16)
                if t:
                    act.wait_ge(sem["sq_done"], NT * rnd + t)
                nc.scalar.activation(sq_junk[:, :], x_tok[:, t, :], ACT.Square,
                                     accum_out=stat[:, t:t + 1]).then_inc(sem["sq_done"], 1)
            act.wait_ge(sem["sq_done"], NT * rnd + NT)
            act.wait_ge(sem["const_in"], 64)
            nc.scalar.activation(stat[:, 8:16], stat[:, 0:8], ACT.Sqrt, scale=1.0 / D,
                                 bias=eps_col[:, 0:1]).then_inc(sem["rms_std"], 1)
            for i in range(2 * KT):
                k, hf = i % KT, i // KT
                act.wait_ge(sem["x_transposed"], 2 * KT * rnd + i + 1)
                nc.scalar.activation(act_hi[:, k * SEQ + hf * HALF:k * SEQ + hf * HALF + HALF],
                                     psum[:, i % 8, :], ACT.Copy,
                                     scale=ln_col[:, rnd, k:k + 1]).then_inc(sem["act_hi_done"], 1)

        def norm_dve(dve, rnd):
            dve.wait_ge(sem["rms_std"], rnd + 1)
            nc.vector.reciprocal(stat[:, 16:24], stat[:, 8:16]).then_inc(sem["rms_rstd"], 1)
            dve.wait_ge(sem["rms_rstd"], rnd + 1)
            for t in range(NT):
                nc.vector.tensor_scalar(x_tok[:, t, :], x_tok[:, t, :], stat[:, 16 + t:17 + t], None,
                                        ALU.mult).then_inc(sem["x_scaled"], 1)
            for i in range(2 * KT):
                k, hf = i % KT, i // KT
                sl = slice(k * SEQ + hf * HALF, k * SEQ + hf * HALF + HALF)
                dve.wait_ge(sem["act_hi_done"], 2 * KT * rnd + i + 1)
                nc.vector.scalar_tensor_tensor(act_lo[:, sl], psum[:, i % 8, :], ln_col[:, rnd, k:k + 1],
                                               act_hi[:, sl].bitcast(F32), ALU.mult, ALU.subtract
                                               ).then_inc(sem["act_lo_done"], 1)

        def norm_pe(pe, rnd):
            for i in range(2 * KT):
                k, hf = i % KT, i // KT
                pe.wait_ge(sem["x_scaled"], NT * rnd + 4 * hf + 4)
                if i >= 8:
                    pe.wait_ge(sem["act_lo_done"], 2 * KT * rnd + i - 7)
                for q in range(4):
                    last = nc.tensor.transpose(psum[:, i % 8, q * P:(q + 1) * P],
                                               x_tok[:, 4 * hf + q, k * P:(k + 1) * P], ident[:, :])
                last.then_inc(sem["x_transposed"], 1)
            pe.wait_ge(sem["act_lo_done"], 2 * KT * rnd + 2 * KT)

        def slab_product(pe, n, j, pair):
            pe.wait_ge(sem["slab_ready"], n + 1)
            for hf in range(2):
                for k in range(KT):
                    sl = slice(k * SEQ + hf * HALF, k * SEQ + hf * HALF + HALF)
                    last = product3(psum[:, 2 * pair + hf, :], w_hi[:, j, k * P:(k + 1) * P],
                                    w_lo[:, j, k * P:(k + 1) * P], act_hi[:, sl], act_lo[:, sl],
                                    k == 0, k == KT - 1)
                last.then_inc(sem["mm_half"], 1)

        def pair_view(pair):
            return bank[:, pair * SEQ:(pair + 1) * SEQ]

        def proj_pe(pe):
            slab_product(pe, SL_LR, 0, 0)
            pe.wait_ge(sem["lr_out"], 2)
            pe.wait_ge(sem["lr_in"], 32)
            for t in range(NT):
                nc.tensor.matmul(psum[:, t, :], lr_aug[:, t * P:(t + 1) * P], wdec_aug[:, :],
                                 start=True, stop=True).then_inc(sem["z_out"], 1)

            def body(k, n, grp, j, early):
                pair = (j - SL_PROJ) % RING
                if early:
                    pe.wait_ge(sem["z_copied"], 2 * pair + 2)
                else:
                    pe.wait_ge(sem["proj_evac"], k - RING + 1)
                slab_product(pe, n, j, pair)
            repeat(pe, SL_PROJ, N_PROJ, body)

        def proj_act(act):
            for t in range(NT):
                b = t % 2
                act.wait_ge(sem["z_abs"], t + 1)
                nc.scalar.activation(z_e[:, b, :], z_a[:, b, :], ACT.Exp, scale=-1.0
                                     ).then_inc(sem["z_exp"], 1)
                act.wait_ge(sem["z_exp"], t + 1)
                nc.scalar.activation(z_a[:, b, :], z_e[:, b, :], ACT.Ln, bias=1.0
                                     ).then_inc(sem["z_ln"], 1)
            act.wait_ge(sem["angle_red"], 1)
            nc.scalar.activation(rope_out[:, 1, :], ang[:, 0, :], ACT.Sin).then_inc(sem["sin_half"], 1)
            nc.scalar.activation(ang[:, 1, :], ang[:, 0, :], ACT.Sin, scale=0.5).then_inc(sem["sin_half"], 1)
            for lo, hi, func in ((0, ROW_GR, ACT.Copy), (ROW_GR, ROW_AG, ACT.Silu),
                                 (ROW_AG, N_PROJ, ACT.Sigmoid)):
                def body(k, row, grp, j, early, func=func):
                    act.wait_ge(sem["mm_half"], 2 * row + 2 * SL_PROJ + 2)
                    if not (isinstance(row, int) and row < RING):
                        act.wait_ge(stored[j], 16 * grp)
                    nc.scalar.activation(stage[:, j, :], pair_view(j), func).then_inc(sem["proj_evac"], 1)
                repeat(act, lo, hi - lo, body)

        def proj_dve(dve):
            nc.vector.memset(lr_aug[:, :], 1.0).then_inc(sem["lr_ones"], 1)
            dve.wait_ge(sem["mm_half"], 2)
            dve.wait_ge(sem["lr_ones"], 1)
            for hf in range(2):
                nc.vector.tensor_copy(lr_aug[0:GLA_RANK, hf * HALF:hf * HALF + HALF],
                                      psum[0:GLA_RANK, hf, :]).then_inc(sem["lr_out"], 1)
            for t in range(NT):
                dve.wait_ge(sem["z_out"], t + 1)
                nc.vector.tensor_copy(z_sb[:, t, :], psum[:, t, :]).then_inc(sem["z_copied"], 1)

            def log_a_tail(t):
                dve.wait_ge(sem["z_ln"], t + 1)
                nc.vector.scalar_tensor_tensor(z_sb[:, t, :], z_sb[:, t, :], 0.0, z_a[:, t % 2, :],
                                               ALU.min, ALU.subtract).then_inc(sem["log_a"], 1)
            dve.wait_ge(sem["z_copied"], NT)
            for t in range(NT):
                if t >= 2:
                    log_a_tail(t - 2)
                    dve.wait_ge(sem["log_a"], t - 1)
                nc.vector.scalar_tensor_tensor(z_a[:, t % 2, :], z_sb[:, t, :], -1.0, z_sb[:, t, :],
                                               ALU.mult, ALU.max).then_inc(sem["z_abs"], 1)
            log_a_tail(NT - 2)
            log_a_tail(NT - 1)
            dve.wait_ge(sem["pos_in"], 32)
            nc.vector.tensor_copy(ang[:, 1, :], pos_i[:, :]).then_inc(sem["pos_f"], 1)
            dve.wait_ge(sem["pos_f"], 1)
            nc.vector.tensor_scalar(ang[:, 0, :], ang[:, 1, :], invf[:, 0:1], None, ALU.mult
                                    ).then_inc(sem["angle"], 1)
            dve.wait_ge(sem["angle"], 1)
            magic = 1.5 * 2.0 ** 23
            nc.vector.tensor_scalar(turn[:, :], ang[:, 0, :], 1.0 / (2.0 * math.pi), magic,
                                    ALU.mult, ALU.add).then_inc(sem["turns0"], 1)
            dve.wait_ge(sem["turns0"], 1)
            nc.vector.tensor_scalar(turn[:, :], turn[:, :], magic, None, ALU.subtract
                                    ).then_inc(sem["turns1"], 1)
            dve.wait_ge(sem["turns1"], 1)
            for i, part in enumerate(two_pi_parts()):
                nc.vector.scalar_tensor_tensor(ang[:, 0, :], turn[:, :], -part, ang[:, 0, :],
                                               ALU.mult, ALU.add).then_inc(sem["angle"], 1)
                dve.wait_ge(sem["angle"], i + 2)
            nc.vector.tensor_scalar(ang[:, 0, :], ang[:, 0, :], 3.1415925, -3.1415925,
                                    ALU.min, ALU.max).then_inc(sem["angle_red"], 1)
            dve.wait_ge(sem["sin_half"], 2)
            nc.vector.tensor_tensor(ang[:, 0, :], ang[:, 1, :], ang[:, 1, :], ALU.mult
                                    ).then_inc(sem["cos_sq"], 1)
            dve.wait_ge(sem["cos_sq"], 1)
            nc.vector.tensor_scalar(rope_out[:, 0, :], ang[:, 0, :], -2.0, 1.0, ALU.mult, ALU.add
                                    ).then_inc(sem["rope_done"], 1)

        def proj_sp(sp):
            sp.dma_start(wdec_aug[0:GLA_RANK, :], w_dec).then_inc(sem["lr_in"], 16)
            sp.dma_start(wdec_aug[GLA_RANK:GLA_RANK + 1, :], b_dec).then_inc(sem["lr_in"], 16)
            sp.dma_start(pos_i[:, :], positions.to_broadcast((P, SEQ))).then_inc(sem["pos_in"], 16)
            sp.dma_start(invf[:, :], inv_freq_in).then_inc(sem["pos_in"], 16)
            stream_step(sp, SL_LR, 0)

            def body(k, n, grp, j, early):
                slot = (j - SL_PROJ) % RING
                sp.wait_ge(sem["proj_evac"], k + 1)
                sp.dma_start(proj_d[k, :, :], stage[:, slot, :]).then_inc(stored[slot], 16)
                stream_step(sp, n, j)
            repeat(sp, SL_PROJ, N_PROJ, body)
            sp.wait_ge(sem["log_a"], NT)
            sp.dma_start(loga_d.rearrange("t p c -> p t c"), z_sb[:, :, :]).then_inc(sem["loga_stored"], 16)
            sp.wait_ge(sem["rope_done"], 1)
            sp.dma_start(rope_d.rearrange("a p n -> p a n"), rope_out[:, :, :]).then_inc(sem["rope_stored"], 16)
            sp.wait_ge(sem["loga_stored"], 16)
            sp.wait_ge(sem["rope_stored"], 16)
            for j in range(RING):
                sp.wait_ge(stored[j], 16 * N_PROJ // RING)

        gate_bank, vt_bank, o_bank, u_bank = (7, 5), (5, 6), (7, 6), (5, 7)
        kt_bank = 6

        def tile_cols(t):
            return slice(t * P, t * P + P) if isinstance(t, int) else bass.ds(t * P, P)

        def gla_sp(sp):
            sp.dma_start(masks[:, :], masks_in).then_inc(sem["g_tab_in"], 16)
            sp.dma_start(e_t[:, 0, :], interval_in).then_inc(sem["g_tab_in"], 16)

            def gates(t):
                if not (isinstance(t, int) and t < 1):
                    sp.wait_ge(sem["g_og"], 2 * t)
                sp.dma_start(g_gate[:, :, :], proj_d[ROW_GR:ROW_GR + GLA_KT, :, tile_cols(t)]
                             .rearrange("r p n -> p r n")).then_inc(sem["g_gate_in"], 16)

            def body(k, t, grp, d, early):
                if not early:
                    sp.wait_ge(sem["g_o"], 2 * t - 2)
                sp.dma_start(g_x[:, d, :, :], proj_d[ROW_GLA:ROW_GLA + 4 * HEADS, :, tile_cols(t)]
                             .rearrange("r p n -> p r n")).then_inc(g_in[d], 16)
                sp.dma_start(g_la[:, d, :], loga_d[t, :, :]).then_inc(g_in[d], 16)
                if not (early and d == 0):
                    gates(t - 1)
            repeat(sp, 0, NT, body, unroll=2)
            gates(NT - 1)

        def gla_act(act):
            act.wait_ge(sem["g_tab_in"], 32)
            nc.scalar.activation(interval[:, :], e_t[:, 0, :], ACT.Copy).then_inc(sem["g_tab"], 1)
            act.wait_ge(sem["g_tab"], 1)

            def gated_hi(t):
                for i in range(2):
                    act.wait_ge(sem["g_og"], 2 * t + i + 1)
                    act.wait_ge(sem["g_tab"], 1)
                    nc.scalar.activation(act_k[:, 4 * i:4 * i + 4, tile_cols(t)],
                                         g_ogb[:, i * HALF:(i + 1) * HALF].rearrange("p (q n) -> p q n", q=4),
                                         ACT.Copy).then_inc(sem["g_hi"], 1)

            def body(k, t, grp, d, early):
                first = early and d == 0
                act.wait_ge(g_in[d], 32 * grp + 32)
                if not first:
                    act.wait_ge(sem["g_E"], 4 * t)
                nc.scalar.activation(la_hi[:, :], g_la[:, d, :], ACT.Copy).then_inc(sem["g_la_hi"], 1)

                def decay(h):
                    e = 4 * t + h
                    act.wait_ge(sem["g_E"], e + 1)
                    if not (first and h < 2):
                        act.wait_ge(sem["g_dec"], e - 1)
                        act.wait_ge(sem["g_kend"], e - 1)
                    nc.scalar.activation(e_t[:, h % 2, :], bank[:, 0:E_BLOCKS * P], ACT.Exp
                                         ).then_inc(sem["g_exp"], 1)

                decay(0)
                for i in range(2):
                    act.wait_ge(sem["g_vT"], 2 * t + i + 1)
                    if not first:
                        act.wait_ge(sem["g_u"], 2 * t)
                    nc.scalar.activation(g_vt[:, i * HALF:(i + 1) * HALF], psum[:, vt_bank[i], :],
                                         ACT.Copy).then_inc(sem["g_v"], 1)
                decay(1)
                decay(2)
                if not first:
                    gated_hi(t - 1)
                decay(3)
                act.wait_ge(sem["g_kT"], t + 1)
                nc.scalar.activation(g_kdt[:, :], psum[:, kt_bank, :], ACT.Copy,
                                     scale=GLA_DK ** -0.5).then_inc(sem["g_kd"], 1)
                for i in range(2):
                    act.wait_ge(sem["g_mv"], 4 * t + 2 * i + 2)
                    nc.scalar.activation(g_rsb[:, 0, 2 * i:2 * i + 2], g_mvb[:, 2 * i:2 * i + 2, 1],
                                         ACT.Ln, bias=eps_col[:, 0:1]).then_inc(sem["g_lnv"], 1)
                    act.wait_ge(sem["g_lnv"], 2 * t + i + 1)
                    nc.scalar.activation(g_rsb[:, 1, 2 * i:2 * i + 2], g_rsb[:, 0, 2 * i:2 * i + 2],
                                         ACT.Exp, scale=-0.5).then_inc(sem["g_rstd"], 1)
            repeat(act, 0, NT, body, unroll=2)
            gated_hi(NT - 1)

        def gla_pool(pool):
            def gated_lo(t):
                pool.wait_ge(sem["g_hi"], 2 * t + 2)
                pool.wait_ge(sem["g_tab"], 1)
                nc.gpsimd.tensor_tensor(act_lo_k[:, :, tile_cols(t)],
                                        g_ogb[:, :].rearrange("p (q n) -> p q n", q=KT),
                                        act_k[:, :, tile_cols(t)].bitcast(F32),
                                        ALU.subtract).then_inc(sem["g_lo"], 1)

            def body(k, t, grp, d, early):
                first = early and d == 0
                for h in range(HEADS):
                    e = 4 * t + h
                    b = h % 2
                    pool.wait_ge(sem["g_exp"], e + 1)
                    if not (first and h < 2):
                        pool.wait_ge(sem["g_S"], e - 1)
                    key = g_x[:, d, 4 * h + 1, :]
                    levels = e_t[:, b, P:(NL + 1) * P].rearrange("p (l n) -> p l n", l=NL)
                    nc.gpsimd.tensor_tensor(k_lev[:, b, :, :], levels,
                                            key.unsqueeze(1).to_broadcast((P, NL, P)),
                                            ALU.mult).then_inc(sem["g_klev"], 1)
                    if not first:
                        pool.wait_ge(sem["g_kT"], t)
                    nc.gpsimd.tensor_tensor(k_end[:, h, :], e_t[:, b, 0:P], key, ALU.mult
                                            ).then_inc(sem["g_kend"], 1)
                    if h == 2 and not first:
                        gated_lo(t - 1)
            repeat(pool, 0, NT, body, unroll=2)
            gated_lo(NT - 1)

        def gla_dve(dve):
            nc.vector.memset(g_st[:, :, :], 0.0).then_inc(sem["state_zero"], 1)
            dve.wait_ge(sem["g_tab_in"], 32)

            def gate(t):
                dve.wait_ge(sem["g_gate_in"], 16 * t + 16)
                if not (isinstance(t, int) and t < 1):
                    dve.wait_ge(sem["g_lo"], t)
                for i in range(2):
                    dve.wait_ge(sem["g_onT"], 2 * t + i + 1)
                    nc.vector.tensor_tensor(g_ogb[:, i * HALF:(i + 1) * HALF], psum[:, gate_bank[i], :],
                                            g_gate[:, 4 * i:4 * i + 4, :].rearrange("p q n -> p (q n)"),
                                            ALU.mult).then_inc(sem["g_og"], 1)

            def body(k, t, grp, d, early):
                first = early and d == 0
                dve.wait_ge(sem["g_la_hi"], t + 1)
                nc.vector.tensor_tensor(la_lo[:, :], g_la[:, d, :], la_hi[:, :].bitcast(F32),
                                        ALU.subtract).then_inc(sem["g_la_lo"], 1)

                def queries(h):
                    e, b = 4 * t + h, h % 2
                    dve.wait_ge(sem["g_exp"], e + 1)
                    if not (first and h < 2):
                        dve.wait_ge(sem["g_S"], e - 1)
                    q = g_x[:, d, 4 * h, :]
                    levels = e_t[:, b, P:(NL + 1) * P].rearrange("p (l n) -> p l n", l=NL)
                    nc.vector.tensor_tensor(q_lev[:, b, :, :], levels,
                                            q.unsqueeze(1).to_broadcast((P, NL, P)),
                                            ALU.mult).then_inc(sem["g_qlev"], 1)
                    if not first:
                        dve.wait_ge(sem["g_o"], 2 * t)
                    nc.vector.tensor_tensor(q_g[:, h, :], e_t[:, b, (NL + 1) * P:], q, ALU.mult
                                            ).then_inc(sem["g_qG"], 1)
                    nc.vector.tensor_copy(g_deccol[:, h:h + 1], e_t[:, b, E_BLOCKS * P - 1:]
                                          ).then_inc(sem["g_dec"], 1)

                def scores(h):
                    e = 4 * t + h
                    dve.wait_ge(sem["g_S"], e + 1)
                    if not (first and h == 0):
                        dve.wait_ge(sem["g_P"], e)
                    nc.vector.tensor_tensor(s_masked[:, :], bank[:, 3 * HALF:5 * HALF], masks[:, :],
                                            ALU.mult).then_inc(sem["g_mask"], 1)
                    dve.wait_ge(sem["g_mask"], e + 1)
                    nc.vector.tensor_reduce(p_t[:, h, :],
                                            s_masked[:, :].rearrange("p (l n) -> p n l", n=P),
                                            AX.X, ALU.add).then_inc(sem["g_P"], 1)

                def stats(h):
                    e = 4 * t + h
                    o = psum[:, o_bank[h // 2], (h % 2) * GLA_DV:(h % 2 + 1) * GLA_DV]
                    nc.vector.bn_stats(g_bst[:, h, 0:6], o).then_inc(sem["g_bn"], 1)
                    dve.wait_ge(sem["g_tab_in"], 32)
                    dve.wait_ge(sem["g_bn"], e + 1)
                    nc.vector.bn_aggr(g_mvb[:, h, :], g_bst[:, h, 0:6]).then_inc(sem["g_mv"], 1)

                def state(h):
                    u = psum[:, u_bank[h // 2], (h % 2) * GLA_DV:(h % 2 + 1) * GLA_DV]
                    nc.vector.scalar_tensor_tensor(g_st[:, h, :], g_st[:, h, :], g_deccol[:, h:h + 1], u,
                                                   ALU.mult, ALU.add).then_inc(sem["g_state"], 1)

                def normed(h):
                    o = psum[:, o_bank[h // 2], (h % 2) * GLA_DV:(h % 2 + 1) * GLA_DV]
                    nc.vector.tensor_scalar(g_onb[:, h * GLA_DV:(h + 1) * GLA_DV], o,
                                            g_mvb[:, h, 0:1], g_rsb[:, 1, h:h + 1],
                                            ALU.subtract, ALU.mult).then_inc(sem["g_on"], 1)

                queries(0)
                queries(1)
                scores(0)
                queries(2)
                scores(1)
                if not first:
                    gate(t - 1)
                queries(3)
                scores(2)
                scores(3)
                dve.wait_ge(sem["g_dec"], 4 * t + 4)
                for i in range(2):
                    dve.wait_ge(sem["g_o"], 2 * t + i + 1)
                    stats(2 * i)
                    stats(2 * i + 1)
                    dve.wait_ge(sem["g_u"], 2 * t + i + 1)
                    state(2 * i)
                    state(2 * i + 1)
                    dve.wait_ge(sem["g_rstd"], 2 * t + i + 1)
                    dve.wait_ge(sem["g_mv"], 4 * t + 2 * i + 2)
                    normed(2 * i)
                    normed(2 * i + 1)
            dve.wait_ge(sem["state_zero"], 1)
            repeat(dve, 0, NT, body, unroll=2)
            gate(NT - 1)

        def gla_pe(pe):
            pe.wait_ge(sem["g_tab"], 1)
            pe.wait_ge(sem["state_zero"], 1)

            def out_transposes(t):
                for i in range(2):
                    pe.wait_ge(sem["g_on"], 4 * t + 4)
                    if i == 0:
                        pe.wait_ge(sem["g_state"], 4 * t + 4)
                    else:
                        pe.wait_ge(sem["g_v"] if not (isinstance(t, int) and t == NT - 1)
                                   else sem["g_state"],
                                   2 * t + 3 if not (isinstance(t, int) and t == NT - 1) else 4 * t + 4)
                    for q in range(4):
                        last = nc.tensor.transpose(psum[:, gate_bank[i], q * P:(q + 1) * P],
                                                   g_onb[:, (4 * i + q) * P:(4 * i + q + 1) * P], ident[:, :])
                    last.then_inc(sem["g_onT"], 1)

            def body(k, t, grp, d, early):
                first = early and d == 0

                def decay(h):
                    e = 4 * t + h
                    pe.wait_ge(sem["g_la_lo"], t + 1)
                    if not (first and h == 0):
                        pe.wait_ge(sem["g_exp"], e)
                    for c0 in range(0, E_BLOCKS * P, HALF):
                        c1 = min(c0 + HALF, E_BLOCKS * P)
                        nc.tensor.matmul(bank[:, c0:c1], la_hi[:, h * P:(h + 1) * P], interval[:, c0:c1],
                                         start=True, stop=False)
                        last = nc.tensor.matmul(bank[:, c0:c1], la_lo[:, h * P:(h + 1) * P],
                                                interval[:, c0:c1], start=False, stop=True)
                    last.then_inc(sem["g_E"], 1)

                def scores(h):
                    e, b = 4 * t + h, h % 2
                    pe.wait_ge(sem["g_klev"], e + 1)
                    pe.wait_ge(sem["g_qlev"], e + 1)
                    if not (first and h == 0):
                        pe.wait_ge(sem["g_mask"], e)
                    for l in range(NL + 1):
                        o = bank[:, 3 * HALF + l * P:3 * HALF + (l + 1) * P]
                        key = k_lev[:, b, l, :] if l < NL else g_x[:, d, 4 * h + 1, :]
                        query = q_lev[:, b, l, :] if l < NL else g_x[:, d, 4 * h, :]
                        last = nc.tensor.matmul(o, key, query, start=True, stop=True)
                    last.then_inc(sem["g_S"], 1)

                decay(0)
                for i in range(2):
                    if not first:
                        pe.wait_ge(sem["g_state"] if i == 0 else sem["g_on"], 4 * t - 2 if i == 0 else 4 * t)
                    for q in range(4):
                        row = 4 * (2 * i + q // 2) + 2 + q % 2
                        last = nc.tensor.transpose(psum[:, vt_bank[i], q * P:(q + 1) * P],
                                                   g_x[:, d, row, :], ident[:, :])
                    last.then_inc(sem["g_vT"], 1)
                decay(1)
                scores(0)
                decay(2)
                scores(1)
                if not first:
                    out_transposes(t - 1)
                decay(3)
                scores(2)
                scores(3)
                pe.wait_ge(sem["g_v"], 2 * t + 2)
                pe.wait_ge(sem["g_kend"], 4 * t + 4)
                for h in range(HEADS):
                    last = nc.tensor.transpose(psum[:, kt_bank, h * P:(h + 1) * P], k_end[:, h, :], ident[:, :])
                last.then_inc(sem["g_kT"], 1)
                for i in range(2):
                    pe.wait_ge(sem["g_P"], 4 * t + 2 * i + 2)
                    pe.wait_ge(sem["g_qG"], 4 * t + 2 * i + 2)
                    if not first:
                        pe.wait_ge(sem["g_state"], 4 * t - 2 + 2 * i)
                    if i == 0 and not first:
                        pe.wait_ge(sem["g_og"], 2 * t - 1)
                    if i == 1:
                        pe.wait_ge(sem["g_kd"], t + 1)
                    for h in (2 * i, 2 * i + 1):
                        o = psum[:, o_bank[i], (h % 2) * GLA_DV:(h % 2 + 1) * GLA_DV]
                        nc.tensor.matmul(o, p_t[:, h, :], g_vt[:, h * GLA_DV:(h + 1) * GLA_DV],
                                         start=True, stop=False)
                        last = nc.tensor.matmul(o, q_g[:, h, :], g_st[:, h, :], start=False, stop=True)
                    last.then_inc(sem["g_o"], 1)
                    pe.wait_ge(sem["g_kd"], t + 1)
                    if i == 0 and not first:
                        pe.wait_ge(sem["g_og"], 2 * t)
                    if i == 1:
                        pe.wait_ge(sem["g_on"], 4 * t + 2)
                    for h in (2 * i, 2 * i + 1):
                        u = psum[:, u_bank[i], (h % 2) * GLA_DV:(h % 2 + 1) * GLA_DV]
                        last = nc.tensor.matmul(u, g_kdt[:, h * P:(h + 1) * P],
                                                g_vt[:, h * GLA_DV:(h + 1) * GLA_DV], start=True, stop=True)
                    last.then_inc(sem["g_u"], 1)
            repeat(pe, 0, NT, body, unroll=2)
            out_transposes(NT - 1)
            pe.wait_ge(sem["g_lo"], NT)

        def ygla_sp(sp):
            def body(k, n, grp, j, early):
                slot = (j - SL_YGLA) % RING
                if not early:
                    sp.wait_ge(sem["y_evac"], k - RING + 1)
                sp.dma_start(y_in[:, slot, :], proj_d[k + ROW_AG, :, :]).then_inc(y_ins[slot], 16)
                if not (isinstance(k, int) and k == 0):
                    out_store(k - 1, (slot - 1) % RING)
                stream_step(sp, n, j)

            def out_store(k, slot):
                sp.wait_ge(sem["y_evac"], k + 1)
                sp.dma_start(gla_d[k, :, :], y_out[:, slot, :]).then_inc(y_st[slot], 16)
            repeat(sp, SL_YGLA, KT, body)
            out_store(KT - 1, (KT - 1) % RING)
            for j in range(RING):
                sp.wait_ge(y_st[j], 16 * KT // RING)

        def ygla_dve(dve):
            def body(k, c, grp, slot, early):
                dve.wait_ge(sem["mm_half"], 2 * k + 2 * SL_YGLA + 2)
                dve.wait_ge(y_ins[slot], 16 * grp + 16)
                if not early:
                    dve.wait_ge(y_st[slot], 16 * grp)
                nc.vector.tensor_tensor(y_out[:, slot, :], pair_view(slot), y_in[:, slot, :], ALU.mult
                                        ).then_inc(sem["y_evac"], 1)
            repeat(dve, 0, KT, body)

        def ygla_pe(pe):
            def body(k, n, grp, j, early):
                if not early:
                    pe.wait_ge(sem["y_evac"], k - RING + 1)
                slab_product(pe, n, j, (j - SL_YGLA) % RING)
            repeat(pe, SL_YGLA, KT, body)

        RS = 4 * HEADS

        def ret_sp(sp, hf):
            if hf == 0:
                sp.dma_start(ret_dec[:, :, :].rearrange("p h n -> p (h n)"), ret_dec_in).then_inc(sem["r_tab_in"], 16)
                sp.dma_start(ret_q[:, :, :].rearrange("p h n -> p (h n)"), ret_q_in).then_inc(sem["r_tab_in"], 16)
                sp.dma_start(ret_k[:, :], ret_k_in).then_inc(sem["r_tab_in"], 16)
                sp.dma_start(cossin[:, :, :], rope_d.rearrange("a p n -> p a n")).then_inc(sem["r_tab_in"], 16)

            def body(k, e, t, h, early):
                if not early:
                    sp.wait_ge(sem["r_og"], e - 3)
                cols = tile_cols(t)
                sp.dma_start(r_x[:, h, 0:8, :], proj_d[ROW_RET + 8 * h:ROW_RET + 8 * h + 8, :, cols]
                             .rearrange("r p n -> p r n")).then_inc(r_in[h], 16)
                sp.dma_start(r_x[:, h, 8:12, :], proj_d[ROW_RG + 4 * h:ROW_RG + 4 * h + 4, :, cols]
                             .rearrange("r p n -> p r n")).then_inc(r_in[h], 16)
            repeat(sp, hf * RS, RS, body)

        def ret_pool(pool, hf):
            if hf == 0:
                pool.wait_ge(sem["r_tab_in"], 64)

            def split_lo(e, g, h):
                b = h % 2
                pool.wait_ge(sem["r_hi"], e + 1)
                pool.wait_ge(sem["r_tab_in"], 64)
                dst = act_lo_r[:, 4 * h:4 * h + 4, tile_cols(g)]
                nc.gpsimd.tensor_tensor(dst, r_ogb[:, b, :].rearrange("p (q n) -> p q n", q=4),
                                        act_r[:, 4 * h:4 * h + 4, tile_cols(g)].bitcast(F32),
                                        ALU.subtract).then_inc(sem["r_lo"], 1)

            def body(k, e, t, h, early):
                b = h % 2
                x4 = r_x[:, h, 0:4, :]
                pool.wait_ge(sem["r_tab_in"], 64)
                pool.wait_ge(r_in[h], 32 * t + 32)
                cos = cossin[:, 0, tile_cols(t)].unsqueeze(1).to_broadcast((P, 4, P))
                sin = cossin[:, 1, tile_cols(t)].unsqueeze(1).to_broadcast((P, 4, P))
                nc.gpsimd.tensor_tensor(r_xcb[:, b, :, :], x4, cos, ALU.mult).then_inc(sem["r_xc"], 1)
                nc.gpsimd.tensor_tensor(r_xsb[:, b, :, :], x4, sin, ALU.mult).then_inc(sem["r_xs"], 1)
                pool.wait_ge(sem["r_xc"], e + 1)
                pool.wait_ge(sem["r_xs"], e + 1)
                if not (hf == 0 and early and h < 2):
                    pool.wait_ge(sem["r_o"], e - 1)
                xc = r_xcb[:, b, :, :].rearrange("p (a c) n -> p a c n", c=2)
                xs = r_xsb[:, b, :, :].rearrange("p (a c) n -> p a c n", c=2)
                qk = r_qk[:, b, :, :].rearrange("p (a c) n -> p a c n", c=2)
                nc.gpsimd.tensor_tensor(qk[:, :, 0, :], xc[:, :, 0, :], xs[:, :, 1, :], ALU.subtract
                                        ).then_inc(sem["r_rope"], 1)
                nc.gpsimd.tensor_tensor(qk[:, :, 1, :], xs[:, :, 0, :], xc[:, :, 1, :], ALU.add
                                        ).then_inc(sem["r_rope"], 1)
                pool.wait_ge(sem["r_rope"], 2 * e + 2)
                nc.gpsimd.tensor_tensor(r_qdb[:, b, :, :], r_qk[:, b, 0:2, :],
                                        ret_q[:, h, :].unsqueeze(1).to_broadcast((P, 2, P)),
                                        ALU.mult).then_inc(sem["r_qd"], 1)
                if not (early and h < 2):
                    split_lo(e - 2, (k - 2) // 4 if isinstance(k, int) else (t - 4 * hf if h >= 2 else t - 4 * hf - 1),
                             (h - 2) % 4)
            repeat(pool, hf * RS, RS, body)
            for k in (RS - 2, RS - 1):
                split_lo(hf * RS + k, k // 4, k % 4)

        def ret_act(act, hf):
            def rstd(e, b):
                act.wait_ge(sem["r_mv"], e + 1)
                nc.scalar.activation(r_rsb[:, b, 0:1], r_mvb[:, b, 1:2], ACT.Ln, bias=eps_col[:, 0:1]
                                     ).then_inc(sem["r_lnv"], 1)
                act.wait_ge(sem["r_lnv"], e + 1)
                nc.scalar.activation(r_rsb[:, b, 1:2], r_rsb[:, b, 0:1], ACT.Exp, scale=-0.5
                                     ).then_inc(sem["r_rstd"], 1)

            def split_hi(e, g, h):
                act.wait_ge(sem["r_og"], e + 1)
                act.wait_ge(sem["r_tab_in"], 64)
                nc.scalar.activation(act_r[:, 4 * h:4 * h + 4, tile_cols(g)],
                                     r_ogb[:, h % 2, :].rearrange("p (q n) -> p q n", q=4), ACT.Copy
                                     ).then_inc(sem["r_hi"], 1)

            def body(k, e, t, h, early):
                b = h % 2
                act.wait_ge(sem["r_vT"], e + 1)
                if not (hf == 0 and early and h < 2):
                    act.wait_ge(sem["r_u"], e - 1)
                nc.scalar.activation(r_vt[:, b, :], psum[:, 0, :], ACT.Copy).then_inc(sem["r_v"], 1)
                act.wait_ge(sem["r_kT"], e + 1)
                nc.scalar.activation(r_kdt[:, b, :], psum[:, 1, 0:RET_DK], ACT.Copy, scale=ret_k[:, h:h + 1]
                                     ).then_inc(sem["r_kd"], 1)
                if not (early and h < 1):
                    rstd(e - 1, 1 - b)
                if not (early and h < 2):
                    split_hi(e - 2, (k - 2) // 4 if isinstance(k, int) else (t - 4 * hf if h >= 2 else t - 4 * hf - 1),
                             (h - 2) % 4)
            if hf == 0:
                act.wait_ge(sem["r_tab_in"], 64)
            repeat(act, hf * RS, RS, body)
            last = hf * RS + RS - 1
            rstd(last, 1)
            split_hi(last - 1, 3, 2)
            split_hi(last, 3, 3)

        def ret_dve(dve, hf):
            if hf == 0:
                nc.vector.memset(r_st[:, :, :, :].rearrange("p h a n -> p (h a n)"), 0.0
                                 ).then_inc(sem["state_zero"], 1)
                dve.wait_ge(sem["state_zero"], 2)
                dve.wait_ge(sem["r_tab_in"], 64)

            def gate(e, h):
                b = h % 2
                dve.wait_ge(sem["r_onT"], e + 1)
                if not (isinstance(e, int) and e < 2):
                    dve.wait_ge(sem["r_lo"], e - 1)
                nc.vector.tensor_tensor(r_ogb[:, b, :], psum[:, 6, :],
                                        r_x[:, h, 8:12, :].rearrange("p q n -> p (q n)"),
                                        ALU.mult).then_inc(sem["r_og"], 1)

            def outputs(e, h, no_on_wait):
                b = h % 2
                o = psum[:, 3 if b == 0 else 7, :]
                dve.wait_ge(sem["r_o"], e + 1)
                nc.vector.bn_stats(r_bst[:, b, 0:6], o).then_inc(sem["r_bn"], 1)
                dve.wait_ge(sem["r_tab_in"], 64)
                dve.wait_ge(sem["r_bn"], e + 1)
                nc.vector.bn_aggr(r_mvb[:, b, :], r_bst[:, b, 0:6]).then_inc(sem["r_mv"], 1)
                dve.wait_ge(sem["r_u"], e + 1)
                gamma_tile = (1.0 - 2.0 ** (-5.0 - h)) ** P
                for a in range(2):
                    nc.vector.scalar_tensor_tensor(r_st[:, h, a, :], r_st[:, h, a, :], gamma_tile,
                                                   psum[:, 4 + a, :], ALU.mult, ALU.add
                                                   ).then_inc(sem["r_state"], 1)
                dve.wait_ge(sem["r_rstd"], e + 1)
                dve.wait_ge(sem["r_mv"], e + 1)
                if not no_on_wait:
                    dve.wait_ge(sem["r_onT"], e - 1)
                nc.vector.tensor_scalar(r_onb[:, b, :], o, r_mvb[:, b, 0:1], r_rsb[:, b, 1:2],
                                        ALU.subtract, ALU.mult).then_inc(sem["r_on"], 1)

            def body(k, e, t, h, early):
                b = h % 2
                dve.wait_ge(sem["r_S"], e + 1)
                if not (hf == 0 and early and h < 2):
                    dve.wait_ge(sem["r_o"], e - 1)
                nc.vector.tensor_tensor(r_pt[:, b, :], psum[:, 2, 0:P], ret_dec[:, h, :], ALU.mult
                                        ).then_inc(sem["r_P"], 1)
                if not (early and h < 2):
                    gate(e - 2, (h - 2) % 4)
                if not (early and h < 1):
                    outputs(e - 1, (h - 1) % 4, hf == 0 and early and h - 1 < 2)
            repeat(dve, hf * RS, RS, body)
            last = hf * RS + RS - 1
            gate(last - 1, 2)
            outputs(last, 3, False)
            gate(last, 3)

        def ret_pe(pe, hf):
            if hf == 0:
                pe.wait_ge(sem["state_zero"], 2)

            def output(e, h, first_tile):
                b = h % 2
                o = psum[:, 3 if b == 0 else 7, :]
                pe.wait_ge(sem["r_P"], e + 1)
                pe.wait_ge(sem["r_v"], e + 1)
                pe.wait_ge(sem["r_qd"], e + 1)
                if not first_tile:
                    pe.wait_ge(sem["r_state"], 2 * e - 6)
                nc.tensor.matmul(o, r_pt[:, b, :], r_vt[:, b, :], start=True, stop=False)
                for a in range(2):
                    last = nc.tensor.matmul(o, r_qdb[:, b, a, :], r_st[:, h, a, :], start=False, stop=a == 1)
                last.then_inc(sem["r_o"], 1)
                pe.wait_ge(sem["r_kd"], e + 1)
                if not (isinstance(e, int) and e < 1):
                    pe.wait_ge(sem["r_state"], 2 * e)
                for a in range(2):
                    last = nc.tensor.matmul(psum[:, 4 + a, :], r_kdt[:, b, a * P:(a + 1) * P], r_vt[:, b, :],
                                            start=True, stop=True)
                last.then_inc(sem["r_u"], 1)

            def out_transposes(e, h):
                pe.wait_ge(sem["r_on"], e + 1)
                if not (isinstance(e, int) and e < 1):
                    pe.wait_ge(sem["r_og"], e)
                for q in range(4):
                    last = nc.tensor.transpose(psum[:, 6, q * P:(q + 1) * P],
                                               r_onb[:, h % 2, q * P:(q + 1) * P], ident[:, :])
                last.then_inc(sem["r_onT"], 1)

            def body(k, e, t, h, early):
                b = h % 2
                start = hf == 0 and early and h == 0
                pe.wait_ge(r_in[h], 32 * t + 32)
                if not start:
                    pe.wait_ge(sem["r_v"], e)
                for q in range(4):
                    last = nc.tensor.transpose(psum[:, 0, q * P:(q + 1) * P], r_x[:, h, 4 + q, :], ident[:, :])
                last.then_inc(sem["r_vT"], 1)
                pe.wait_ge(sem["r_rope"], 2 * e + 2)
                if not start:
                    pe.wait_ge(sem["r_kd"], e)
                for a in range(2):
                    last = nc.tensor.transpose(psum[:, 1, a * P:(a + 1) * P], r_qk[:, b, 2 + a, :], ident[:, :])
                last.then_inc(sem["r_kT"], 1)
                if not start:
                    pe.wait_ge(sem["r_P"], e)
                for a in range(2):
                    last = nc.tensor.matmul(psum[:, 2, 0:P], r_qk[:, b, 2 + a, :], r_qk[:, b, a, :],
                                            start=a == 0, stop=a == 1)
                last.then_inc(sem["r_S"], 1)
                if not (early and h < 2):
                    out_transposes(e - 2, (h - 2) % 4)
                if not (early and h < 1):
                    output(e - 1, (h - 1) % 4, hf == 0 and early)
            repeat(pe, hf * RS, RS, body, peel=1)
            last = hf * RS + RS - 1
            out_transposes(last - 1, 2)
            output(last, 3, False)
            out_transposes(last, 3)
            pe.wait_ge(sem["r_lo"], last + 1)

        def yret_pe(pe, hf):
            groups = 2 * KT // RING
            def group(g):
                for jj in range(RING):
                    n0 = SL_YRET + hf * 2 * KT + jj
                    kh, b = jj % 2, jj // 2
                    n = g * RING + n0
                    j = n0 % RING
                    pe.wait_ge(sem["slab_ready"], n + 1)
                    if kh == 0 and not (isinstance(g, int) and g == 0):
                        pe.wait_ge(sem["y_evac"], 2 * g + (y_count[hf] + b - 1))
                    for kk in range(KT):
                        sl = slice((kh * KT + kk) * HALF, (kh * KT + kk + 1) * HALF)
                        last = product3(psum[:, b, :], w_hi[:, j, kk * P:(kk + 1) * P],
                                        w_lo[:, j, kk * P:(kk + 1) * P], act_hi[:, sl], act_lo[:, sl],
                                        kh == 0 and kk == 0, kh == 1 and kk == KT - 1)
                        if kk % 4 == 3:
                            last.then_inc(sem["mm_half"], 1)
            group(0)
            with pe.Fori(1, groups) as g:
                group(g)

        y_count = [KT, 2 * KT]

        def yret_sp(sp, hf):
            cols = slice(hf * HALF, hf * HALF + HALF)

            def out_store(c, s, slot):
                sp.wait_ge(sem["y_evac"], s + 1)
                sp.dma_start(merged_d[c, :, cols], y_out[:, slot, 0:HALF]).then_inc(y_st[slot], 16)

            def body(c, s, grp, slot, early):
                if not early:
                    sp.wait_ge(sem["y_evac"], s - RING + 1)
                sp.dma_start(y_in[:, slot, 0:HALF], proj_d[c + ROW_AR, :, cols]).then_inc(y_ins[slot], 16)
                sp.dma_start(y_in[:, slot, HALF:], gla_d[c, :, cols]).then_inc(y_ins[slot], 16)
                if not (isinstance(c, int) and c == 0):
                    out_store(c - 1, s - 1, (slot - 1) % RING)
                for i in range(2):
                    n = 2 * c + (SL_YRET + hf * 2 * KT + i)
                    stream_step(sp, n, (SL_YRET + 2 * slot + i) % RING)
            repeat(sp, y_count[hf], KT, body)
            out_store(KT - 1, y_count[hf] + KT - 1, RING - 1)
            for j in range(RING):
                sp.wait_ge(y_st[j], 16 * (y_count[hf] + KT) // RING)

        def yret_dve(dve, hf):
            def body(c, s, grp, slot, early):
                b = slot % 2
                n = 2 * c + (SL_YRET + hf * 2 * KT + 1)
                dve.wait_ge(sem["mm_half"], 2 * n + 2)
                dve.wait_ge(y_ins[slot], 32 * grp - 16 * (KT // RING) + 32)
                nc.vector.tensor_tensor(y_tmp[:, b, :], psum[:, b, :], y_in[:, slot, 0:HALF], ALU.mult
                                        ).then_inc(sem["y_mul"], 1)
                dve.wait_ge(sem["y_mul"], s - KT + 1)
                if not early:
                    dve.wait_ge(y_st[slot], 16 * grp)
                nc.vector.tensor_tensor(y_out[:, slot, 0:HALF], y_tmp[:, b, :], y_in[:, slot, HALF:], ALU.add
                                        ).then_inc(sem["y_evac"], 1)
            repeat(dve, y_count[hf], KT, body)

        def dense_sp(sp, job, K, n0, q0, src, res, ln, dst):
            sp.dma_start(d_ln[:, :], ln.to_broadcast((P, D))).then_inc(sem["d_ln_in"], 16)
            for hf in range(2):
                rows = slice(hf * HALF, hf * HALF + HALF)
                if hf:
                    sp.wait_ge(sem["d_res"], 8 * job + 4)
                sp.dma_start(d_x[:, :, :], res[rows, :].rearrange("(t p) d -> p t d", p=P)
                             ).then_inc(sem["d_x_in"], 16)
                nn, qq = n0 + hf * K, q0 + hf * K

                def body(k, q, grp, slot, early, nn=nn, hf=hf, base=0, stream=True):
                    if not (isinstance(q, int) and q < RING):
                        sp.wait_ge(sem["d_lo"], q - RING + 1)
                    sp.dma_start(d_raw[:, slot, :], src[k + base, :, hf * HALF:hf * HALF + HALF]
                                 ).then_inc(d_in[slot], 16)
                    if stream:
                        stream_step(sp, k + (nn + base), (slot + n0 - q0) % RING)
                tail = max(0, min(K, nn + K + 2 * RING - N_SLABS))
                repeat(sp, qq, K - tail, body)
                if tail:
                    repeat(sp, qq + K - tail, tail,
                           lambda k, q, g, s, e, body=body, base=K - tail: body(k, q, g, s, e, base=base, stream=False))
                if hf:
                    store(sp, job, 0, dst)
            store(sp, job, 1, dst)
            sp.wait_ge(sem["d_stored"], 32 * job + 32)

        def store(sp, job, hf, dst):
            sp.wait_ge(sem["d_res"], 8 * job + 4 * hf + 4)
            sp.dma_start(dst[hf * HALF:hf * HALF + HALF, :].rearrange("(t p) d -> p t d", p=P), d_out[:, :, :]
                         ).then_inc(sem["d_stored"], 16)

        def dense_pe(pe, job, K, n0, q0):
            for hf in range(2):
                if job or hf:
                    pe.wait_ge(sem["d_act_evac"], 4 * job + 2 * hf)
                    pe.wait_ge(sem["d_dve_evac"], 4 * job + 2 * hf)

                def body(k, q, grp, slot, early):
                    j = (slot + n0 - q0) % RING
                    pe.wait_ge(sem["slab_ready"], k + (n0 + hf * K + 1))
                    pe.wait_ge(sem["d_lo"], q + 1)
                    start = isinstance(k, int) and k == 0
                    stop = isinstance(k, int) and k == K - 1
                    for tok in range(4):
                        s_hi = d_hib[:, slot, tok * P:(tok + 1) * P]
                        s_lo = d_lob[:, slot, tok * P:(tok + 1) * P]
                        for cc in range(2):
                            last = product3(psum[:, 2 * tok + cc, :], s_hi, s_lo,
                                            w_hi[:, j, cc * HALF:(cc + 1) * HALF],
                                            w_lo[:, j, cc * HALF:(cc + 1) * HALF], start, stop)
                        if tok % 2:
                            last.then_inc(sem["mm_half"], 1)
                repeat(pe, q0 + hf * K, K, body)

        def dense_act(act, job, K, n0, q0):
            for hf in range(2):
                def body(k, q, grp, slot, early):
                    act.wait_ge(d_in[slot], 16 * grp + 16)
                    if not (isinstance(q, int) and q < RING):
                        act.wait_ge(sem["mm_half"], 2 * k + 2 * (n0 + hf * K - RING) + 2)
                    nc.scalar.activation(d_hib[:, slot, :], d_raw[:, slot, :], ACT.Copy
                                         ).then_inc(sem["d_hi"], 1)
                repeat(act, q0 + hf * K, K, body)
                e = 2 * job + hf
                act.wait_ge(sem["mm_half"], 2 * (n0 + hf * K + K))
                if e:
                    act.wait_ge(sem["d_stored"], 16 * e)
                for tok in (0, 1):
                    nc.scalar.activation(d_out[:, tok, :], pair_view(tok), ACT.Copy
                                         ).then_inc(sem["d_act_evac"], 1)
                act.wait_ge(sem["d_act_evac"], 2 * e + 2)
                act.wait_ge(sem["d_dve_evac"], 2 * e + 2)
                for tok in range(4):
                    if e or tok:
                        act.wait_ge(sem["d_sq"], 4 * e + tok)
                    nc.scalar.activation(d_junk[:, :], d_out[:, tok, :], ACT.Square,
                                         accum_out=stat[:, 32 + tok:33 + tok]).then_inc(sem["d_sq"], 1)
                act.wait_ge(sem["d_sq"], 4 * e + 4)
                nc.scalar.activation(stat[:, 36:40], stat[:, 32:36], ACT.Sqrt, scale=1.0 / D,
                                     bias=eps_col[:, 0:1]).then_inc(sem["d_std"], 1)

        def dense_dve(dve, job, K, n0, q0):
            for hf in range(2):
                def body(k, q, grp, slot, early):
                    dve.wait_ge(sem["d_hi"], q + 1)
                    nc.vector.tensor_tensor(d_lob[:, slot, :], d_raw[:, slot, :], d_hib[:, slot, :].bitcast(F32),
                                            ALU.subtract).then_inc(sem["d_lo"], 1)
                repeat(dve, q0 + hf * K, K, body)
                e = 2 * job + hf
                dve.wait_ge(sem["mm_half"], 2 * (n0 + hf * K + K))
                if e:
                    dve.wait_ge(sem["d_stored"], 16 * e)
                for tok in (2, 3):
                    nc.vector.tensor_copy(d_out[:, tok, :], pair_view(tok)).then_inc(sem["d_dve_evac"], 1)
                dve.wait_ge(sem["d_std"], e + 1)
                nc.vector.reciprocal(stat[:, 40:44], stat[:, 36:40]).then_inc(sem["d_rstd"], 1)
                dve.wait_ge(sem["d_rstd"], e + 1)
                dve.wait_ge(sem["d_ln_in"], 16 * job + 16)
                dve.wait_ge(sem["d_x_in"], 16 * e + 16)
                for tok in range(4):
                    nc.vector.scalar_tensor_tensor(d_out[:, tok, :], d_out[:, tok, :],
                                                   stat[:, 40 + tok:41 + tok], d_ln[:, :],
                                                   ALU.mult, ALU.mult).then_inc(sem["d_scaled"], 1)
                for tok in range(4):
                    dve.wait_ge(sem["d_scaled"], 4 * e + tok + 1)
                    nc.vector.tensor_tensor(d_out[:, tok, :], d_out[:, tok, :], d_x[:, tok, :], ALU.add
                                            ).then_inc(sem["d_res"], 1)

        def up_sp(sp):
            def pair(p, s, grp, slot, early):
                for i in range(2):
                    n = 2 * p + (SL_UP + i)
                    stream_step(sp, n, (SL_UP + 2 * slot + i) % RING)
                sp.wait_ge(sem["u_f"], p + 1)
                sp.dma_start(f_d[p, :, :], u_fb[:, slot, :]).then_inc(stored[slot], 16)
            repeat(sp, 0, FT, pair)
            for j in range(RING):
                sp.wait_ge(stored[j], 16 * (N_PROJ // RING) + 16 * len(range(j, FT, RING)))

        def up_act(act):
            def pair(p, s, grp, b, early):
                for i in range(2):
                    k = 2 * p + i
                    act.wait_ge(sem["mm_half"], 2 * k + 2 * SL_UP + 2)
                    if not early:
                        act.wait_ge(sem["u_f"], p - 1)
                    act.wait_ge(sem["const_in"], 64)
                    nc.scalar.activation(u_conv[:, 2 * b + i, :], pair_view(2 * b + i), ACT.Identity,
                                         scale=col(k, 2), bias=col(k, 3)).then_inc(sem["u_lin"], 1)
                act.wait_ge(sem["u_tap0"], 2 * p + 2)
                nc.scalar.activation(u_conv[:, 2 * b + 1, :], u_conv[:, 2 * b + 1, :], ACT.Gelu_apprx_tanh
                                     ).then_inc(sem["u_gelu"], 1)
            repeat(act, 0, FT, pair, unroll=2)

        def col(k, tap):
            return conv_col[:, 4 * k + tap:4 * k + tap + 1] if isinstance(k, int) else \
                conv_col[:, bass.ds(4 * k + tap, 1)]

        def up_dve(dve):
            def pair(p, s, grp, slot, early):
                for i in range(2):
                    k = 2 * p + i
                    b = (2 * slot + i) % RING
                    dve.wait_ge(sem["u_lin"], k + 1)
                    dve.wait_ge(sem["const_in"], 64)
                    nc.vector.scalar_tensor_tensor(u_conv[:, b, 1:], pair_view(b)[:, 0:SEQ - 1], col(k, 1),
                                                   u_conv[:, b, 1:], ALU.mult, ALU.add
                                                   ).then_inc(sem["u_tap1"], 1)
                    dve.wait_ge(sem["u_tap1"], k + 1)
                    dve.wait_ge(sem["const_in"], 64)
                    nc.vector.scalar_tensor_tensor(u_conv[:, b, 2:], pair_view(b)[:, 0:SEQ - 2], col(k, 0),
                                                   u_conv[:, b, 2:], ALU.mult, ALU.add
                                                   ).then_inc(sem["u_tap0"], 1)
                if not early:
                    dve.wait_ge(stored[slot], 16 * (N_PROJ // RING) + 16 * grp)
                dve.wait_ge(sem["u_gelu"], p + 1)
                b = (2 * slot) % RING
                nc.vector.tensor_tensor(u_fb[:, slot, :], u_conv[:, b, :], u_conv[:, b + 1, :], ALU.mult
                                        ).then_inc(sem["u_f"], 1)
            repeat(dve, 0, FT, pair)

        def up_pe(pe):
            def body(k, n, grp, j, early):
                if not early:
                    pe.wait_ge(sem["u_tap0"], k - RING + 1)
                slab_product(pe, n, j, (j - SL_UP) % RING)
            repeat(pe, SL_UP, 2 * FT, body)

        block = ctx.enter_context(nc.Block())
        MIX = dict(job=0, K=KT, n0=SL_MIX, q0=0)
        DOWN = dict(job=1, K=FT, n0=SL_DOWN, q0=2 * KT)

        @block.sync
        def _(sp):
            sp.dma_start(ident[:, :], ident_in).then_inc(sem["const_in"], 16)
            sp.dma_start(ln_col[:, :, :], ln_cols_in).then_inc(sem["const_in"], 16)
            sp.dma_start(conv_col[:, :], conv_in).then_inc(sem["const_in"], 16)
            sp.dma_start(eps_col[:, :], eps_in).then_inc(sem["const_in"], 16)
            norm_sp(sp, x)
            stream_prologue(sp)
            phases = (proj_sp, gla_sp, ygla_sp, lambda e: ret_sp(e, 0), lambda e: yret_sp(e, 0),
                      lambda e: ret_sp(e, 1), lambda e: yret_sp(e, 1),
                      lambda e: dense_sp(e, **MIX, src=merged_d, res=x, ln=ln_post_mix, dst=x1_d),
                      lambda e: norm_sp(e, x1_d), up_sp,
                      lambda e: dense_sp(e, **DOWN, src=f_d, res=x1_d, ln=ln_post_ffn, dst=out))
            for i, phase in enumerate(phases):
                sp.sem_inc(sem["phase_done"], 1)
                begin_phase(sp, i + 1)
                phase(sp)

        @block.tensor
        def _(pe):
            pe.wait_ge(sem["const_in"], 64)
            phases = (lambda e: norm_pe(e, 0), proj_pe, gla_pe, ygla_pe, lambda e: ret_pe(e, 0),
                      lambda e: yret_pe(e, 0), lambda e: ret_pe(e, 1), lambda e: yret_pe(e, 1),
                      lambda e: dense_pe(e, **MIX), lambda e: norm_pe(e, 1), up_pe,
                      lambda e: dense_pe(e, **DOWN))
            for i, phase in enumerate(phases):
                begin_phase(pe, i)
                phase(pe)
                end_phase(pe)

        @block.scalar
        def _(act):
            phases = (lambda e: norm_act(e, 0), proj_act, gla_act, lambda e: None, lambda e: ret_act(e, 0),
                      lambda e: None, lambda e: ret_act(e, 1), lambda e: None,
                      lambda e: dense_act(e, **MIX), lambda e: norm_act(e, 1), up_act,
                      lambda e: dense_act(e, **DOWN))
            for i, phase in enumerate(phases):
                begin_phase(act, i)
                phase(act)
                end_phase(act)

        @block.vector
        def _(dve):
            dve.wait_ge(sem["const_in"], 64)
            phases = (lambda e: norm_dve(e, 0), proj_dve, gla_dve, ygla_dve, lambda e: ret_dve(e, 0),
                      lambda e: yret_dve(e, 0), lambda e: ret_dve(e, 1), lambda e: yret_dve(e, 1),
                      lambda e: dense_dve(e, **MIX), lambda e: norm_dve(e, 1), up_dve,
                      lambda e: dense_dve(e, **DOWN))
            for i, phase in enumerate(phases):
                begin_phase(dve, i)
                phase(dve)
                end_phase(dve)

        @block.gpsimd
        def _(pool):
            nc.gpsimd.memset(zero_col[:, :], 0.0).then_inc(sem["zero_set"], 1)
            pool.wait_ge(sem["zero_set"], 1)
            split_slabs(pool, 0, SL_YGLA + RING)
            begin_phase(pool, 2)
            gla_pool(pool)
            split_slabs(pool, SL_YGLA + RING, SL_YRET + RING)
            begin_phase(pool, 4)
            ret_pool(pool, 0)
            split_slabs(pool, SL_YRET + RING, SL_YRET + 2 * KT + RING)
            begin_phase(pool, 6)
            ret_pool(pool, 1)
            split_slabs(pool, SL_YRET + 2 * KT + RING, N_SLABS)


def kernel(**inputs):
    import numpy as _np
    import concourse.bacc as _bacc
    from concourse import mybir as _mybir
    from concourse.bass_utils import run_bass_kernel_spmd as _run

    a = {k: _np.asarray(v) for k, v in inputs.items()}

    def slabs(w, cols=None):
        cols = range(0, w.shape[1], P) if cols is None else cols
        return [w[:, c:c + P].reshape(KT, P, P).transpose(1, 0, 2).reshape(P, D) for c in cols]

    w_in, w_up, w_down = a["w_in"][0], a["w_ffn_up"][0], a["w_ffn_down"][0]
    w_ret, w_mix = a["w_ret_out"][0], a["w_mix_out"][0]
    lr = _np.zeros((D, P), _np.float32)
    lr[:, :GLA_RANK] = w_in[:, O_LR:O_LR + GLA_RANK]
    ret = [s for c in range(KT) for kh in range(2)
           for s in slabs(w_ret[kh * D:(kh + 1) * D], [c * P])]
    rows = lambda w: [w[k * P:(k + 1) * P] for k in range(w.shape[0] // P)]
    stream = (slabs(lr) + slabs(w_in, projection_columns()) + slabs(a["w_gla_out"][0]) + ret + ret
              + rows(w_mix) + rows(w_mix)
              + slabs(w_up, [v for p in range(FT) for v in (p * P, D_FF + p * P)])
              + rows(w_down) + rows(w_down))
    w_stream = _np.stack(stream)
    assert w_stream.shape[0] == N_SLABS
    pair_cols = [v for p in range(FT) for v in (p * P, D_FF + p * P)]
    taps = _np.concatenate([a["conv_w"][0], a["conv_b"]], 0)
    conv = _np.stack([taps[:, c:c + P] for c in pair_cols]).transpose(2, 0, 1).reshape(P, -1)
    ln_cols = _np.stack([a["ln_pre_mix"][0].reshape(KT, P).T, a["ln_pre_ffn"][0].reshape(KT, P).T], 1)
    ret_dec, ret_q, ret_k = retention_tables()
    inv_freq = (10000.0 ** (-_np.arange(0, RET_DK, 2) / RET_DK)).astype(_np.float32).reshape(P, 1)
    feeds = {
        "x": a["x"][0], "positions": a["positions"], "w_stream": w_stream, "w_dec": a["w_gla_decay"][0],
        "b_dec": a["b_gla_decay"], "ln_post_mix": a["ln_post_mix"], "ln_post_ffn": a["ln_post_ffn"],
        "ln_cols_in": ln_cols, "conv_in": conv, "ident_in": _np.eye(P, dtype=_np.float32),
        "interval_in": interval_table(), "masks_in": level_masks(), "ret_dec_in": ret_dec,
        "ret_q_in": ret_q, "ret_k_in": ret_k, "inv_freq_in": inv_freq,
        "eps_in": _np.full((P, 1), EPS, _np.float32),
    }
    nc = _bacc.Bacc("TRN2", target_bir_lowering=False, num_devices=1)
    arrays, args = {}, {}
    for name, v in feeds.items():
        v = _np.ascontiguousarray(v)
        arrays[f"in_{name}"] = v
        args[name] = nc.dram_tensor(f"in_{name}", v.shape, _mybir.dt.from_np(v.dtype), kind="ExternalInput").ap()
    out = nc.dram_tensor("out_0", (SEQ, D), F32, kind="ExternalOutput").ap()
    build(nc, out=out, **args)
    r = _run(nc, [arrays], core_ids=[0])
    return _np.asarray(r.results[0]["out_0"]).reshape(a["x"].shape)
```

```python
import math
from contextlib import ExitStack

import numpy as np

import concourse.bass as bass
from concourse import mybir

F32 = mybir.dt.float32
F32R = mybir.dt.float32r
I32 = mybir.dt.int32
ALU = mybir.AluOpType
ACT = mybir.ActivationFunctionType
AX = mybir.AxisListType

ACT_SET_EXP_LN = 6

P = 128
D = 1024
SEQ = 1024
KT = D // P
NT = SEQ // P
HALF = 512
CHUNK = 64
EPS = 1e-6
HEADS = 4
GLA_DK, GLA_DV, GLA_RANK, GLA_TAU = D // 8, D // 4, 16, 16.0
RET_DK, RET_DV = D // 4, D // 2
D_FF = 2816
FT = D_FF // P
GLA_QK, GLA_V, RET_QK, RET_V = HEADS * GLA_DK, HEADS * GLA_DV, HEADS * RET_DK, HEADS * RET_DV
GLA_KT, RET_KT = GLA_V // P, RET_V // P

_SPLITS = (GLA_QK, GLA_QK, GLA_V, GLA_V, GLA_RANK, RET_QK, RET_QK, RET_V, RET_V, D, D)
_OFF = [0]
for _s in _SPLITS:
    _OFF.append(_OFF[-1] + _s)
O_GQ, O_GK, O_GV, O_GR, O_LR, O_RQ, O_RK, O_RV, O_RG, O_AG, O_AR = _OFF[:11]


def projection_columns():
    cols = []
    for h in range(HEADS):
        cols += [O_GQ + h * P, O_GK + h * P, O_GV + h * 2 * P, O_GV + h * 2 * P + P]
    for h in range(HEADS):
        cols += [O_RQ + h * 2 * P, O_RQ + h * 2 * P + P, O_RK + h * 2 * P, O_RK + h * 2 * P + P]
        cols += [O_RV + (4 * h + j) * P for j in range(4)]
    cols += [O_GR + j * P for j in range(GLA_KT)]
    cols += [O_RG + j * P for j in range(RET_KT)]
    cols += [O_AG + j * P for j in range(KT)]
    cols += [O_AR + j * P for j in range(KT)]
    return cols


N_PROJ = len(projection_columns())
ROW_GLA, ROW_RET = 0, 4 * HEADS
ROW_GR = ROW_RET + 8 * HEADS
ROW_RG = ROW_GR + GLA_KT
ROW_AG = ROW_RG + RET_KT
ROW_AR = ROW_AG + KT
SL_LR = 0
SL_PROJ = 1
SL_YGLA = SL_PROJ + N_PROJ
SL_YRET = SL_YGLA + KT
SL_MIX = SL_YRET + 2 * 2 * KT
SL_UP = SL_MIX + 2 * KT
SL_DOWN = SL_UP + 2 * FT
N_SLABS = SL_DOWN + 2 * FT
RING = 4

LEVELS = [128 >> i for i in range(7)]
NL = len(LEVELS)
E_BLOCKS = NL + 2


def interval_table():
    m, n = np.meshgrid(np.arange(P), np.arange(P), indexing="ij")
    t = np.zeros((P, E_BLOCKS, P), np.float32)
    t[:, 0] = m > n
    for i, b in enumerate(LEVELS):
        mid = (n // b) * b + b // 2
        t[:, 1 + i] = np.where(n >= mid, (m >= mid) & (m <= n), (m > n) & (m < mid))
    t[:, NL + 1] = m <= n
    return (t / GLA_TAU).astype(np.float32).reshape(P, E_BLOCKS * P)


def level_masks():
    m, n = np.meshgrid(np.arange(P), np.arange(P), indexing="ij")
    t = np.zeros((P, NL + 1, P), np.float32)
    for i, b in enumerate(LEVELS):
        same = (m // b) == (n // b)
        mid = (n // b) * b + b // 2
        t[:, i] = same & ((m >= mid) != (n >= mid)) & (m // CHUNK <= n // CHUNK)
    t[:, NL] = m == n
    return (t * GLA_DK ** -0.5).astype(np.float32).reshape(P, (NL + 1) * P)


def retention_tables():
    g = 1.0 - 2.0 ** (-5.0 - np.arange(HEADS))
    m, n = np.meshgrid(np.arange(P), np.arange(P), indexing="ij")
    scale = RET_DK ** -0.5
    dec = np.stack([g[h] ** np.abs(n - m) * (m // CHUNK <= n // CHUNK) * scale for h in range(HEADS)], 1)
    qd = np.stack([g[h] ** (n + 1.0) for h in range(HEADS)], 1)
    kd = np.stack([g[h] ** (P - 1.0 - np.arange(P)) * scale for h in range(HEADS)], 1)
    return (dec.reshape(P, -1).astype(np.float32), qd.reshape(P, -1).astype(np.float32),
            kd.astype(np.float32))


def two_pi_parts(bits=7, count=7):
    parts, rest = [], 2.0 * math.pi
    for _ in range(count):
        e = math.floor(math.log2(rest)) - (bits - 1)
        part = math.floor(rest / 2.0 ** e) * 2.0 ** e
        parts.append(part)
        rest -= part
    return parts


SEMS = """
const_in const2_in x_in0 x_in1 x_in2 x_in3 sq_done rms_std rms_rstd x_scaled x_transposed
act_hi_done act_lo_done raw_in0 raw_in1 raw_in2 raw_in3 hi_split slab_ready mm_half
lr_in lr_out lr_ones z_out z_copied z_abs z_exp z_ln log_a loga_stored
pos_in pos_f turns0 turns1 angle angle_red sin_half cos_sq rope_done rope_stored
proj_evac st0 st1 st2 st3
g_in0 g_in1 g_gate_in g_tab_in g_tab g_la_hi g_la_lo g_vT g_v g_E g_exp g_qlev g_qG g_dec g_klev g_kend
g_S g_mask g_P g_kT g_kd g_o g_u g_state g_bn g_mv g_lnv g_rstd g_on g_onT g_og g_hi g_lo
r_tab_in r_in0 r_in1 r_in2 r_in3 r_gate_in0 r_gate_in1 r_gate_in2 r_gate_in3 r_xc r_xs r_rope r_qd r_kT r_kd r_vT r_v r_S r_P r_o r_u r_state
r_bn r_mv r_lnv r_rstd r_on r_onT r_og r_hi r_lo state_zero
y_in0 y_in1 y_in2 y_in3 y_mul y_evac yst0 yst1 yst2 yst3
d_in0 d_in1 d_in2 d_in3 d_ln_in d_hi d_lo d_evac d_sq d_std d_rstd d_scaled d_res d_x_in
d_stored zero_set u_lin u_tap1 u_tap0 u_gelu u_f pe_phases act_phases dve_phases sp_phases n_sq
""".split()


def build(nc, x, positions, w_stream, w_dec, b_dec, ln_post_mix, ln_post_ffn, ln_cols_in, conv_in,
          ident_in, interval_in, masks_in, ret_dec_in, ret_q_in, ret_k_in, inv_freq_in, eps_in, out):
    ctx = ExitStack()
    with ctx:
        sem = {name: ctx.enter_context(nc.semaphore(name)) for name in SEMS}

        def dram(name, shape):
            return nc.dram_tensor(name, list(shape), F32, kind="Internal").ap()

        proj_d = dram("proj_scratch", (N_PROJ, P, SEQ))
        loga_d = dram("loga_scratch", (NT, P, GLA_QK))
        gla_d = dram("gated_gla_scratch", (KT, P, SEQ))
        merged_d = dram("merged_scratch", (KT, P, SEQ))
        x1_d = dram("x1_scratch", (SEQ, D))
        f_d = dram("ffn_scratch", (FT, P, SEQ))
        rope_d = dram("rope_scratch", (2, P, SEQ))

        def sb(stack, name, shape, dt=F32):
            return stack.enter_context(nc.sbuf_tensor(name, list(shape), dt))

        act_hi = sb(ctx, "act_hi", (P, KT * SEQ), F32R)
        act_lo = sb(ctx, "act_lo", (P, KT * SEQ), F32R)
        w_raw = sb(ctx, "w_raw", (P, RING, D))
        w_hi = sb(ctx, "w_hi", (P, RING, D), F32R)
        w_lo = sb(ctx, "w_lo", (P, RING, D), F32R)
        ident = sb(ctx, "ident", (P, P))
        ln_col = sb(ctx, "ln_col", (P, 2, KT))
        conv_col = sb(ctx, "conv_col", (P, 2 * FT * 4))
        eps_col = sb(ctx, "eps_col", (P, 1))
        zero_col = sb(ctx, "zero_col", (P, 1))
        stat = sb(ctx, "stat", (P, 64))
        psum = ctx.enter_context(nc.psum_tensor("psum", [P, 8, HALF], F32))
        bank = psum[:, :, :].rearrange("p b n -> p (b n)")
        act_k = act_hi[:, :].rearrange("p (k n) -> p k n", k=KT)
        act_lo_k = act_lo[:, :].rearrange("p (k n) -> p k n", k=KT)
        act_r = act_hi[:, :].rearrange("p (k n) -> p k n", k=RET_KT)
        act_lo_r = act_lo[:, :].rearrange("p (k n) -> p k n", k=RET_KT)

        with ExitStack() as s:
            x_tok = sb(s, "x_tok", (P, NT, D))
            sq_junk = sb(s, "sq_junk", (P, D))
        with ExitStack() as s:
            z_sb = sb(s, "z_sb", (P, NT, GLA_QK))
            z_a = sb(s, "z_a", (P, 2, GLA_QK))
            z_e = sb(s, "z_e", (P, 2, GLA_QK))
            lr_aug = sb(s, "lr_aug", (GLA_RANK + 1, SEQ))
            wdec_aug = sb(s, "wdec_aug", (GLA_RANK + 1, GLA_QK))
            pos_i = sb(s, "pos_i", (P, SEQ), I32)
            ang = sb(s, "ang", (P, 2, SEQ))
            turn = sb(s, "turn", (P, SEQ))
            rope_out = sb(s, "rope_out", (P, 2, SEQ))
            invf = sb(s, "invf", (P, 1))
            stage = sb(s, "stage", (P, RING, SEQ))
        with ExitStack() as s:
            g_x = sb(s, "g_x", (P, 2, 4 * HEADS, P))
            g_la = sb(s, "g_la", (P, 2, GLA_QK))
            g_gate = sb(s, "g_gate", (P, GLA_KT, P))
            masks = sb(s, "masks", (P, (NL + 1) * P))
            e_t = sb(s, "e_t", (P, 2, E_BLOCKS * P))
            g_st = sb(s, "g_st", (P, HEADS, GLA_DV))
            la_hi = sb(s, "la_hi", (P, 2, GLA_QK), F32R)
            la_lo = sb(s, "la_lo", (P, 2, GLA_QK), F32R)
            interval = sb(s, "interval", (P, E_BLOCKS * P), F32R)
            q_lev = sb(s, "q_lev", (P, 2, NL, P))
            k_lev = sb(s, "k_lev", (P, 2, NL, P))
            q_g = sb(s, "q_g", (P, 2, HEADS, P))
            k_end = sb(s, "k_end", (P, HEADS, P))
            g_vt = sb(s, "g_vt", (P, GLA_V))
            g_kdt = sb(s, "g_kdt", (P, GLA_QK))
            s_masked = sb(s, "s_masked", (P, (NL + 1) * P))
            p_t = sb(s, "p_t", (P, HEADS, P))
            g_deccol = sb(s, "g_deccol", (P, 2, HEADS))
            g_onb = sb(s, "g_onb", (P, GLA_V))
            g_ogb = sb(s, "g_ogb", (P, GLA_V))
            g_bst = sb(s, "g_bst", (P, HEADS, 8))
            g_mvb = sb(s, "g_mvb", (P, HEADS, 2))
            g_rsb = sb(s, "g_rsb", (P, 2, HEADS))
        with ExitStack() as s:
            r_st = sb(s, "r_st", (P, HEADS, 2, RET_DV))
            ret_dec = sb(s, "ret_dec", (P, HEADS, P))
            ret_q = sb(s, "ret_q", (P, HEADS, P))
            ret_k = sb(s, "ret_k", (P, HEADS))
            cossin = sb(s, "cossin", (P, 2, SEQ))
            r_x = sb(s, "r_x", (P, HEADS, 12, P))
            with ExitStack() as s2:
                r_xcb = sb(s2, "r_xcb", (P, 2, 4, P))
                r_xsb = sb(s2, "r_xsb", (P, 2, 4, P))
                r_qk = sb(s2, "r_qk", (P, HEADS, 4, P))
                r_qdb = sb(s2, "r_qdb", (P, HEADS, 2, P))
                r_kdt = sb(s2, "r_kdt", (P, 2, RET_DK))
                r_vt = sb(s2, "r_vt", (P, 2, RET_DV))
                r_pt = sb(s2, "r_pt", (P, 2, P))
                r_onb = sb(s2, "r_onb", (P, 2, RET_DV))
                r_ogb = sb(s2, "r_ogb", (P, 2, RET_DV))
                r_bst = sb(s2, "r_bst", (P, 2, 8))
                r_mvb = sb(s2, "r_mvb", (P, 2, 2))
                r_rsb = sb(s2, "r_rsb", (P, 2, 2))
            with ExitStack() as s2:
                y_in = sb(s2, "y_in", (P, RING, SEQ))
                y_out = sb(s2, "y_out", (P, RING, SEQ))
                y_tmp = sb(s2, "y_tmp", (P, 2, HALF))
        with ExitStack() as s:
            d_raw = sb(s, "d_raw", (P, RING, HALF))
            d_hib = sb(s, "d_hib", (P, RING, HALF), F32R)
            d_lob = sb(s, "d_lob", (P, RING, HALF), F32R)
            d_ln = sb(s, "d_ln", (P, D))
            d_x = sb(s, "d_x", (P, 4, D))
            d_junk = sb(s, "d_junk", (P, D))
            with ExitStack() as s2:
                d_out = sb(s2, "d_out", (P, NT, D))
            with ExitStack() as s2:
                u_conv = sb(s2, "u_conv", (P, RING, SEQ))
                u_fb = sb(s2, "u_fb", (P, RING, SEQ))

        def repeat(eng, lo, count, body, unroll=RING, peel=1):
            def group(g):
                for j in range(unroll):
                    body(g * unroll + j, g * unroll + (lo + j), g + (lo + j) // unroll,
                         (lo + j) % unroll, isinstance(g, int) and g == 0)
            groups = count // unroll
            first = min(peel, groups)
            for g in range(first):
                group(g)
            if groups - first >= 2:
                with eng.Fori(first, groups) as g:
                    group(g)
            elif groups - first == 1:
                group(first)
            for k in range(groups * unroll, count):
                body(k, lo + k, (lo + k) // unroll, (lo + k) % unroll, groups == 0)

        raw_in = [sem[f"raw_in{j}"] for j in range(RING)]
        stored = [sem[f"st{j}"] for j in range(RING)]
        x_in = [sem[f"x_in{j}"] for j in range(4)]
        g_in = [sem["g_in0"], sem["g_in1"]]
        r_in = [sem[f"r_in{j}"] for j in range(RING)]
        r_gate_in = [sem[f"r_gate_in{j}"] for j in range(RING)]
        y_ins = [sem[f"y_in{j}"] for j in range(RING)]
        y_st = [sem[f"yst{j}"] for j in range(RING)]
        d_in = [sem[f"d_in{j}"] for j in range(RING)]

        def product3(o, s_hi, s_lo, m_hi, m_lo, start, stop):
            nc.tensor.matmul(o, s_hi, m_hi, start=start, stop=False)
            nc.tensor.matmul(o, s_hi, m_lo, start=False, stop=False)
            return nc.tensor.matmul(o, s_lo, m_hi, start=False, stop=stop)

        def end_phase(eng, who):
            eng.drain().then_inc(sem[f"{who}_phases"], 1)

        def begin_phase(eng, n):
            for who in ("pe", "act", "dve", "sp"):
                eng.wait_ge(sem[f"{who}_phases"], n)

        def load_slab(sp, n, j):
            sp.dma_start(w_raw[:, j, :], w_stream[n, :, :]).then_inc(raw_in[j], 16)

        def stream_prologue(sp):
            for n in range(RING):
                load_slab(sp, n, n)
            for n in range(RING):
                sp.wait_ge(sem["slab_ready"], n + 1)
                load_slab(sp, n + RING, n)

        def stream_step(sp, n, j):
            sp.wait_ge(sem["slab_ready"], n + RING + 1)
            load_slab(sp, n + 2 * RING, j)

        def split_slabs(pool, lo, hi):
            def body(k, n, grp, j, early):
                pool.wait_ge(raw_in[j], 16 * grp + 16)
                if not (early and lo == 0):
                    pool.wait_ge(sem["mm_half"], 2 * n - 2 * RING + 2)
                nc.gpsimd.tensor_tensor(w_hi[:, j, :], w_raw[:, j, :],
                                        zero_col[:, :].to_broadcast((P, D)), ALU.add).then_inc(sem["hi_split"], 1)
                pool.wait_ge(sem["hi_split"], n + 1)
                nc.gpsimd.tensor_tensor(w_lo[:, j, :], w_raw[:, j, :], w_hi[:, j, :].bitcast(F32),
                                        ALU.subtract).then_inc(sem["slab_ready"], 1)
            repeat(pool, lo, hi - lo, body)

        def norm_sp(sp):
            for c in range(4):
                sp.dma_start(x_tok[:, 2 * c:2 * c + 2, :],
                             x[c * 256:c * 256 + 256, :].rearrange("(t p) d -> p t d", p=P)
                             ).then_inc(x_in[c], 16)

        def norm_bank(rnd, i):
            return 2 * (i % 4) + 1 if rnd and i >= KT else i % 8

        def unit_cols(i):
            k, hf = i % KT, i // KT
            return slice(k * SEQ + hf * HALF, k * SEQ + hf * HALF + HALF)

        def norm_hi(act, rnd, units):
            for i in units:
                act.wait_ge(sem["x_transposed"], 2 * KT * rnd + i + 1)
                nc.scalar.activation(act_hi[:, unit_cols(i)], psum[:, norm_bank(rnd, i), :], ACT.Copy,
                                     scale=ln_col[:, rnd, i % KT:i % KT + 1]).then_inc(sem["act_hi_done"], 1)

        def norm_lo(dve, rnd, units):
            for i in units:
                dve.wait_ge(sem["act_hi_done"], 2 * KT * rnd + i + 1)
                nc.vector.scalar_tensor_tensor(act_lo[:, unit_cols(i)], psum[:, norm_bank(rnd, i), :],
                                               ln_col[:, rnd, i % KT:i % KT + 1],
                                               act_hi[:, unit_cols(i)].bitcast(F32), ALU.mult, ALU.subtract
                                               ).then_inc(sem["act_lo_done"], 1)

        def norm_act(act):
            for hf in range(2):
                for t in range(4 * hf, 4 * hf + 4):
                    if t % 2 == 0:
                        act.wait_ge(x_in[t // 2], 16)
                    if t:
                        act.wait_ge(sem["sq_done"], t)
                    nc.scalar.activation(sq_junk[:, :], x_tok[:, t, :], ACT.Square,
                                         accum_out=stat[:, t:t + 1]).then_inc(sem["sq_done"], 1)
                act.wait_ge(sem["sq_done"], 4 * hf + 4)
                act.wait_ge(sem["const_in"], 64)
                nc.scalar.activation(stat[:, 8 + 4 * hf:12 + 4 * hf], stat[:, 4 * hf:4 * hf + 4], ACT.Sqrt,
                                     scale=1.0 / D, bias=eps_col[:, 0:1]).then_inc(sem["rms_std"], 1)
            norm_hi(act, 0, range(2 * KT))

        def norm_dve(dve):
            for hf in range(2):
                dve.wait_ge(sem["rms_std"], hf + 1)
                nc.vector.reciprocal(stat[:, 16 + 4 * hf:20 + 4 * hf], stat[:, 8 + 4 * hf:12 + 4 * hf]
                                     ).then_inc(sem["rms_rstd"], 1)
                dve.wait_ge(sem["rms_rstd"], hf + 1)
                for t in range(4 * hf, 4 * hf + 4):
                    nc.vector.tensor_scalar(x_tok[:, t, :], x_tok[:, t, :], stat[:, 16 + t:17 + t], None,
                                            ALU.mult).then_inc(sem["x_scaled"], 1)
            norm_lo(dve, 0, range(2 * KT))

        def norm_pe(pe):
            for i in range(2 * KT):
                k, hf = i % KT, i // KT
                pe.wait_ge(sem["x_scaled"], 4 * hf + 4)
                if i >= 8:
                    pe.wait_ge(sem["act_lo_done"], i - 7)
                for q in range(4):
                    last = nc.tensor.transpose(psum[:, norm_bank(0, i), q * P:(q + 1) * P],
                                               x_tok[:, 4 * hf + q, k * P:(k + 1) * P], ident[:, :])
                last.then_inc(sem["x_transposed"], 1)
            pe.wait_ge(sem["act_lo_done"], 2 * KT)

        def half_product(j, pair, hf):
            for k in range(KT):
                sl = slice(k * SEQ + hf * HALF, k * SEQ + hf * HALF + HALF)
                last = product3(psum[:, 2 * pair + hf, :], w_hi[:, j, k * P:(k + 1) * P],
                                w_lo[:, j, k * P:(k + 1) * P], act_hi[:, sl], act_lo[:, sl],
                                k == 0, k == KT - 1)
            return last

        def slab_product(pe, n, j, pair):
            pe.wait_ge(sem["slab_ready"], n + 1)
            half_product(j, pair, 0)
            half_product(j, pair, 1).then_inc(sem["mm_half"], 2)

        def pair_view(pair):
            return bank[:, pair * SEQ:(pair + 1) * SEQ]

        def proj_pe(pe):
            slab_product(pe, SL_LR, 0, 0)
            pe.wait_ge(sem["lr_out"], 2)
            pe.wait_ge(sem["lr_in"], 32)
            for t in range(NT):
                nc.tensor.matmul(psum[:, t, :], lr_aug[:, t * P:(t + 1) * P], wdec_aug[:, :],
                                 start=True, stop=True).then_inc(sem["z_out"], 1)

            def body(k, n, grp, j, early):
                pair = (j - SL_PROJ) % RING
                if early:
                    pe.wait_ge(sem["z_copied"], 2 * pair + 2)
                else:
                    pe.wait_ge(sem["proj_evac"], k - RING + 1)
                slab_product(pe, n, j, pair)
            repeat(pe, SL_PROJ, N_PROJ, body)

        def proj_act(act):
            for t in range(NT):
                b = t % 2
                act.wait_ge(sem["z_abs"], t + 1)
                nc.scalar.activation(z_e[:, b, :], z_a[:, b, :], ACT.Exp, scale=-1.0
                                     ).then_inc(sem["z_exp"], 1)
                act.wait_ge(sem["z_exp"], t + 1)
                nc.scalar.activation(z_a[:, b, :], z_e[:, b, :], ACT.Ln, bias=1.0
                                     ).then_inc(sem["z_ln"], 1)
            act.wait_ge(sem["angle_red"], 1)
            nc.scalar.activation(rope_out[:, 1, :], ang[:, 0, :], ACT.Sin).then_inc(sem["sin_half"], 1)
            nc.scalar.activation(ang[:, 1, :], ang[:, 0, :], ACT.Sin, scale=0.5).then_inc(sem["sin_half"], 1)
            for lo, hi, func in ((0, ROW_GR, ACT.Copy), (ROW_GR, ROW_AG, ACT.Silu),
                                 (ROW_AG, N_PROJ, ACT.Sigmoid)):
                def body(k, row, grp, j, early, func=func):
                    act.wait_ge(sem["mm_half"], 2 * row + 2 * SL_PROJ + 2)
                    if not (isinstance(row, int) and row < RING):
                        act.wait_ge(stored[j], 16 * grp)
                    nc.scalar.activation(stage[:, j, :], pair_view(j), func).then_inc(sem["proj_evac"], 1)
                repeat(act, lo, hi - lo, body)

        def proj_dve(dve):
            nc.vector.memset(lr_aug[:, :], 1.0).then_inc(sem["lr_ones"], 1)
            dve.wait_ge(sem["mm_half"], 2)
            dve.wait_ge(sem["lr_ones"], 1)
            for hf in range(2):
                nc.vector.tensor_copy(lr_aug[0:GLA_RANK, hf * HALF:hf * HALF + HALF],
                                      psum[0:GLA_RANK, hf, :]).then_inc(sem["lr_out"], 1)
            for t in range(NT):
                dve.wait_ge(sem["z_out"], t + 1)
                nc.vector.tensor_copy(z_sb[:, t, :], psum[:, t, :]).then_inc(sem["z_copied"], 1)

            def log_a_tail(t):
                dve.wait_ge(sem["z_ln"], t + 1)
                nc.vector.scalar_tensor_tensor(z_sb[:, t, :], z_sb[:, t, :], 0.0, z_a[:, t % 2, :],
                                               ALU.min, ALU.subtract).then_inc(sem["log_a"], 1)
            dve.wait_ge(sem["z_copied"], NT)
            for t in range(NT):
                if t >= 2:
                    log_a_tail(t - 2)
                    dve.wait_ge(sem["log_a"], t - 1)
                nc.vector.scalar_tensor_tensor(z_a[:, t % 2, :], z_sb[:, t, :], -1.0, z_sb[:, t, :],
                                               ALU.mult, ALU.max).then_inc(sem["z_abs"], 1)
            log_a_tail(NT - 2)
            log_a_tail(NT - 1)
            dve.wait_ge(sem["pos_in"], 32)
            nc.vector.tensor_copy(ang[:, 1, :], pos_i[:, :]).then_inc(sem["pos_f"], 1)
            dve.wait_ge(sem["pos_f"], 1)
            nc.vector.tensor_scalar(ang[:, 0, :], ang[:, 1, :], invf[:, 0:1], None, ALU.mult
                                    ).then_inc(sem["angle"], 1)
            dve.wait_ge(sem["angle"], 1)
            magic = 1.5 * 2.0 ** 23
            nc.vector.tensor_scalar(turn[:, :], ang[:, 0, :], 1.0 / (2.0 * math.pi), magic,
                                    ALU.mult, ALU.add).then_inc(sem["turns0"], 1)
            dve.wait_ge(sem["turns0"], 1)
            nc.vector.tensor_scalar(turn[:, :], turn[:, :], magic, None, ALU.subtract
                                    ).then_inc(sem["turns1"], 1)
            dve.wait_ge(sem["turns1"], 1)
            for i, part in enumerate(two_pi_parts()):
                nc.vector.scalar_tensor_tensor(ang[:, 0, :], turn[:, :], -part, ang[:, 0, :],
                                               ALU.mult, ALU.add).then_inc(sem["angle"], 1)
                dve.wait_ge(sem["angle"], i + 2)
            nc.vector.tensor_scalar(ang[:, 0, :], ang[:, 0, :], 3.1415925, -3.1415925,
                                    ALU.min, ALU.max).then_inc(sem["angle_red"], 1)
            dve.wait_ge(sem["sin_half"], 2)
            nc.vector.tensor_tensor(ang[:, 0, :], ang[:, 1, :], ang[:, 1, :], ALU.mult
                                    ).then_inc(sem["cos_sq"], 1)
            dve.wait_ge(sem["cos_sq"], 1)
            nc.vector.tensor_scalar(rope_out[:, 0, :], ang[:, 0, :], -2.0, 1.0, ALU.mult, ALU.add
                                    ).then_inc(sem["rope_done"], 1)

        def proj_sp(sp):
            sp.dma_start(wdec_aug[0:GLA_RANK, :], w_dec).then_inc(sem["lr_in"], 16)
            sp.dma_start(wdec_aug[GLA_RANK:GLA_RANK + 1, :], b_dec).then_inc(sem["lr_in"], 16)
            sp.dma_start(pos_i[:, :], positions.to_broadcast((P, SEQ))).then_inc(sem["pos_in"], 16)
            sp.dma_start(invf[:, :], inv_freq_in).then_inc(sem["pos_in"], 16)
            stream_step(sp, SL_LR, 0)

            def body(k, n, grp, j, early):
                slot = (j - SL_PROJ) % RING
                sp.wait_ge(sem["proj_evac"], k + 1)
                sp.dma_start(proj_d[k, :, :], stage[:, slot, :]).then_inc(stored[slot], 16)
                stream_step(sp, n, j)
            ahead = 2 * RING
            repeat(sp, SL_PROJ, N_PROJ - ahead, body)
            sp.wait_ge(sem["log_a"], NT)
            sp.dma_start(loga_d.rearrange("t p c -> p t c"), z_sb[:, :, :]).then_inc(sem["loga_stored"], 16)
            sp.wait_ge(sem["rope_done"], 1)
            sp.dma_start(rope_d.rearrange("a p n -> p a n"), rope_out[:, :, :]).then_inc(sem["rope_stored"], 16)
            sp.wait_ge(sem["loga_stored"], 16)
            sp.wait_ge(sem["rope_stored"], 16)
            for j in range(RING):
                sp.wait_ge(stored[j], 16 * (N_PROJ - ahead) // RING)
            gla_first_loads(sp)
            for k in range(N_PROJ - ahead, N_PROJ):
                body(k, SL_PROJ + k, (SL_PROJ + k) // RING, (SL_PROJ + k) % RING, False)
            for j in range(RING):
                sp.wait_ge(stored[j], 16 * N_PROJ // RING)

        o_bank, vt_bank, gate_bank = (6, 7), (6, 5), (7, 5)
        kt_bank, u_bank = 6, 5

        def tile_cols(t):
            return slice(t * P, t * P + P) if isinstance(t, int) else bass.ds(t * P, P)

        def over_gla_tiles(eng, body):
            repeat(eng, 0, NT - 1, body, unroll=2)
            body(NT - 1, NT - 1, (NT - 1) // 2, (NT - 1) % 2, False, last=True)

        def head_cols(h):
            return slice((h % 2) * GLA_DV, (h % 2 + 1) * GLA_DV)

        def gla_gates(sp, t):
            if not (isinstance(t, int) and t < 1):
                sp.wait_ge(sem["g_og"], 2 * t)
            sp.dma_start(g_gate[:, :, :], proj_d[ROW_GR:ROW_GR + GLA_KT, :, tile_cols(t)]
                         .rearrange("r p n -> p r n")).then_inc(sem["g_gate_in"], 16)

        def gla_tile_loads(sp, t, d):
            sp.dma_start(g_x[:, d, :, :], proj_d[ROW_GLA:ROW_GLA + 4 * HEADS, :, tile_cols(t)]
                         .rearrange("r p n -> p r n")).then_inc(g_in[d], 16)
            sp.dma_start(g_la[:, d, :], loga_d[t, :, :]).then_inc(g_in[d], 16)

        def gla_first_loads(sp):
            sp.dma_start(masks[:, :], masks_in).then_inc(sem["g_tab_in"], 16)
            sp.dma_start(e_t[:, 0, :], interval_in).then_inc(sem["g_tab_in"], 16)
            for t in range(2):
                gla_tile_loads(sp, t, t)
            gla_gates(sp, 0)

        def gla_sp(sp):
            def body(k, t, grp, d, early):
                sp.wait_ge(sem["g_o"], 2 * k + 2)
                gla_tile_loads(sp, k + 2, d)
                gla_gates(sp, k + 1)
            repeat(sp, 2, NT - 2, body, unroll=2)
            gla_gates(sp, NT - 1)

        def load_exp_ln(act):
            act.add_instruction(mybir.InstLoadActFuncSet(name=nc.get_next_instruction_name(), engine=act.engine,
                                                         act_func_set_id=ACT_SET_EXP_LN))

        def gla_act(act):
            load_exp_ln(act)
            act.wait_ge(sem["g_tab_in"], 32)
            nc.scalar.activation(interval[:, :], e_t[:, 0, :], ACT.Copy).then_inc(sem["g_tab"], 1)
            act.wait_ge(sem["g_tab"], 1)

            def log_a_hi(t, grp, d):
                act.wait_ge(g_in[d], 32 * grp + 32)
                if not (isinstance(t, int) and t < 2):
                    act.wait_ge(sem["g_E"], 4 * t - 4)
                nc.scalar.activation(la_hi[:, d, :], g_la[:, d, :], ACT.Copy).then_inc(sem["g_la_hi"], 1)

            def gated_hi(t):
                for i in range(2):
                    act.wait_ge(sem["g_og"], 2 * t + i + 1)
                    act.wait_ge(sem["g_tab"], 1)
                    nc.scalar.activation(act_k[:, 4 * i:4 * i + 4, tile_cols(t)],
                                         g_ogb[:, i * HALF:(i + 1) * HALF].rearrange("p (q n) -> p q n", q=4),
                                         ACT.Copy).then_inc(sem["g_hi"], 1)

            def keys(t):
                act.wait_ge(sem["g_kT"], t + 1)
                if not (isinstance(t, int) and t < 1):
                    act.wait_ge(sem["g_u"], 2 * t)
                nc.scalar.activation(g_kdt[:, :], psum[:, kt_bank, :], ACT.Copy,
                                     scale=GLA_DK ** -0.5).then_inc(sem["g_kd"], 1)

            def rstd(t, i):
                act.wait_ge(sem["g_mv"], 4 * t + 2 * i + 2)
                nc.scalar.activation(g_rsb[:, 0, 2 * i:2 * i + 2], g_mvb[:, 2 * i:2 * i + 2, 1],
                                     ACT.Ln, bias=eps_col[:, 0:1]).then_inc(sem["g_lnv"], 1)
                act.wait_ge(sem["g_lnv"], 2 * t + i + 1)
                nc.scalar.activation(g_rsb[:, 1, 2 * i:2 * i + 2], g_rsb[:, 0, 2 * i:2 * i + 2],
                                     ACT.Exp, scale=-0.5).then_inc(sem["g_rstd"], 1)

            def body(k, t, grp, d, early, last=False):
                first = early and d == 0

                def decay(h):
                    e = 4 * t + h
                    act.wait_ge(sem["g_E"], e + 1)
                    if not (first and h < 2):
                        act.wait_ge(sem["g_dec"], e - 1)
                        act.wait_ge(sem["g_kend"], e - 1)
                    nc.scalar.activation(e_t[:, h % 2, :], bank[:, 0:E_BLOCKS * P], ACT.Exp
                                         ).then_inc(sem["g_exp"], 1)

                if not first:
                    keys(t - 1)
                decay(0)
                if not first:
                    rstd(t - 1, 0)
                decay(1)
                if not first:
                    rstd(t - 1, 1)
                decay(2)
                for i in range(2):
                    act.wait_ge(sem["g_vT"], 2 * t + i + 1)
                    if not first:
                        act.wait_ge(sem["g_u"], 2 * t)
                    nc.scalar.activation(g_vt[:, i * HALF:(i + 1) * HALF], psum[:, vt_bank[i], :],
                                         ACT.Copy).then_inc(sem["g_v"], 1)
                decay(3)
                if not last:
                    log_a_hi(t + 1, grp + d, 1 - d)
                if not first:
                    gated_hi(t - 1)
            log_a_hi(0, 0, 0)
            begin_phase(act, 2)
            over_gla_tiles(act, body)
            keys(NT - 1)
            rstd(NT - 1, 0)
            rstd(NT - 1, 1)
            gated_hi(NT - 1)

        def gla_pool(pool):
            def gated_lo(t):
                pool.wait_ge(sem["g_hi"], 2 * t + 2)
                pool.wait_ge(sem["g_tab"], 1)
                nc.gpsimd.tensor_tensor(act_lo_k[:, :, tile_cols(t)],
                                        g_ogb[:, :].rearrange("p (q n) -> p q n", q=KT),
                                        act_k[:, :, tile_cols(t)].bitcast(F32),
                                        ALU.subtract).then_inc(sem["g_lo"], 1)

            def body(k, t, grp, d, early, last=False):
                first = early and d == 0
                for h in range(HEADS):
                    e = 4 * t + h
                    b = h % 2
                    pool.wait_ge(sem["g_exp"], e + 1)
                    if not (first and h < 2):
                        pool.wait_ge(sem["g_S"], e - 1)
                    key = g_x[:, d, 4 * h + 1, :]
                    levels = e_t[:, b, P:(NL + 1) * P].rearrange("p (l n) -> p l n", l=NL)
                    nc.gpsimd.tensor_tensor(k_lev[:, b, :, :], levels,
                                            key.unsqueeze(1).to_broadcast((P, NL, P)),
                                            ALU.mult).then_inc(sem["g_klev"], 1)
                    if not first:
                        pool.wait_ge(sem["g_kT"], t)
                    nc.gpsimd.tensor_tensor(k_end[:, h, :], e_t[:, b, 0:P], key, ALU.mult
                                            ).then_inc(sem["g_kend"], 1)
                if not first:
                    gated_lo(t - 1)
            over_gla_tiles(pool, body)
            gated_lo(NT - 1)

        def gla_dve(dve):
            nc.vector.memset(g_st[:, :, :], 0.0).then_inc(sem["state_zero"], 1)
            dve.wait_ge(sem["g_tab_in"], 32)

            def log_a_lo(t, d):
                dve.wait_ge(sem["g_la_hi"], t + 1)
                nc.vector.tensor_tensor(la_lo[:, d, :], g_la[:, d, :], la_hi[:, d, :].bitcast(F32),
                                        ALU.subtract).then_inc(sem["g_la_lo"], 1)

            def gate(t):
                dve.wait_ge(sem["g_gate_in"], 16 * t + 16)
                if not (isinstance(t, int) and t < 1):
                    dve.wait_ge(sem["g_lo"], t)
                for i in range(2):
                    dve.wait_ge(sem["g_onT"], 2 * t + i + 1)
                    nc.vector.tensor_tensor(g_ogb[:, i * HALF:(i + 1) * HALF], psum[:, gate_bank[i], :],
                                            g_gate[:, 4 * i:4 * i + 4, :].rearrange("p q n -> p (q n)"),
                                            ALU.mult).then_inc(sem["g_og"], 1)

            def normed(t, i):
                dve.wait_ge(sem["g_o"], 2 * t + i + 1)
                for h in (2 * i, 2 * i + 1):
                    both = nc.vector.bn_stats(g_bst[:, h, 0:6], psum[:, o_bank[i], head_cols(h)])
                both.then_inc(sem["g_bn"], 1)
                dve.wait_ge(sem["g_tab_in"], 32)
                dve.wait_ge(sem["g_bn"], 2 * t + i + 1)
                for h in (2 * i, 2 * i + 1):
                    nc.vector.bn_aggr(g_mvb[:, h, :], g_bst[:, h, 0:6]).then_inc(sem["g_mv"], 1)
                dve.wait_ge(sem["g_mv"], 4 * t + 2 * i + 2)
                dve.wait_ge(sem["g_rstd"], 2 * t + i + 1)
                if not (isinstance(t, int) and t < 1):
                    dve.wait_ge(sem["g_onT"], 2 * t)
                for h in (2 * i, 2 * i + 1):
                    nc.vector.tensor_scalar(g_onb[:, h * GLA_DV:(h + 1) * GLA_DV],
                                            psum[:, o_bank[i], head_cols(h)],
                                            g_mvb[:, h, 0:1], g_rsb[:, 1, h:h + 1],
                                            ALU.subtract, ALU.mult).then_inc(sem["g_on"], 1)

            def states(t, d, i):
                dve.wait_ge(sem["g_dec"], 4 * t + 4)
                dve.wait_ge(sem["g_u"], 2 * t + i + 1)
                for h in (2 * i, 2 * i + 1):
                    nc.vector.scalar_tensor_tensor(g_st[:, h, :], g_st[:, h, :], g_deccol[:, d, h:h + 1],
                                                   psum[:, u_bank, head_cols(h)],
                                                   ALU.mult, ALU.add).then_inc(sem["g_state"], 1)

            def body(k, t, grp, d, early, last=False):
                first = early and d == 0

                def queries(h):
                    e, b = 4 * t + h, h % 2
                    dve.wait_ge(sem["g_exp"], e + 1)
                    if not (first and h < 2):
                        dve.wait_ge(sem["g_S"], e - 1)
                    q = g_x[:, d, 4 * h, :]
                    levels = e_t[:, b, P:(NL + 1) * P].rearrange("p (l n) -> p l n", l=NL)
                    nc.vector.tensor_tensor(q_lev[:, b, :, :], levels,
                                            q.unsqueeze(1).to_broadcast((P, NL, P)),
                                            ALU.mult).then_inc(sem["g_qlev"], 1)
                    if not early:
                        dve.wait_ge(sem["g_o"], 2 * t - 2)
                    nc.vector.tensor_tensor(q_g[:, d, h, :], e_t[:, b, (NL + 1) * P:], q, ALU.mult
                                            ).then_inc(sem["g_qG"], 1)
                    nc.vector.tensor_copy(g_deccol[:, d, h:h + 1], e_t[:, b, E_BLOCKS * P - 1:]
                                          ).then_inc(sem["g_dec"], 1)

                def scores(h):
                    e = 4 * t + h
                    dve.wait_ge(sem["g_S"], e + 1)
                    if not (first and h == 0):
                        dve.wait_ge(sem["g_P"], e)
                    nc.vector.tensor_tensor(s_masked[:, :], bank[:, 3 * HALF:5 * HALF], masks[:, :],
                                            ALU.mult).then_inc(sem["g_mask"], 1)
                    dve.wait_ge(sem["g_mask"], e + 1)
                    if not first:
                        dve.wait_ge(sem["g_o"], 2 * t - 1 + h // 2)
                    nc.vector.tensor_reduce(p_t[:, h, :],
                                            s_masked[:, :].rearrange("p (l n) -> p n l", n=P),
                                            AX.X, ALU.add).then_inc(sem["g_P"], 1)

                queries(0)
                if not first:
                    normed(t - 1, 0)
                queries(1)
                if not first:
                    states(t - 1, 1 - d, 0)
                scores(0)
                if not first:
                    normed(t - 1, 1)
                queries(2)
                if not first:
                    states(t - 1, 1 - d, 1)
                scores(1)
                queries(3)
                scores(2)
                if not first:
                    gate(t - 1)
                if not last:
                    log_a_lo(t + 1, 1 - d)
                scores(3)
            log_a_lo(0, 0)
            begin_phase(dve, 2)
            dve.wait_ge(sem["state_zero"], 1)
            over_gla_tiles(dve, body)
            d = (NT - 1) % 2
            for i in range(2):
                normed(NT - 1, i)
                states(NT - 1, d, i)
            gate(NT - 1)

        def gla_pe(pe):
            pe.wait_ge(sem["g_tab"], 1)
            pe.wait_ge(sem["state_zero"], 1)
            pe.wait_ge(sem["proj_evac"], N_PROJ)

            def out_transposes(t):
                for i in range(2):
                    if i == 0:
                        pe.wait_ge(sem["g_on"], 4 * t + 4)
                    elif isinstance(t, int) and t == NT - 1:
                        pe.wait_ge(sem["g_state"], 4 * t + 4)
                    else:
                        pe.wait_ge(sem["g_v"], 2 * t + 4)
                    for q in range(4):
                        last = nc.tensor.transpose(psum[:, gate_bank[i], q * P:(q + 1) * P],
                                                   g_onb[:, (4 * i + q) * P:(4 * i + q + 1) * P], ident[:, :])
                    last.then_inc(sem["g_onT"], 1)

            def key_transposes(t):
                pe.wait_ge(sem["g_kend"], 4 * t + 4)
                pe.wait_ge(sem["g_v"], 2 * t + 2)
                for h in range(HEADS):
                    last = nc.tensor.transpose(psum[:, kt_bank, h * P:(h + 1) * P], k_end[:, h, :], ident[:, :])
                last.then_inc(sem["g_kT"], 1)

            def outputs(t, d, i):
                start = isinstance(t, int) and t < 1
                pe.wait_ge(sem["g_kd"], t + 1)
                pe.wait_ge(sem["g_P"], 4 * t + 2 * i + 2)
                pe.wait_ge(sem["g_qG"], 4 * t + 2 * i + 2)
                if not start:
                    pe.wait_ge(sem["g_state"], 4 * t - 2 + 2 * i)
                    if i == 1:
                        pe.wait_ge(sem["g_og"], 2 * t)
                for h in (2 * i, 2 * i + 1):
                    o = psum[:, o_bank[i], head_cols(h)]
                    nc.tensor.matmul(o, p_t[:, h, :], g_vt[:, h * GLA_DV:(h + 1) * GLA_DV],
                                     start=True, stop=False)
                    last = nc.tensor.matmul(o, q_g[:, d, h, :], g_st[:, h, :], start=False, stop=True)
                last.then_inc(sem["g_o"], 1)

            def state_inputs(t, i):
                if i == 1:
                    pe.wait_ge(sem["g_state"], 4 * t + 2)
                elif not (isinstance(t, int) and t < 1):
                    pe.wait_ge(sem["g_og"], 2 * t)
                for h in (2 * i, 2 * i + 1):
                    last = nc.tensor.matmul(psum[:, u_bank, head_cols(h)], g_kdt[:, h * P:(h + 1) * P],
                                            g_vt[:, h * GLA_DV:(h + 1) * GLA_DV], start=True, stop=True)
                last.then_inc(sem["g_u"], 1)

            def body(k, t, grp, d, early, last=False):
                first = early and d == 0

                def decay(h):
                    e = 4 * t + h
                    pe.wait_ge(sem["g_la_lo"], t + 1)
                    if not (first and h == 0):
                        pe.wait_ge(sem["g_exp"], e)
                    for c0 in range(0, E_BLOCKS * P, HALF):
                        c1 = min(c0 + HALF, E_BLOCKS * P)
                        nc.tensor.matmul(bank[:, c0:c1], la_hi[:, d, h * P:(h + 1) * P], interval[:, c0:c1],
                                         start=True, stop=False)
                        done = nc.tensor.matmul(bank[:, c0:c1], la_lo[:, d, h * P:(h + 1) * P],
                                                interval[:, c0:c1], start=False, stop=True)
                    done.then_inc(sem["g_E"], 1)

                def scores(h):
                    e, b = 4 * t + h, h % 2
                    pe.wait_ge(sem["g_klev"], e + 1)
                    pe.wait_ge(sem["g_qlev"], e + 1)
                    if not (first and h == 0):
                        pe.wait_ge(sem["g_mask"], e)
                    for l in range(NL + 1):
                        o = bank[:, 3 * HALF + l * P:3 * HALF + (l + 1) * P]
                        key = k_lev[:, b, l, :] if l < NL else g_x[:, d, 4 * h + 1, :]
                        query = q_lev[:, b, l, :] if l < NL else g_x[:, d, 4 * h, :]
                        done = nc.tensor.matmul(o, key, query, start=True, stop=True)
                    done.then_inc(sem["g_S"], 1)

                if not first:
                    key_transposes(t - 1)
                decay(0)
                if not first:
                    outputs(t - 1, 1 - d, 0)
                decay(1)
                if not first:
                    state_inputs(t - 1, 0)
                scores(0)
                if not first:
                    outputs(t - 1, 1 - d, 1)
                    state_inputs(t - 1, 1)
                decay(2)
                scores(1)
                for i in range(2):
                    if not first:
                        pe.wait_ge(sem["g_on"] if i == 0 else sem["g_state"], 4 * t - 2 if i == 0 else 4 * t)
                    for q in range(4):
                        row = 4 * (2 * i + q // 2) + 2 + q % 2
                        done = nc.tensor.transpose(psum[:, vt_bank[i], q * P:(q + 1) * P],
                                                   g_x[:, d, row, :], ident[:, :])
                    done.then_inc(sem["g_vT"], 1)
                decay(3)
                scores(2)
                if not first:
                    out_transposes(t - 1)
                scores(3)
            over_gla_tiles(pe, body)
            key_transposes(NT - 1)
            for i in range(2):
                outputs(NT - 1, (NT - 1) % 2, i)
                state_inputs(NT - 1, i)
            out_transposes(NT - 1)
            pe.wait_ge(sem["g_lo"], NT)

        def ygla_sp(sp):
            begin_phase(sp, 3)

            def body(k, n, grp, j, early):
                slot = (j - SL_YGLA) % RING
                if isinstance(k, int) and k == 2:
                    ret_first_loads(sp)
                if not early:
                    sp.wait_ge(sem["y_evac"], k - RING + 1)
                sp.dma_start(y_in[:, slot, :], proj_d[k + ROW_AG, :, :]).then_inc(y_ins[slot], 16)
                if not (isinstance(k, int) and k == 0):
                    out_store(k - 1, (slot - 1) % RING)
                stream_step(sp, n, j)

            def out_store(k, slot):
                sp.wait_ge(sem["y_evac"], k + 1)
                sp.dma_start(gla_d[k, :, :], y_out[:, slot, :]).then_inc(y_st[slot], 16)
            repeat(sp, SL_YGLA, KT, body)
            out_store(KT - 1, (KT - 1) % RING)
            for j in range(RING):
                sp.wait_ge(y_st[j], 16 * KT // RING)

        def ygla_dve(dve):
            begin_phase(dve, 3)
            nc.vector.memset(r_st[:, :, :, :].rearrange("p h a n -> p (h a n)"), 0.0
                             ).then_inc(sem["state_zero"], 1)

            def body(k, c, grp, slot, early):
                dve.wait_ge(sem["mm_half"], 2 * k + 2 * SL_YGLA + 2)
                dve.wait_ge(y_ins[slot], 16 * grp + 16)
                if not early:
                    dve.wait_ge(y_st[slot], 16 * grp)
                nc.vector.tensor_tensor(y_out[:, slot, :], pair_view(slot), y_in[:, slot, :], ALU.mult
                                        ).then_inc(sem["y_evac"], 1)
            repeat(dve, 0, KT, body)

        def ygla_pe(pe):
            def body(k, n, grp, j, early):
                if not early:
                    pe.wait_ge(sem["y_evac"], k - RING + 1)
                slab_product(pe, n, j, (j - SL_YGLA) % RING)
            repeat(pe, SL_YGLA, KT, body)

        y_count = [KT, 2 * KT]
        RS = 4 * HEADS

        def ret_step_loads(sp, e, t, h, wait):
            cols = tile_cols(t)
            if wait:
                sp.wait_ge(sem["r_o"], e - 3)
            sp.dma_start(r_x[:, h, 0:8, :], proj_d[ROW_RET + 8 * h:ROW_RET + 8 * h + 8, :, cols]
                         .rearrange("r p n -> p r n")).then_inc(r_in[h], 16)
            if wait:
                sp.wait_ge(sem["r_og"], e - 3)
            sp.dma_start(r_x[:, h, 8:12, :], proj_d[ROW_RG + 4 * h:ROW_RG + 4 * h + 4, :, cols]
                         .rearrange("r p n -> p r n")).then_inc(r_gate_in[h], 16)

        def ret_first_loads(sp):
            sp.dma_start(ret_dec[:, :, :].rearrange("p h n -> p (h n)"), ret_dec_in).then_inc(sem["r_tab_in"], 16)
            sp.dma_start(ret_q[:, :, :].rearrange("p h n -> p (h n)"), ret_q_in).then_inc(sem["r_tab_in"], 16)
            sp.dma_start(ret_k[:, :], ret_k_in).then_inc(sem["r_tab_in"], 16)
            sp.dma_start(cossin[:, :, :], rope_d.rearrange("a p n -> p a n")).then_inc(sem["r_tab_in"], 16)
            for h in range(HEADS):
                ret_step_loads(sp, h, 0, h, False)

        def ret_sp(sp, hf):
            repeat(sp, hf * RS + HEADS, RS - HEADS,
                   lambda k, e, t, h, early: ret_step_loads(sp, e, t, h, True))

        def tile_before(k, t, h, back):
            return (k - back) // HEADS if isinstance(k, int) else t if h >= back else t - 1

        def ret_pool(pool, hf):
            begin_phase(pool, 4 + 2 * hf)
            if hf == 0:
                pool.wait_ge(sem["r_tab_in"], 64)

            def split_lo(e, g, h):
                b = h % 2
                pool.wait_ge(sem["r_hi"], e + 1)
                pool.wait_ge(sem["r_tab_in"], 64)
                dst = act_lo_r[:, 4 * h:4 * h + 4, tile_cols(g)]
                nc.gpsimd.tensor_tensor(dst, r_ogb[:, b, :].rearrange("p (q n) -> p q n", q=4),
                                        act_r[:, 4 * h:4 * h + 4, tile_cols(g)].bitcast(F32),
                                        ALU.subtract).then_inc(sem["r_lo"], 1)

            def body(k, e, t, h, early):
                b = h % 2
                x4 = r_x[:, h, 0:4, :]
                pool.wait_ge(sem["r_tab_in"], 64)
                pool.wait_ge(r_in[h], 16 * t + 16)
                cos = cossin[:, 0, tile_cols(t)].unsqueeze(1).to_broadcast((P, 4, P))
                sin = cossin[:, 1, tile_cols(t)].unsqueeze(1).to_broadcast((P, 4, P))
                nc.gpsimd.tensor_tensor(r_xcb[:, b, :, :], x4, cos, ALU.mult).then_inc(sem["r_xc"], 1)
                nc.gpsimd.tensor_tensor(r_xsb[:, b, :, :], x4, sin, ALU.mult).then_inc(sem["r_xs"], 1)
                pool.wait_ge(sem["r_xc"], e + 1)
                pool.wait_ge(sem["r_xs"], e + 1)
                if not (hf == 0 and early):
                    pool.wait_ge(sem["r_o"], e - 3)
                xc = r_xcb[:, b, :, :].rearrange("p (a c) n -> p a c n", c=2)
                xs = r_xsb[:, b, :, :].rearrange("p (a c) n -> p a c n", c=2)
                qk = r_qk[:, h, :, :].rearrange("p (a c) n -> p a c n", c=2)
                nc.gpsimd.tensor_tensor(qk[:, :, 0, :], xc[:, :, 0, :], xs[:, :, 1, :], ALU.subtract
                                        ).then_inc(sem["r_rope"], 1)
                nc.gpsimd.tensor_tensor(qk[:, :, 1, :], xs[:, :, 0, :], xc[:, :, 1, :], ALU.add
                                        ).then_inc(sem["r_rope"], 1)
                pool.wait_ge(sem["r_rope"], 2 * e + 2)
                nc.gpsimd.tensor_tensor(r_qdb[:, h, :, :], r_qk[:, h, 0:2, :],
                                        ret_q[:, h, :].unsqueeze(1).to_broadcast((P, 2, P)),
                                        ALU.mult).then_inc(sem["r_qd"], 1)
                if not (early and h < 3):
                    split_lo(e - 3, tile_before(k, t, h, 3) - (0 if isinstance(k, int) else 4 * hf), (h - 3) % 4)
            repeat(pool, hf * RS, RS, body)
            for k in (RS - 3, RS - 2, RS - 1):
                split_lo(hf * RS + k, k // 4, k % 4)

        def ret_act(act, hf):
            load_exp_ln(act)
            begin_phase(act, 4 + 2 * hf)

            def rstd(e, b):
                act.wait_ge(sem["r_mv"], e + 1)
                nc.scalar.activation(r_rsb[:, b, 0:1], r_mvb[:, b, 1:2], ACT.Ln, bias=eps_col[:, 0:1]
                                     ).then_inc(sem["r_lnv"], 1)
                act.wait_ge(sem["r_lnv"], e + 1)
                nc.scalar.activation(r_rsb[:, b, 1:2], r_rsb[:, b, 0:1], ACT.Exp, scale=-0.5
                                     ).then_inc(sem["r_rstd"], 1)

            def split_hi(e, g, h):
                act.wait_ge(sem["r_og"], e + 1)
                act.wait_ge(sem["r_tab_in"], 64)
                nc.scalar.activation(act_r[:, 4 * h:4 * h + 4, tile_cols(g)],
                                     r_ogb[:, h % 2, :].rearrange("p (q n) -> p q n", q=4), ACT.Copy
                                     ).then_inc(sem["r_hi"], 1)

            def body(k, e, t, h, early):
                b = h % 2
                act.wait_ge(sem["r_vT"], e + 1)
                if not (hf == 0 and early and h < 2):
                    act.wait_ge(sem["r_u"], e - 1)
                nc.scalar.activation(r_vt[:, b, :], psum[:, 0, :], ACT.Copy).then_inc(sem["r_v"], 1)
                act.wait_ge(sem["r_kT"], e + 1)
                nc.scalar.activation(r_kdt[:, b, :], psum[:, 1, 0:RET_DK], ACT.Copy, scale=ret_k[:, h:h + 1]
                                     ).then_inc(sem["r_kd"], 1)
                if not (early and h < 2):
                    split_hi(e - 2, tile_before(k, t, h, 2) - (0 if isinstance(k, int) else 4 * hf), (h - 2) % 4)
                if not (early and h < 1):
                    rstd(e - 1, 1 - b)
            if hf == 0:
                act.wait_ge(sem["r_tab_in"], 64)
            repeat(act, hf * RS, RS, body)
            last = hf * RS + RS - 1
            split_hi(last - 1, 3, 2)
            rstd(last, 1)
            split_hi(last, 3, 3)

        def ret_dve(dve, hf):
            begin_phase(dve, 4 + 2 * hf)
            if hf == 0:
                dve.wait_ge(sem["state_zero"], 2)
                dve.wait_ge(sem["r_tab_in"], 64)

            def gate(e, t, h):
                b = h % 2
                dve.wait_ge(r_gate_in[h], 16 * t + 16)
                dve.wait_ge(sem["r_onT"], e + 1)
                if not (isinstance(e, int) and e < 2):
                    dve.wait_ge(sem["r_lo"], e - 1)
                nc.vector.tensor_tensor(r_ogb[:, b, :], psum[:, 6, :],
                                        r_x[:, h, 8:12, :].rearrange("p q n -> p (q n)"),
                                        ALU.mult).then_inc(sem["r_og"], 1)

            def outputs(e, h, no_on_wait):
                b = h % 2
                o = psum[:, 3 if b == 0 else 7, :]
                dve.wait_ge(sem["r_o"], e + 1)
                nc.vector.bn_stats(r_bst[:, b, 0:6], o).then_inc(sem["r_bn"], 1)
                dve.wait_ge(sem["r_tab_in"], 64)
                dve.wait_ge(sem["r_bn"], e + 1)
                nc.vector.bn_aggr(r_mvb[:, b, :], r_bst[:, b, 0:6]).then_inc(sem["r_mv"], 1)
                dve.wait_ge(sem["r_rstd"], e + 1)
                dve.wait_ge(sem["r_mv"], e + 1)
                if not no_on_wait:
                    dve.wait_ge(sem["r_onT"], e - 1)
                nc.vector.tensor_scalar(r_onb[:, b, :], o, r_mvb[:, b, 0:1], r_rsb[:, b, 1:2],
                                        ALU.subtract, ALU.mult).then_inc(sem["r_on"], 1)
                dve.wait_ge(sem["r_u"], e + 1)
                gamma_tile = (1.0 - 2.0 ** (-5.0 - h)) ** P
                for a in range(2):
                    nc.vector.scalar_tensor_tensor(r_st[:, h, a, :], r_st[:, h, a, :], gamma_tile,
                                                   psum[:, 4 + a, :], ALU.mult, ALU.add
                                                   ).then_inc(sem["r_state"], 1)

            def body(k, e, t, h, early):
                b = h % 2
                dve.wait_ge(sem["r_S"], e + 1)
                if not (hf == 0 and early and h < 2):
                    dve.wait_ge(sem["r_o"], e - 1)
                nc.vector.tensor_tensor(r_pt[:, b, :], psum[:, 2, 0:P], ret_dec[:, h, :], ALU.mult
                                        ).then_inc(sem["r_P"], 1)
                if not (early and h < 2):
                    gate(e - 2, tile_before(k, t, h, 2) + (4 * hf if isinstance(k, int) else 0), (h - 2) % 4)
                if not (early and h < 1):
                    outputs(e - 1, (h - 1) % 4, hf == 0 and early and h - 1 < 2)
            repeat(dve, hf * RS, RS, body)
            last = hf * RS + RS - 1
            gate(last - 1, last // HEADS, 2)
            outputs(last, 3, False)
            gate(last, last // HEADS, 3)

        def ret_pe(pe, hf):
            pe.wait_ge(sem["y_evac"], y_count[hf])
            if hf == 0:
                pe.wait_ge(sem["state_zero"], 2)

            def output(e, h, first_tile):
                b = h % 2
                o = psum[:, 3 if b == 0 else 7, :]
                pe.wait_ge(sem["r_P"], e + 1)
                pe.wait_ge(sem["r_v"], e + 1)
                pe.wait_ge(sem["r_qd"], e + 1)
                if not first_tile:
                    pe.wait_ge(sem["r_state"], 2 * e - 6)
                nc.tensor.matmul(o, r_pt[:, b, :], r_vt[:, b, :], start=True, stop=False)
                for a in range(2):
                    last = nc.tensor.matmul(o, r_qdb[:, h, a, :], r_st[:, h, a, :], start=False, stop=a == 1)
                last.then_inc(sem["r_o"], 1)
                pe.wait_ge(sem["r_kd"], e + 1)
                if not (isinstance(e, int) and e < 1):
                    pe.wait_ge(sem["r_state"], 2 * e)
                for a in range(2):
                    last = nc.tensor.matmul(psum[:, 4 + a, :], r_kdt[:, b, a * P:(a + 1) * P], r_vt[:, b, :],
                                            start=True, stop=True)
                last.then_inc(sem["r_u"], 1)

            def out_transposes(e, h):
                pe.wait_ge(sem["r_on"], e + 1)
                if not (isinstance(e, int) and e < 1):
                    pe.wait_ge(sem["r_og"], e)
                for q in range(4):
                    last = nc.tensor.transpose(psum[:, 6, q * P:(q + 1) * P],
                                               r_onb[:, h % 2, q * P:(q + 1) * P], ident[:, :])
                last.then_inc(sem["r_onT"], 1)

            def body(k, e, t, h, early):
                b = h % 2
                start = hf == 0 and early and h == 0
                pe.wait_ge(r_in[h], 16 * t + 16)
                if not start:
                    pe.wait_ge(sem["r_v"], e)
                for q in range(4):
                    last = nc.tensor.transpose(psum[:, 0, q * P:(q + 1) * P], r_x[:, h, 4 + q, :], ident[:, :])
                last.then_inc(sem["r_vT"], 1)
                pe.wait_ge(sem["r_rope"], 2 * e + 2)
                if not start:
                    pe.wait_ge(sem["r_kd"], e)
                for a in range(2):
                    last = nc.tensor.transpose(psum[:, 1, a * P:(a + 1) * P], r_qk[:, h, 2 + a, :], ident[:, :])
                last.then_inc(sem["r_kT"], 1)
                if not start:
                    pe.wait_ge(sem["r_P"], e)
                for a in range(2):
                    last = nc.tensor.matmul(psum[:, 2, 0:P], r_qk[:, h, 2 + a, :], r_qk[:, h, a, :],
                                            start=a == 0, stop=a == 1)
                last.then_inc(sem["r_S"], 1)
                if not (early and h < 2):
                    out_transposes(e - 2, (h - 2) % 4)
                if not (early and h < 1):
                    output(e - 1, (h - 1) % 4, hf == 0 and early)
            repeat(pe, hf * RS, RS, body, peel=1)
            last = hf * RS + RS - 1
            out_transposes(last - 1, 2)
            output(last, 3, False)
            out_transposes(last, 3)
            pe.wait_ge(sem["r_lo"], last + 1)

        def yret_pe(pe, hf):
            groups = 2 * KT // RING
            def group(g):
                for jj in range(RING):
                    n0 = SL_YRET + hf * 2 * KT + jj
                    kh, b = jj % 2, jj // 2
                    n = g * RING + n0
                    j = n0 % RING
                    pe.wait_ge(sem["slab_ready"], n + 1)
                    if kh == 0 and not (isinstance(g, int) and g == 0):
                        pe.wait_ge(sem["y_evac"], 2 * g + (y_count[hf] + b - 1))
                    for kk in range(KT):
                        sl = slice((kh * KT + kk) * HALF, (kh * KT + kk + 1) * HALF)
                        last = product3(psum[:, b, :], w_hi[:, j, kk * P:(kk + 1) * P],
                                        w_lo[:, j, kk * P:(kk + 1) * P], act_hi[:, sl], act_lo[:, sl],
                                        kh == 0 and kk == 0, kh == 1 and kk == KT - 1)
                        if kk % 4 == 3:
                            last.then_inc(sem["mm_half"], 1)
            group(0)
            with pe.Fori(1, groups) as g:
                group(g)

        def yret_sp(sp, hf):
            begin_phase(sp, 5 + 2 * hf)
            cols = slice(hf * HALF, hf * HALF + HALF)

            def out_store(c, s, slot):
                sp.wait_ge(sem["y_evac"], s + 1)
                sp.dma_start(merged_d[c, :, cols], y_out[:, slot, 0:HALF]).then_inc(y_st[slot], 16)

            def body(c, s, grp, slot, early):
                if isinstance(c, int) and c == 2 and hf == 0:
                    for h in range(HEADS):
                        ret_step_loads(sp, RS + h, RS // HEADS, h, False)
                if isinstance(c, int) and c == 2 and hf == 1:
                    dense_first_loads(sp, 0, 0, merged_d, x, ln_post_mix)
                if not early:
                    sp.wait_ge(sem["y_evac"], s - RING + 1)
                sp.dma_start(y_in[:, slot, 0:HALF], proj_d[c + ROW_AR, :, cols]).then_inc(y_ins[slot], 16)
                sp.dma_start(y_in[:, slot, HALF:], gla_d[c, :, cols]).then_inc(y_ins[slot], 16)
                if not (isinstance(c, int) and c == 0):
                    out_store(c - 1, s - 1, (slot - 1) % RING)
                for i in range(2):
                    n = 2 * c + (SL_YRET + hf * 2 * KT + i)
                    stream_step(sp, n, (SL_YRET + 2 * slot + i) % RING)
            repeat(sp, y_count[hf], KT, body)
            out_store(KT - 1, y_count[hf] + KT - 1, RING - 1)
            for j in range(RING):
                sp.wait_ge(y_st[j], 16 * (y_count[hf] + KT) // RING)

        def yret_dve(dve, hf):
            begin_phase(dve, 5 + 2 * hf)

            def body(c, s, grp, slot, early):
                b = slot % 2
                n = 2 * c + (SL_YRET + hf * 2 * KT + 1)
                dve.wait_ge(sem["mm_half"], 2 * n + 2)
                dve.wait_ge(y_ins[slot], 32 * grp - 16 * (KT // RING) + 32)
                nc.vector.tensor_tensor(y_tmp[:, b, :], psum[:, b, :], y_in[:, slot, 0:HALF], ALU.mult
                                        ).then_inc(sem["y_mul"], 1)
                dve.wait_ge(sem["y_mul"], s - KT + 1)
                if not early:
                    dve.wait_ge(y_st[slot], 16 * grp)
                nc.vector.tensor_tensor(y_out[:, slot, 0:HALF], y_tmp[:, b, :], y_in[:, slot, HALF:], ALU.add
                                        ).then_inc(sem["y_evac"], 1)
            repeat(dve, y_count[hf], KT, body)

        def piece(sp, src, k, hf, slot):
            sp.dma_start(d_raw[:, slot, :], src[k, :, hf * HALF:hf * HALF + HALF]).then_inc(d_in[slot], 16)

        def dense_first_loads(sp, job, q0, src, res, ln):
            for k in range(RING):
                if job:
                    sp.wait_ge(sem["d_lo"], q0)
                piece(sp, src, k, 0, (q0 + k) % RING)
            sp.dma_start(d_ln[:, :], ln.to_broadcast((P, D))).then_inc(sem["d_ln_in"], 16)
            residual_rows(sp, res, 0)

        def residual_rows(sp, res, hf):
            sp.dma_start(d_x[:, :, :], res[hf * HALF:hf * HALF + HALF, :].rearrange("(t p) d -> p t d", p=P)
                         ).then_inc(sem["d_x_in"], 16)

        def dense_sp(sp, job, K, n0, q0, src, res, dst):
            loading = N_SLABS - n0 - 2 * RING

            def step(s, q, slot, hf, next_k):
                if hf == 0 or not isinstance(s, int) or s < loading:
                    stream_step(sp, s + n0, (slot + n0 - q0) % RING)
                if next_k is not None:
                    sp.wait_ge(sem["d_lo"], q + 1)
                    piece(sp, src, next_k, hf, slot)

            repeat(sp, q0, K - RING, lambda k, q, grp, slot, early: step(k, q, slot, 0, k + RING))
            for k in range(RING):
                step(K - RING + k, q0 + K - RING + k, (q0 + K + k) % RING, 1, k)
            base = q0 + K
            looped = min(K - RING, loading - K)
            repeat(sp, base, looped, lambda k, q, grp, slot, early: step(k + K, q, slot, 1, k + RING))
            for k in range(looped, K):
                step(K + k, base + k, (base + k) % RING, 1, k + RING if k + RING < K else None)
                if k == K - RING - 1:
                    store(sp, job, 0, dst)
                    residual_rows(sp, res, 1)
            if looped == K - RING:
                store(sp, job, 0, dst)
                residual_rows(sp, res, 1)
            store(sp, job, 1, dst)
            sp.wait_ge(sem["d_stored"], 16 * NT * (job + 1))

        def store(sp, job, hf, dst):
            for tok in range(4):
                t = 4 * hf + tok
                sp.wait_ge(sem["d_res"], NT * job + t + 1)
                sp.dma_start(dst[t * P:(t + 1) * P, :], d_out[:, t, :]).then_inc(sem["d_stored"], 16)

        def dense_pe(pe, job, K, n0, q0, banks_free):
            for hf in range(2):
                def body(k, q, grp, slot, early):
                    j = (slot + n0 - q0) % RING
                    pe.wait_ge(sem["slab_ready"], k + (n0 + hf * K + 1))
                    pe.wait_ge(sem["d_lo"], q + 1)
                    start = isinstance(k, int) and k == 0
                    stop = isinstance(k, int) and k == K - 1
                    for tok in range(4):
                        if start and hf:
                            pe.wait_ge(sem["d_evac"], NT * job + tok + 1)
                        elif start:
                            banks_free(pe, tok)
                        s_hi = d_hib[:, slot, tok * P:(tok + 1) * P]
                        s_lo = d_lob[:, slot, tok * P:(tok + 1) * P]
                        for cc in range(2):
                            last = product3(psum[:, 2 * tok + cc, :], s_hi, s_lo,
                                            w_hi[:, j, cc * HALF:(cc + 1) * HALF],
                                            w_lo[:, j, cc * HALF:(cc + 1) * HALF], start, stop)
                        if tok % 2:
                            last.then_inc(sem["mm_half"], 1)
                repeat(pe, q0 + hf * K, K, body)

        def over_pieces(eng, lo, count, k0, body):
            repeat(eng, lo, count, lambda k, q, grp, slot, early: body(k, k + k0, q, grp, slot, k0 == 0 and early))

        def dense_act(act, job, K, n0, q0):
            def split(k, s, q, grp, slot, start):
                act.wait_ge(d_in[slot], 16 * grp + 16)
                if not start:
                    act.wait_ge(sem["mm_half"], 2 * s + 2 * (n0 - RING) + 2)
                elif job:
                    act.wait_ge(sem["mm_half"], 2 * SL_UP)
                nc.scalar.activation(d_hib[:, slot, :], d_raw[:, slot, :], ACT.Copy
                                     ).then_inc(sem["d_hi"], 1)

            def tail(hf):
                for tok in range(4):
                    t = 4 * hf + tok
                    act.wait_ge(sem["mm_half"], 2 * (n0 + hf * K + K) - (tok < 2))
                    if job or t:
                        act.wait_ge(sem["d_sq"], NT * job + t)
                    nc.scalar.activation(d_junk[:, :], pair_view(tok), ACT.Square,
                                         accum_out=stat[:, 24 + t:25 + t]).then_inc(sem["d_sq"], 1)
                    act.wait_ge(sem["d_sq"], NT * job + t + 1)
                    nc.scalar.activation(stat[:, 32 + t:33 + t], stat[:, 24 + t:25 + t], ACT.Sqrt, scale=1.0 / D,
                                         bias=eps_col[:, 0:1]).then_inc(sem["d_std"], 1)

            over_pieces(act, q0, K + RING, 0, split)
            tail(0)
            over_pieces(act, q0 + K + RING, K - RING, K + RING, split)
            if job == 0:
                norm2_squares(act, 0)
            tail(1)
            if job == 0:
                norm_hi(act, 1, range(KT))
                norm2_squares(act, 1)
                norm_hi(act, 1, range(KT, 2 * KT))

        def dense_dve(dve, job, K, n0, q0):
            def split(k, s, q, grp, slot, start):
                dve.wait_ge(sem["d_hi"], q + 1)
                nc.vector.tensor_tensor(d_lob[:, slot, :], d_raw[:, slot, :], d_hib[:, slot, :].bitcast(F32),
                                        ALU.subtract).then_inc(sem["d_lo"], 1)

            def evacuate(hf):
                for tok in range(4):
                    dve.wait_ge(sem["d_sq"], NT * job + 4 * hf + tok + 1)
                    nc.vector.tensor_copy(d_out[:, 4 * hf + tok, :], pair_view(tok)).then_inc(sem["d_evac"], 1)

            def tail(hf):
                dve.wait_ge(sem["d_ln_in"], 16 * job + 16)
                dve.wait_ge(sem["d_x_in"], 16 * (2 * job + hf) + 16)
                for tok in range(4):
                    t = 4 * hf + tok
                    dve.wait_ge(sem["d_std"], NT * job + t + 1)
                    nc.vector.reciprocal(stat[:, 40 + t:41 + t], stat[:, 32 + t:33 + t]).then_inc(sem["d_rstd"], 1)
                    dve.wait_ge(sem["d_rstd"], NT * job + t + 1)
                    dve.wait_ge(sem["d_evac"], NT * job + t + 1)
                    nc.vector.scalar_tensor_tensor(d_out[:, t, :], d_out[:, t, :],
                                                   stat[:, 40 + t:41 + t], d_ln[:, :],
                                                   ALU.mult, ALU.mult).then_inc(sem["d_scaled"], 1)
                    dve.wait_ge(sem["d_scaled"], NT * job + t + 1)
                    nc.vector.tensor_tensor(d_out[:, t, :], d_out[:, t, :], d_x[:, tok, :], ALU.add
                                            ).then_inc(sem["d_res"], 1)

            over_pieces(dve, q0, K + RING, 0, split)
            begin_phase(dve, 8 if job == 0 else 10)
            evacuate(0)
            tail(0)
            over_pieces(dve, q0 + K + RING, K - RING, K + RING, split)
            if job == 0:
                norm2_scale(dve, 0)
            evacuate(1)
            if job == 0:
                norm_lo(dve, 1, range(KT))
            tail(1)
            if job == 0:
                norm2_scale(dve, 1)
                norm_lo(dve, 1, range(KT, 2 * KT))

        def norm2_squares(act, hf):
            for tok in range(4):
                t = 4 * hf + tok
                act.wait_ge(sem["d_res"], t + 1)
                act.wait_ge(sem["n_sq"], t) if t else None
                act.wait_ge(sem["d_sq"], 4 + 4 * hf)
                nc.scalar.activation(d_junk[:, :], d_out[:, t, :], ACT.Square,
                                     accum_out=stat[:, t:t + 1]).then_inc(sem["n_sq"], 1)
            act.wait_ge(sem["n_sq"], 4 * hf + 4)
            nc.scalar.activation(stat[:, 8 + 4 * hf:12 + 4 * hf], stat[:, 4 * hf:4 * hf + 4], ACT.Sqrt,
                                 scale=1.0 / D, bias=eps_col[:, 0:1]).then_inc(sem["rms_std"], 1)

        def norm2_scale(dve, hf):
            dve.wait_ge(sem["rms_std"], 2 + hf + 1)
            nc.vector.reciprocal(stat[:, 16 + 4 * hf:20 + 4 * hf], stat[:, 8 + 4 * hf:12 + 4 * hf]
                                 ).then_inc(sem["rms_rstd"], 1)
            dve.wait_ge(sem["rms_rstd"], 2 + hf + 1)
            if hf == 0:
                dve.wait_ge(sem["d_stored"], 16 * 4)
            else:
                dve.wait_ge(sem["d_res"], NT)
            for tok in range(4):
                t = 4 * hf + tok
                nc.vector.tensor_scalar(d_out[:, t, :] if hf == 0 else d_x[:, tok, :], d_out[:, t, :],
                                        stat[:, 16 + t:17 + t], None, ALU.mult).then_inc(sem["x_scaled"], 1)

        def norm2_transposes(pe, hf):
            for i in range(hf * KT, hf * KT + KT):
                k = i % KT
                pe.wait_ge(sem["x_scaled"], NT + 4 * hf + 4)
                if hf == 0:
                    pe.wait_ge(sem["d_evac"], 4 + i // 2 + 1)
                else:
                    pe.wait_ge(sem["act_lo_done"], 2 * KT + (KT if i < KT + 4 else i - 3))
                for q in range(4):
                    src = d_out[:, q, k * P:(k + 1) * P] if hf == 0 else d_x[:, q, k * P:(k + 1) * P]
                    last = nc.tensor.transpose(psum[:, norm_bank(1, i), q * P:(q + 1) * P], src, ident[:, :])
                last.then_inc(sem["x_transposed"], 1)

        def up_sp(sp):
            def pair(p, s, grp, slot, early):
                for i in range(2):
                    n = 2 * p + (SL_UP + i)
                    stream_step(sp, n, (SL_UP + 2 * slot + i) % RING)
                sp.wait_ge(sem["u_f"], p + 1)
                sp.dma_start(f_d[p, :, :], u_fb[:, slot, :]).then_inc(stored[slot], 16)
            begin_phase(sp, 9)
            repeat(sp, 0, FT - 1, pair)
            for j in range(RING):
                sp.wait_ge(stored[j], 16 * (N_PROJ // RING) + 16)
            dense_first_loads(sp, 1, 2 * KT, f_d, x1_d, ln_post_ffn)
            pair(FT - 1, FT - 1, (FT - 1) // RING, (FT - 1) % RING, False)
            for j in range(RING):
                sp.wait_ge(stored[j], 16 * (N_PROJ // RING) + 16 * len(range(j, FT, RING)))

        def up_act(act):
            begin_phase(act, 9)
            def pair(p, s, grp, b, early):
                for i in range(2):
                    k = 2 * p + i
                    act.wait_ge(sem["mm_half"], 2 * k + 2 * SL_UP + 2)
                    if not early:
                        act.wait_ge(sem["u_f"], p - 1)
                    act.wait_ge(sem["const_in"], 64)
                    nc.scalar.activation(u_conv[:, 2 * b + i, :], pair_view(2 * b + i), ACT.Identity,
                                         scale=col(k, 2), bias=col(k, 3)).then_inc(sem["u_lin"], 1)
                act.wait_ge(sem["u_tap0"], 2 * p + 2)
                nc.scalar.activation(u_conv[:, 2 * b + 1, :], u_conv[:, 2 * b + 1, :], ACT.Gelu_apprx_tanh
                                     ).then_inc(sem["u_gelu"], 1)
            repeat(act, 0, FT, pair, unroll=2)

        def col(k, tap):
            return conv_col[:, 4 * k + tap:4 * k + tap + 1] if isinstance(k, int) else \
                conv_col[:, bass.ds(4 * k + tap, 1)]

        def up_dve(dve):
            begin_phase(dve, 9)
            def pair(p, s, grp, slot, early):
                for i in range(2):
                    k = 2 * p + i
                    b = (2 * slot + i) % RING
                    dve.wait_ge(sem["u_lin"], k + 1)
                    dve.wait_ge(sem["const_in"], 64)
                    nc.vector.scalar_tensor_tensor(u_conv[:, b, 1:], pair_view(b)[:, 0:SEQ - 1], col(k, 1),
                                                   u_conv[:, b, 1:], ALU.mult, ALU.add
                                                   ).then_inc(sem["u_tap1"], 1)
                    dve.wait_ge(sem["u_tap1"], k + 1)
                    dve.wait_ge(sem["const_in"], 64)
                    nc.vector.scalar_tensor_tensor(u_conv[:, b, 2:], pair_view(b)[:, 0:SEQ - 2], col(k, 0),
                                                   u_conv[:, b, 2:], ALU.mult, ALU.add
                                                   ).then_inc(sem["u_tap0"], 1)
                if not early:
                    dve.wait_ge(stored[slot], 16 * (N_PROJ // RING) + 16 * grp)
                dve.wait_ge(sem["u_gelu"], p + 1)
                b = (2 * slot) % RING
                nc.vector.tensor_tensor(u_fb[:, slot, :], u_conv[:, b, :], u_conv[:, b + 1, :], ALU.mult
                                        ).then_inc(sem["u_f"], 1)
            repeat(dve, 0, FT, pair)

        def up_pe(pe):
            for k in range(RING):
                pe.wait_ge(sem["slab_ready"], SL_UP + k + 1)
                pe.wait_ge(sem["act_lo_done"], 3 * KT)
                half_product((SL_UP + k) % RING, k, 0)
            norm2_transposes(pe, 1)
            end_phase(pe, "pe")
            pe.wait_ge(sem["act_lo_done"], 4 * KT)
            for k in range(RING):
                half_product((SL_UP + k) % RING, k, 1).then_inc(sem["mm_half"], 2)

            def body(k, n, grp, j, early):
                pe.wait_ge(sem["u_tap0"], k + 1)
                slab_product(pe, n, j, (j - SL_UP) % RING)
            repeat(pe, SL_UP + RING, 2 * FT - RING, body)

        block = ctx.enter_context(nc.Block())
        MIX = dict(job=0, K=KT, n0=SL_MIX, q0=0)
        DOWN = dict(job=1, K=FT, n0=SL_DOWN, q0=2 * KT)

        def mix_banks_free(pe, tok):
            if tok == 0:
                pe.wait_ge(sem["y_evac"], 3 * KT)

        def down_banks_free(pe, tok):
            pe.wait_ge(sem["u_tap0"], 2 * FT - RING + tok + 1)

        @block.sync
        def _(sp):
            sp.dma_start(ident[:, :], ident_in).then_inc(sem["const_in"], 16)
            sp.dma_start(ln_col[:, :, :], ln_cols_in).then_inc(sem["const_in"], 16)
            sp.dma_start(conv_col[:, :], conv_in).then_inc(sem["const_in"], 16)
            sp.dma_start(eps_col[:, :], eps_in).then_inc(sem["const_in"], 16)
            norm_sp(sp)
            stream_prologue(sp)
            sp.sem_inc(sem["sp_phases"], 1)
            begin_phase(sp, 1)
            for phase in (proj_sp, gla_sp, ygla_sp, lambda e: ret_sp(e, 0), lambda e: yret_sp(e, 0),
                          lambda e: ret_sp(e, 1), lambda e: yret_sp(e, 1),
                          lambda e: dense_sp(e, **MIX, src=merged_d, res=x, dst=x1_d), up_sp,
                          lambda e: dense_sp(e, **DOWN, src=f_d, res=x1_d, dst=out)):
                phase(sp)
                sp.sem_inc(sem["sp_phases"], 1)

        @block.tensor
        def _(pe):
            pe.wait_ge(sem["const_in"], 64)
            for phase in (norm_pe, proj_pe, gla_pe, ygla_pe, lambda e: ret_pe(e, 0), lambda e: yret_pe(e, 0),
                          lambda e: ret_pe(e, 1), lambda e: yret_pe(e, 1)):
                phase(pe)
                end_phase(pe, "pe")
            dense_pe(pe, **MIX, banks_free=mix_banks_free)
            norm2_transposes(pe, 0)
            up_pe(pe)
            end_phase(pe, "pe")
            dense_pe(pe, **DOWN, banks_free=down_banks_free)

        @block.scalar
        def _(act):
            for phase in (norm_act, lambda e: (begin_phase(e, 1), proj_act(e)), gla_act, lambda e: None,
                          lambda e: ret_act(e, 0), lambda e: None, lambda e: ret_act(e, 1), lambda e: None,
                          lambda e: dense_act(e, **MIX), up_act, lambda e: dense_act(e, **DOWN)):
                phase(act)
                end_phase(act, "act")

        @block.vector
        def _(dve):
            dve.wait_ge(sem["const_in"], 64)
            for phase in (norm_dve, lambda e: (begin_phase(e, 1), proj_dve(e)), gla_dve, ygla_dve,
                          lambda e: ret_dve(e, 0), lambda e: yret_dve(e, 0), lambda e: ret_dve(e, 1),
                          lambda e: yret_dve(e, 1), lambda e: dense_dve(e, **MIX), up_dve,
                          lambda e: dense_dve(e, **DOWN)):
                phase(dve)
                end_phase(dve, "dve")

        @block.gpsimd
        def _(pool):
            nc.gpsimd.memset(zero_col[:, :], 0.0).then_inc(sem["zero_set"], 1)
            pool.wait_ge(sem["zero_set"], 1)
            split_slabs(pool, 0, SL_YGLA + RING)
            begin_phase(pool, 2)
            gla_pool(pool)
            split_slabs(pool, SL_YGLA + RING, SL_YRET + RING)
            ret_pool(pool, 0)
            split_slabs(pool, SL_YRET + RING, SL_YRET + 2 * KT + RING)
            ret_pool(pool, 1)
            split_slabs(pool, SL_YRET + 2 * KT + RING, N_SLABS)


def kernel(**inputs):
    import numpy as _np
    import concourse.bacc as _bacc
    from concourse import mybir as _mybir
    from concourse.bass_utils import run_bass_kernel_spmd as _run

    a = {k: _np.asarray(v) for k, v in inputs.items()}

    def slabs(w, cols=None):
        cols = range(0, w.shape[1], P) if cols is None else cols
        return [w[:, c:c + P].reshape(KT, P, P).transpose(1, 0, 2).reshape(P, D) for c in cols]

    w_in, w_up, w_down = a["w_in"][0], a["w_ffn_up"][0], a["w_ffn_down"][0]
    w_ret, w_mix = a["w_ret_out"][0], a["w_mix_out"][0]
    lr = _np.zeros((D, P), _np.float32)
    lr[:, :GLA_RANK] = w_in[:, O_LR:O_LR + GLA_RANK]
    ret = [s for c in range(KT) for kh in range(2)
           for s in slabs(w_ret[kh * D:(kh + 1) * D], [c * P])]
    rows = lambda w: [w[k * P:(k + 1) * P] for k in range(w.shape[0] // P)]
    stream = (slabs(lr) + slabs(w_in, projection_columns()) + slabs(a["w_gla_out"][0]) + ret + ret
              + rows(w_mix) + rows(w_mix)
              + slabs(w_up, [v for p in range(FT) for v in (p * P, D_FF + p * P)])
              + rows(w_down) + rows(w_down))
    w_stream = _np.stack(stream)
    assert w_stream.shape[0] == N_SLABS
    pair_cols = [v for p in range(FT) for v in (p * P, D_FF + p * P)]
    taps = _np.concatenate([a["conv_w"][0], a["conv_b"]], 0)
    conv = _np.stack([taps[:, c:c + P] for c in pair_cols]).transpose(2, 0, 1).reshape(P, -1)
    ln_cols = _np.stack([a["ln_pre_mix"][0].reshape(KT, P).T, a["ln_pre_ffn"][0].reshape(KT, P).T], 1)
    ret_dec, ret_q, ret_k = retention_tables()
    inv_freq = (10000.0 ** (-_np.arange(0, RET_DK, 2) / RET_DK)).astype(_np.float32).reshape(P, 1)
    feeds = {
        "x": a["x"][0], "positions": a["positions"], "w_stream": w_stream, "w_dec": a["w_gla_decay"][0],
        "b_dec": a["b_gla_decay"], "ln_post_mix": a["ln_post_mix"], "ln_post_ffn": a["ln_post_ffn"],
        "ln_cols_in": ln_cols, "conv_in": conv, "ident_in": _np.eye(P, dtype=_np.float32),
        "interval_in": interval_table(), "masks_in": level_masks(), "ret_dec_in": ret_dec,
        "ret_q_in": ret_q, "ret_k_in": ret_k, "inv_freq_in": inv_freq,
        "eps_in": _np.full((P, 1), EPS, _np.float32),
    }
    nc = _bacc.Bacc("TRN2", target_bir_lowering=False, num_devices=1)
    arrays, args = {}, {}
    for name, v in feeds.items():
        v = _np.ascontiguousarray(v)
        arrays[f"in_{name}"] = v
        args[name] = nc.dram_tensor(f"in_{name}", v.shape, _mybir.dt.from_np(v.dtype), kind="ExternalInput").ap()
    out = nc.dram_tensor("out_0", (SEQ, D), F32, kind="ExternalOutput").ap()
    build(nc, out=out, **args)
    r = _run(nc, [arrays], core_ids=[0])
    return _np.asarray(r.results[0]["out_0"]).reshape(a["x"].shape)
```

```python
import math
from contextlib import ExitStack

import numpy as np

import concourse.bass as bass
from concourse import mybir

F32 = mybir.dt.float32
F32R = mybir.dt.float32r
I32 = mybir.dt.int32
ALU = mybir.AluOpType
ACT = mybir.ActivationFunctionType
AX = mybir.AxisListType

ACT_SET_EXP_LN = 6

P = 128
D = 1024
SEQ = 1024
KT = D // P
NT = SEQ // P
HALF = 512
CHUNK = 64
EPS = 1e-6
HEADS = 4
GLA_DK, GLA_DV, GLA_RANK, GLA_TAU = D // 8, D // 4, 16, 16.0
RET_DK, RET_DV = D // 4, D // 2
D_FF = 2816
FT = D_FF // P
GLA_QK, GLA_V, RET_QK, RET_V = HEADS * GLA_DK, HEADS * GLA_DV, HEADS * RET_DK, HEADS * RET_DV
GLA_KT, RET_KT = GLA_V // P, RET_V // P

_SPLITS = (GLA_QK, GLA_QK, GLA_V, GLA_V, GLA_RANK, RET_QK, RET_QK, RET_V, RET_V, D, D)
_OFF = [0]
for _s in _SPLITS:
    _OFF.append(_OFF[-1] + _s)
O_GQ, O_GK, O_GV, O_GR, O_LR, O_RQ, O_RK, O_RV, O_RG, O_AG, O_AR = _OFF[:11]


def projection_columns():
    cols = []
    for h in range(HEADS):
        cols += [O_GQ + h * P, O_GK + h * P]
    for h in range(HEADS):
        cols += [O_RQ + h * 2 * P, O_RQ + h * 2 * P + P, O_RK + h * 2 * P, O_RK + h * 2 * P + P]
    cols += [O_GR + j * P for j in range(GLA_KT)]
    cols += [O_RG + j * P for j in range(RET_KT)]
    cols += [O_AG + j * P for j in range(KT)]
    cols += [O_AR + j * P for j in range(KT)]
    return cols


def value_columns():
    return [O_GV + c for c in range(0, GLA_V, HALF)] + [O_RV + c for c in range(0, RET_V, HALF)]


N_ROWS = len(projection_columns())
N_VGROUPS = len(value_columns())
GV_GROUPS = GLA_V // HALF
ROW_GLA, ROW_RET = 0, 2 * HEADS
ROW_GR = ROW_RET + 4 * HEADS
ROW_RG = ROW_GR + GLA_KT
ROW_AG = ROW_RG + RET_KT
ROW_AR = ROW_AG + KT
SL_VAL = 0
SL_LR = SL_VAL + 4 * N_VGROUPS
SL_PROJ = SL_LR + 1
SL_YGLA = SL_PROJ + N_ROWS
SL_YRET = SL_YGLA + KT
SL_MIX = SL_YRET + 2 * 2 * KT
SL_UP = SL_MIX + 2 * KT
SL_DOWN = SL_UP + 2 * FT
N_SLABS = SL_DOWN + 2 * FT
RING = 4
STAGE_OFFSET = 6080
PROJ_STORES = N_VGROUPS + N_ROWS // RING

LEVELS = [128 >> i for i in range(7)]
NL = len(LEVELS)
E_BLOCKS = NL + 2


def interval_table():
    m, n = np.meshgrid(np.arange(P), np.arange(P), indexing="ij")
    t = np.zeros((P, E_BLOCKS, P), np.float32)
    t[:, 0] = m > n
    for i, b in enumerate(LEVELS):
        mid = (n // b) * b + b // 2
        t[:, 1 + i] = np.where(n >= mid, (m >= mid) & (m <= n), (m > n) & (m < mid))
    t[:, NL + 1] = m <= n
    return (t / GLA_TAU).astype(np.float32).reshape(P, E_BLOCKS * P)


def level_masks():
    m, n = np.meshgrid(np.arange(P), np.arange(P), indexing="ij")
    t = np.zeros((P, NL + 1, P), np.float32)
    for i, b in enumerate(LEVELS):
        same = (m // b) == (n // b)
        mid = (n // b) * b + b // 2
        t[:, i] = same & ((m >= mid) != (n >= mid)) & (m // CHUNK <= n // CHUNK)
    t[:, NL] = m == n
    return (t * GLA_DK ** -0.5).astype(np.float32).reshape(P, (NL + 1) * P)


def retention_tables():
    g = 1.0 - 2.0 ** (-5.0 - np.arange(HEADS))
    m, n = np.meshgrid(np.arange(P), np.arange(P), indexing="ij")
    scale = RET_DK ** -0.5
    dec = np.stack([g[h] ** np.abs(n - m) * (m // CHUNK <= n // CHUNK) * scale for h in range(HEADS)], 1)
    qd = np.stack([g[h] ** (n + 1.0) for h in range(HEADS)], 1)
    kd = np.stack([g[h] ** (P - 1.0 - np.arange(P)) * scale for h in range(HEADS)], 1)
    return (dec.reshape(P, -1).astype(np.float32), qd.reshape(P, -1).astype(np.float32),
            kd.astype(np.float32))


def two_pi_parts(bits=7, count=7):
    parts, rest = [], 2.0 * math.pi
    for _ in range(count):
        e = math.floor(math.log2(rest)) - (bits - 1)
        part = math.floor(rest / 2.0 ** e) * 2.0 ** e
        parts.append(part)
        rest -= part
    return parts


SEMS = """
const_in x_in0 x_in1 x_in2 x_in3 sq_done rms_std rms_rstd x_scaled x_transposed
act_hi_done act_lo_done raw_in0 raw_in1 raw_in2 raw_in3 hi_split slab_ready mm_half
lr_in lr_out lr_ones z_out z_copied z_abs z_exp z_ln log_a loga_stored
pos_in pos_f turns0 turns1 angle angle_red sin_half cos_sq rope_done rope_stored
proj_evac val_half val_evac st0 st1 st2 st3
g_in0 g_in1 g_gate_in g_tab_in g_tab g_la_hi g_la_lo g_E g_exp g_qG g_dec g_klev g_kend
g_S g_mask g_P g_kT g_kd g_o g_u g_state g_bn g_mv g_lnv g_rstd g_on g_onT g_og g_hi g_lo
r_tab_in r_in0 r_in1 r_in2 r_in3 r_gate_in0 r_gate_in1 r_gate_in2 r_gate_in3 r_xc r_xs r_rope r_qd r_kT r_kd r_S r_P r_o r_u r_state
r_bn r_mv r_lnv r_rstd r_on r_onT r_og r_hi r_lo state_zero
y_in0 y_in1 y_in2 y_in3 y_mul y_evac yst0 yst1 yst2 yst3
d_in0 d_in1 d_in2 d_in3 d_ln_in d_hi d_lo d_evac d_sq d_std d_rstd d_scaled d_res d_x_in
d_stored x1_stored zero_set u_lin u_tap1 u_tap0 u_gelu u_f pe_phases act_phases dve_phases sp_phases n_sq
""".split()


def build(nc, x, positions, w_stream, w_dec, b_dec, ln_post_mix, ln_post_ffn, ln_cols_in, conv_in,
          ident_in, interval_in, masks_in, ret_dec_in, ret_q_in, ret_k_in, inv_freq_in, eps_in, out):
    ctx = ExitStack()
    with ctx:
        sem = {name: ctx.enter_context(nc.semaphore(name)) for name in SEMS}

        def dram(name, shape):
            return nc.dram_tensor(name, list(shape), F32, kind="Internal").ap()

        proj_d = dram("proj_scratch", (N_ROWS, P, SEQ))
        val_d = dram("value_scratch", (N_VGROUPS, NT, P, HALF))
        loga_d = dram("loga_scratch", (NT, P, GLA_QK))
        gla_d = dram("gated_gla_scratch", (KT, P, SEQ))
        merged_d = dram("merged_scratch", (KT, P, SEQ))
        x1_d = dram("x1_scratch", (SEQ, D))
        f_d = dram("ffn_scratch", (FT, P, SEQ))
        rope_d = dram("rope_scratch", (2, P, SEQ))

        def sb(stack, name, shape, dt=F32):
            return stack.enter_context(nc.sbuf_tensor(name, list(shape), dt))

        act_hi = sb(ctx, "act_hi", (P, KT * SEQ), F32R)
        act_lo = sb(ctx, "act_lo", (P, KT * SEQ), F32R)
        w_raw = sb(ctx, "w_raw", (P, RING, D))
        w_hi = sb(ctx, "w_hi", (P, RING, D), F32R)
        w_lo = sb(ctx, "w_lo", (P, RING, D), F32R)
        ident = sb(ctx, "ident", (P, P))
        ln_col = sb(ctx, "ln_col", (P, 2, KT))
        conv_col = sb(ctx, "conv_col", (P, 2 * FT * 4))
        eps_col = sb(ctx, "eps_col", (P, 1))
        zero_col = sb(ctx, "zero_col", (P, 1))
        stat = sb(ctx, "stat", (P, 64))
        psum = ctx.enter_context(nc.psum_tensor("psum", [P, 8, HALF], F32))
        bank = psum[:, :, :].rearrange("p b n -> p (b n)")
        act_k = act_hi[:, :].rearrange("p (k n) -> p k n", k=KT)
        act_lo_k = act_lo[:, :].rearrange("p (k n) -> p k n", k=KT)
        act_r = act_hi[:, :].rearrange("p (k n) -> p k n", k=RET_KT)
        act_lo_r = act_lo[:, :].rearrange("p (k n) -> p k n", k=RET_KT)

        with ExitStack() as s:
            x_tok = sb(s, "x_tok", (P, NT, D))
            sq_junk = sb(s, "sq_junk", (P, D))
        with ExitStack() as s:
            z_sb = sb(s, "z_sb", (P, NT, GLA_QK))
            z_a = sb(s, "z_a", (P, 2, GLA_QK))
            z_e = sb(s, "z_e", (P, 2, GLA_QK))
            lr_aug = sb(s, "lr_aug", (GLA_RANK + 1, SEQ))
            wdec_aug = sb(s, "wdec_aug", (GLA_RANK + 1, GLA_QK))
            pos_i = sb(s, "pos_i", (P, SEQ), I32)
            ang = sb(s, "ang", (P, 2, SEQ))
            turn = sb(s, "turn", (P, SEQ))
            rope_out = sb(s, "rope_out", (P, 2, SEQ))
            invf = sb(s, "invf", (P, 1))
            stage_offset = sb(s, "stage_offset", (P, STAGE_OFFSET))
            stage = sb(s, "stage", (P, RING, SEQ))
        with ExitStack() as s:
            g_deccol = sb(s, "g_deccol", (P, 2, HEADS))
            g_x = sb(s, "g_x", (P, 2, 2 * HEADS, P))
            g_v = sb(s, "g_v", (P, 2, GLA_V))
            g_la = sb(s, "g_la", (P, 2, GLA_QK))
            g_gate = sb(s, "g_gate", (P, GLA_KT, P))
            masks = sb(s, "masks", (P, (NL + 1) * P))
            e_t = sb(s, "e_t", (P, 2, E_BLOCKS * P))
            g_st = sb(s, "g_st", (P, HEADS, GLA_DV))
            la_hi = sb(s, "la_hi", (P, 2, GLA_QK), F32R)
            la_lo = sb(s, "la_lo", (P, 2, GLA_QK), F32R)
            interval = sb(s, "interval", (P, E_BLOCKS * P), F32R)
            q_lev = sb(s, "q_lev", (P, 2, NL, P))
            k_lev = sb(s, "k_lev", (P, 2, NL, P))
            q_g = sb(s, "q_g", (P, 2, HEADS, P))
            k_end = sb(s, "k_end", (P, HEADS, P))
            s_masked = sb(s, "s_masked", (P, (NL + 1) * P))
            g_kdt = sb(s, "g_kdt", (P, GLA_QK))
            p_t = sb(s, "p_t", (P, HEADS, P))
            g_onb = sb(s, "g_onb", (P, GLA_V))
            g_ogb = sb(s, "g_ogb", (P, GLA_V))
            g_bst = sb(s, "g_bst", (P, HEADS, 8))
            g_mvb = sb(s, "g_mvb", (P, HEADS, 2))
            g_rsb = sb(s, "g_rsb", (P, 2, HEADS))
        with ExitStack() as s:
            r_st = sb(s, "r_st", (P, HEADS, 2, RET_DV))
            ret_dec = sb(s, "ret_dec", (P, HEADS, P))
            ret_q = sb(s, "ret_q", (P, HEADS, P))
            ret_k = sb(s, "ret_k", (P, HEADS))
            cossin = sb(s, "cossin", (P, 2, SEQ))
            r_x = sb(s, "r_x", (P, HEADS, 8, P))
            r_v = sb(s, "r_v", (P, HEADS, RET_DV))
            r_xcb = sb(s, "r_xcb", (P, 2, 4, P))
            r_xsb = sb(s, "r_xsb", (P, 2, 4, P))
            r_qk = sb(s, "r_qk", (P, HEADS, 4, P))
            r_qdb = sb(s, "r_qdb", (P, HEADS, 2, P))
            r_kdt = sb(s, "r_kdt", (P, 2, RET_DK))
            r_pt = sb(s, "r_pt", (P, 2, P))
            r_bst = sb(s, "r_bst", (P, 2, 8))
            r_mvb = sb(s, "r_mvb", (P, 2, 2))
            r_rsb = sb(s, "r_rsb", (P, 2, 2))
            with ExitStack() as s2:
                r_onb = sb(s2, "r_onb", (P, 2, RET_DV))
                r_ogb = sb(s2, "r_ogb", (P, 2, RET_DV))
            with ExitStack() as s2:
                y_in = sb(s2, "y_in", (P, 2, SEQ))
                y_out = sb(s2, "y_out", (P, 2, SEQ))
        with ExitStack() as s:
            d_raw = sb(s, "d_raw", (P, RING, HALF))
            d_hib = sb(s, "d_hib", (P, RING, HALF), F32R)
            d_lob = sb(s, "d_lob", (P, RING, HALF), F32R)
            d_ln = sb(s, "d_ln", (P, D))
            d_x = sb(s, "d_x", (P, 4, D))
            d_junk = sb(s, "d_junk", (P, D))
            with ExitStack() as s2:
                d_out = sb(s2, "d_out", (P, NT, D))
            with ExitStack() as s2:
                u_conv = sb(s2, "u_conv", (P, RING, SEQ))
                u_fb = sb(s2, "u_fb", (P, RING, SEQ))

        def repeat(eng, lo, count, body, unroll=RING, peel=1):
            def group(g):
                for j in range(unroll):
                    body(g * unroll + j, g * unroll + (lo + j), g + (lo + j) // unroll,
                         (lo + j) % unroll, isinstance(g, int) and g == 0)
            groups = count // unroll
            first = min(peel, groups)
            for g in range(first):
                group(g)
            if groups - first >= 2:
                with eng.Fori(first, groups) as g:
                    group(g)
            elif groups - first == 1:
                group(first)
            for k in range(groups * unroll, count):
                body(k, lo + k, (lo + k) // unroll, (lo + k) % unroll, groups == 0)

        raw_in = [sem[f"raw_in{j}"] for j in range(RING)]
        stored = [sem[f"st{j}"] for j in range(RING)]
        x_in = [sem[f"x_in{j}"] for j in range(4)]
        g_in = [sem["g_in0"], sem["g_in1"]]
        r_in = [sem[f"r_in{j}"] for j in range(RING)]
        r_gate_in = [sem[f"r_gate_in{j}"] for j in range(RING)]
        y_ins = [sem[f"y_in{j}"] for j in range(RING)]
        y_st = [sem[f"yst{j}"] for j in range(RING)]
        d_in = [sem[f"d_in{j}"] for j in range(RING)]

        def product3(o, s_hi, s_lo, m_hi, m_lo, start, stop):
            nc.tensor.matmul(o, s_hi, m_hi, start=start, stop=False)
            nc.tensor.matmul(o, s_hi, m_lo, start=False, stop=False)
            return nc.tensor.matmul(o, s_lo, m_hi, start=False, stop=stop)

        def end_phase(eng, who):
            eng.drain().then_inc(sem[f"{who}_phases"], 1)

        def begin_phase(eng, n):
            for who in ("pe", "act", "dve", "sp"):
                eng.wait_ge(sem[f"{who}_phases"], n)

        def load_slab(sp, n, j):
            sp.dma_start(w_raw[:, j, :], w_stream[n, :, :]).then_inc(raw_in[j], 16)

        def stream_prologue(sp):
            for n in range(RING):
                load_slab(sp, n, n)
            for n in range(RING):
                sp.wait_ge(sem["slab_ready"], n + 1)
                load_slab(sp, n + RING, n)

        def stream_step(sp, n, j):
            sp.wait_ge(sem["slab_ready"], n + RING + 1)
            load_slab(sp, n + 2 * RING, j)

        def split_slabs(pool, lo, hi):
            def body(k, n, grp, j, early):
                pool.wait_ge(raw_in[j], 16 * grp + 16)
                if not (early and lo == 0):
                    pool.wait_ge(sem["mm_half"], 2 * n - 2 * RING + 2)
                nc.gpsimd.tensor_tensor(w_hi[:, j, :], w_raw[:, j, :],
                                        zero_col[:, :].to_broadcast((P, D)), ALU.add).then_inc(sem["hi_split"], 1)
                pool.wait_ge(sem["hi_split"], n + 1)
                nc.gpsimd.tensor_tensor(w_lo[:, j, :], w_raw[:, j, :], w_hi[:, j, :].bitcast(F32),
                                        ALU.subtract).then_inc(sem["slab_ready"], 1)
            repeat(pool, lo, hi - lo, body)

        def norm_sp(sp):
            for c in range(4):
                sp.dma_start(x_tok[:, 2 * c:2 * c + 2, :],
                             x[c * 256:c * 256 + 256, :].rearrange("(t p) d -> p t d", p=P)
                             ).then_inc(x_in[c], 16)

        def norm_bank(rnd, i):
            if i < KT:
                return i
            return 2 * (i % 4) + 1 if rnd else 4 + i % 4

        def unit_cols(i):
            k, hf = i % KT, i // KT
            return slice(k * SEQ + hf * HALF, k * SEQ + hf * HALF + HALF)

        def norm_hi(act, rnd, units):
            for i in units:
                act.wait_ge(sem["x_transposed"], 2 * KT * rnd + i + 1)
                nc.scalar.activation(act_hi[:, unit_cols(i)], psum[:, norm_bank(rnd, i), :], ACT.Copy,
                                     scale=ln_col[:, rnd, i % KT:i % KT + 1]).then_inc(sem["act_hi_done"], 1)

        def norm_lo(dve, rnd, units):
            for i in units:
                dve.wait_ge(sem["act_hi_done"], 2 * KT * rnd + i + 1)
                nc.vector.scalar_tensor_tensor(act_lo[:, unit_cols(i)], psum[:, norm_bank(rnd, i), :],
                                               ln_col[:, rnd, i % KT:i % KT + 1],
                                               act_hi[:, unit_cols(i)].bitcast(F32), ALU.mult, ALU.subtract
                                               ).then_inc(sem["act_lo_done"], 1)

        def norm_act(act):
            for hf in range(2):
                for t in range(4 * hf, 4 * hf + 4):
                    if t % 2 == 0:
                        act.wait_ge(x_in[t // 2], 16)
                    if t:
                        act.wait_ge(sem["sq_done"], t)
                    nc.scalar.activation(sq_junk[:, :], x_tok[:, t, :], ACT.Square,
                                         accum_out=stat[:, t:t + 1]).then_inc(sem["sq_done"], 1)
                act.wait_ge(sem["sq_done"], 4 * hf + 4)
                act.wait_ge(sem["const_in"], 64)
                nc.scalar.activation(stat[:, 8 + 4 * hf:12 + 4 * hf], stat[:, 4 * hf:4 * hf + 4], ACT.Sqrt,
                                     scale=1.0 / D, bias=eps_col[:, 0:1]).then_inc(sem["rms_std"], 1)
                norm_hi(act, 0, range(KT * hf, KT * hf + KT))

        def norm_dve(dve):
            for hf in range(2):
                dve.wait_ge(sem["rms_std"], hf + 1)
                nc.vector.reciprocal(stat[:, 16 + 4 * hf:20 + 4 * hf], stat[:, 8 + 4 * hf:12 + 4 * hf]
                                     ).then_inc(sem["rms_rstd"], 1)
                dve.wait_ge(sem["rms_rstd"], hf + 1)
                for t in range(4 * hf, 4 * hf + 4):
                    nc.vector.tensor_scalar(x_tok[:, t, :], x_tok[:, t, :], stat[:, 16 + t:17 + t], None,
                                            ALU.mult).then_inc(sem["x_scaled"], 1)
                norm_lo(dve, 0, range(KT * hf, KT * hf + KT))

        def norm_transposes(pe, hf):
            for i in range(KT * hf, KT * hf + KT):
                pe.wait_ge(sem["x_scaled"], 4 * hf + 4)
                if hf:
                    pe.wait_ge(sem["act_lo_done"], KT if i < KT + 4 else i - 3)
                for q in range(4):
                    last = nc.tensor.transpose(psum[:, norm_bank(0, i), q * P:(q + 1) * P],
                                               x_tok[:, 4 * hf + q, (i % KT) * P:(i % KT + 1) * P], ident[:, :])
                last.then_inc(sem["x_transposed"], 1)

        def half_product(j, pair, hf):
            for k in range(KT):
                sl = slice(k * SEQ + hf * HALF, k * SEQ + hf * HALF + HALF)
                last = product3(psum[:, 2 * pair + hf, :], w_hi[:, j, k * P:(k + 1) * P],
                                w_lo[:, j, k * P:(k + 1) * P], act_hi[:, sl], act_lo[:, sl],
                                k == 0, k == KT - 1)
            return last

        def slab_product(pe, n, j, pair):
            pe.wait_ge(sem["slab_ready"], n + 1)
            half_product(j, pair, 0)
            half_product(j, pair, 1).then_inc(sem["mm_half"], 2)

        def pair_view(pair):
            return bank[:, pair * SEQ:(pair + 1) * SEQ]

        def proj_pe(pe):
            def values(g, a):
                for i in range(4):
                    j = (SL_VAL + i) % RING
                    pe.wait_ge(sem["slab_ready"], 4 * g + (SL_VAL + i + 1))
                    for c in range(2):
                        k = 2 * i + c
                        for tok in range(4):
                            sl = slice(k * SEQ + (4 * a + tok) * P, k * SEQ + (4 * a + tok + 1) * P)
                            last = product3(psum[:, 4 * a + tok, :], act_hi[:, sl], act_lo[:, sl],
                                            w_hi[:, j, c * HALF:(c + 1) * HALF],
                                            w_lo[:, j, c * HALF:(c + 1) * HALF], k == 0, k == KT - 1)
                    if a:
                        last.then_inc(sem["mm_half"], 2)
                if not a:
                    last.then_inc(sem["val_half"], 1)

            norm_transposes(pe, 0)
            pe.wait_ge(sem["act_lo_done"], KT)
            values(0, 0)
            norm_transposes(pe, 1)
            end_phase(pe, "pe")
            pe.wait_ge(sem["act_lo_done"], 2 * KT)
            values(0, 1)
            with pe.Fori(1, N_VGROUPS) as g:
                for a in range(2):
                    pe.wait_ge(sem["val_evac"], 4 * g - 2 + 2 * a)
                    values(g, a)

            pe.wait_ge(sem["val_evac"], 4 * N_VGROUPS - 3)
            slab_product(pe, SL_LR, SL_LR % RING, 0)
            pe.wait_ge(sem["lr_out"], 2)
            pe.wait_ge(sem["lr_in"], 32)
            for t in range(NT):
                if t >= 2:
                    pe.wait_ge(sem["val_evac"], 4 * N_VGROUPS - 3 + t // 2)
                nc.tensor.matmul(psum[:, t, :], lr_aug[:, t * P:(t + 1) * P], wdec_aug[:, :],
                                 start=True, stop=True).then_inc(sem["z_out"], 1)

            def body(k, n, grp, j, early):
                pair = (j - SL_PROJ) % RING
                if early:
                    pe.wait_ge(sem["z_copied"], 2 * pair + 2)
                else:
                    pe.wait_ge(sem["proj_evac"], k - RING + 1)
                slab_product(pe, n, j, pair)
            repeat(pe, SL_PROJ, N_ROWS, body)

        def proj_act(act):
            def values(g):
                for u in range(RING):
                    if u < 2:
                        act.wait_ge(sem["val_half"], g + 1)
                    else:
                        act.wait_ge(sem["mm_half"], 8 * g + 2 * (SL_VAL + 4))
                    if not (isinstance(g, int) and g == 0):
                        act.wait_ge(stored[u], 16 * g)
                    nc.scalar.activation(stage[:, u, :], pair_view(u), ACT.Copy).then_inc(sem["val_evac"], 1)
            values(0)
            with act.Fori(1, N_VGROUPS) as g:
                values(g)
            load_exp_ln(act)
            for t in range(NT):
                b = t % 2
                act.wait_ge(sem["z_abs"], t + 1)
                nc.scalar.activation(z_e[:, b, :], z_a[:, b, :], ACT.Exp, scale=-1.0
                                     ).then_inc(sem["z_exp"], 1)
                act.wait_ge(sem["z_exp"], t + 1)
                nc.scalar.activation(z_a[:, b, :], z_e[:, b, :], ACT.Ln, bias=1.0
                                     ).then_inc(sem["z_ln"], 1)
            act.wait_ge(sem["angle_red"], 1)
            nc.scalar.activation(rope_out[:, 1, :], ang[:, 0, :], ACT.Sin).then_inc(sem["sin_half"], 1)
            nc.scalar.activation(ang[:, 1, :], ang[:, 0, :], ACT.Sin, scale=0.5).then_inc(sem["sin_half"], 1)

            def rows(lo, hi, func):
                def body(k, row, grp, j, early):
                    act.wait_ge(sem["mm_half"], 2 * row + 2 * SL_PROJ + 2)
                    act.wait_ge(stored[j], 16 * (N_VGROUPS + grp))
                    nc.scalar.activation(stage[:, j, :], pair_view(j), func).then_inc(sem["proj_evac"], 1)
                repeat(act, lo, hi - lo, body)
            rows(0, ROW_GR, ACT.Copy)
            rows(ROW_GR, ROW_AG, ACT.Silu)
            rows(ROW_AG, N_ROWS - 2, ACT.Sigmoid)
            gla_first_parts(act)
            rows(N_ROWS - 2, N_ROWS, ACT.Sigmoid)

        def proj_dve(dve):
            nc.vector.memset(lr_aug[:, :], 1.0).then_inc(sem["lr_ones"], 1)
            dve.wait_ge(sem["mm_half"], 2 * SL_LR + 2)
            dve.wait_ge(sem["lr_ones"], 1)
            for hf in range(2):
                nc.vector.tensor_copy(lr_aug[0:GLA_RANK, hf * HALF:hf * HALF + HALF],
                                      psum[0:GLA_RANK, hf, :]).then_inc(sem["lr_out"], 1)
            for t in range(NT):
                dve.wait_ge(sem["z_out"], t + 1)
                nc.vector.tensor_copy(z_sb[:, t, :], psum[:, t, :]).then_inc(sem["z_copied"], 1)

            def log_a_tail(t):
                dve.wait_ge(sem["z_ln"], t + 1)
                nc.vector.scalar_tensor_tensor(z_sb[:, t, :], z_sb[:, t, :], 0.0, z_a[:, t % 2, :],
                                               ALU.min, ALU.subtract).then_inc(sem["log_a"], 1)
            dve.wait_ge(sem["z_copied"], NT)
            for t in range(NT):
                if t >= 2:
                    log_a_tail(t - 2)
                    dve.wait_ge(sem["log_a"], t - 1)
                nc.vector.scalar_tensor_tensor(z_a[:, t % 2, :], z_sb[:, t, :], -1.0, z_sb[:, t, :],
                                               ALU.mult, ALU.max).then_inc(sem["z_abs"], 1)
            log_a_tail(NT - 2)
            log_a_tail(NT - 1)
            dve.wait_ge(sem["pos_in"], 32)
            nc.vector.tensor_copy(ang[:, 1, :], pos_i[:, :]).then_inc(sem["pos_f"], 1)
            dve.wait_ge(sem["pos_f"], 1)
            nc.vector.tensor_scalar(ang[:, 0, :], ang[:, 1, :], invf[:, 0:1], None, ALU.mult
                                    ).then_inc(sem["angle"], 1)
            dve.wait_ge(sem["angle"], 1)
            magic = 1.5 * 2.0 ** 23
            nc.vector.tensor_scalar(turn[:, :], ang[:, 0, :], 1.0 / (2.0 * math.pi), magic,
                                    ALU.mult, ALU.add).then_inc(sem["turns0"], 1)
            dve.wait_ge(sem["turns0"], 1)
            nc.vector.tensor_scalar(turn[:, :], turn[:, :], magic, None, ALU.subtract
                                    ).then_inc(sem["turns1"], 1)
            dve.wait_ge(sem["turns1"], 1)
            for i, part in enumerate(two_pi_parts()):
                nc.vector.scalar_tensor_tensor(ang[:, 0, :], turn[:, :], -part, ang[:, 0, :],
                                               ALU.mult, ALU.add).then_inc(sem["angle"], 1)
                dve.wait_ge(sem["angle"], i + 2)
            nc.vector.tensor_scalar(ang[:, 0, :], ang[:, 0, :], 3.1415925, -3.1415925,
                                    ALU.min, ALU.max).then_inc(sem["angle_red"], 1)
            dve.wait_ge(sem["sin_half"], 2)
            nc.vector.tensor_tensor(ang[:, 0, :], ang[:, 1, :], ang[:, 1, :], ALU.mult
                                    ).then_inc(sem["cos_sq"], 1)
            dve.wait_ge(sem["cos_sq"], 1)
            nc.vector.tensor_scalar(rope_out[:, 0, :], ang[:, 0, :], -2.0, 1.0, ALU.mult, ALU.add
                                    ).then_inc(sem["rope_done"], 1)

        def proj_sp(sp):
            sp.dma_start(wdec_aug[0:GLA_RANK, :], w_dec).then_inc(sem["lr_in"], 16)
            sp.dma_start(wdec_aug[GLA_RANK:GLA_RANK + 1, :], b_dec).then_inc(sem["lr_in"], 16)
            sp.dma_start(pos_i[:, :], positions.to_broadcast((P, SEQ))).then_inc(sem["pos_in"], 16)
            sp.dma_start(invf[:, :], inv_freq_in).then_inc(sem["pos_in"], 16)

            def values(g):
                for u in range(RING):
                    sp.wait_ge(sem["val_evac"], 4 * g + u + 1)
                    sp.dma_start(val_d[g, 2 * u:2 * u + 2, :, :].rearrange("t p n -> p t n"),
                                 stage[:, u, :].rearrange("p (t n) -> p t n", t=2)).then_inc(stored[u], 16)
                    if u == 1:
                        for i in range(4):
                            stream_step(sp, 4 * g + (SL_VAL + i), (SL_VAL + i) % RING)
            values(0)
            with sp.Fori(1, N_VGROUPS) as g:
                values(g)
            stream_step(sp, SL_LR, SL_LR % RING)

            def body(k, n, grp, j, early):
                slot = (j - SL_PROJ) % RING
                sp.wait_ge(sem["proj_evac"], k + 1)
                sp.dma_start(proj_d[k, :, :], stage[:, slot, :]).then_inc(stored[slot], 16)
                if not (isinstance(k, int) and k >= N_ROWS - RING):
                    stream_step(sp, n, j)
            ahead = 2 * RING
            repeat(sp, SL_PROJ, N_ROWS - ahead, body)
            sp.wait_ge(sem["log_a"], NT)
            sp.dma_start(loga_d.rearrange("t p c -> p t c"), z_sb[:, :, :]).then_inc(sem["loga_stored"], 16)
            sp.wait_ge(sem["rope_done"], 1)
            sp.dma_start(rope_d.rearrange("a p n -> p a n"), rope_out[:, :, :]).then_inc(sem["rope_stored"], 16)
            sp.wait_ge(sem["loga_stored"], 16)
            sp.wait_ge(sem["rope_stored"], 16)
            for j in range(RING):
                sp.wait_ge(stored[j], 16 * (PROJ_STORES - ahead // RING))
            gla_first_loads(sp)
            for k in range(N_ROWS - ahead, N_ROWS):
                body(k, SL_PROJ + k, (SL_PROJ + k) // RING, (SL_PROJ + k) % RING, False)
            for j in range(RING):
                sp.wait_ge(stored[j], 16 * PROJ_STORES)

        o_bank, gate_bank = (6, 7), (7, 5)
        kt_bank, u_bank = 6, 5

        def tile_cols(t):
            return slice(t * P, t * P + P) if isinstance(t, int) else bass.ds(t * P, P)

        def over_gla_tiles(eng, body):
            repeat(eng, 0, NT - 1, body, unroll=2)
            body(NT - 1, NT - 1, (NT - 1) // 2, (NT - 1) % 2, False, last=True)

        def head_cols(h):
            return slice((h % 2) * GLA_DV, (h % 2 + 1) * GLA_DV)

        def gla_gates(sp, t):
            if not (isinstance(t, int) and t < 1):
                sp.wait_ge(sem["g_og"], 2 * t)
            sp.dma_start(g_gate[:, :, :], proj_d[ROW_GR:ROW_GR + GLA_KT, :, tile_cols(t)]
                         .rearrange("r p n -> p r n")).then_inc(sem["g_gate_in"], 16)

        def gla_tile_loads(sp, t, d):
            sp.dma_start(g_x[:, d, :, :], proj_d[ROW_GLA:ROW_GLA + 2 * HEADS, :, tile_cols(t)]
                         .rearrange("r p n -> p r n")).then_inc(g_in[d], 16)
            sp.dma_start(g_v[:, d, :].rearrange("p (g n) -> p g n", n=HALF),
                         val_d[0:GV_GROUPS, t, :, :].rearrange("g p n -> p g n")).then_inc(g_in[d], 16)
            sp.dma_start(g_la[:, d, :], loga_d[t, :, :]).then_inc(g_in[d], 16)

        def gla_first_loads(sp):
            sp.dma_start(masks[:, :], masks_in).then_inc(sem["g_tab_in"], 16)
            sp.dma_start(e_t[:, 0, :], interval_in).then_inc(sem["g_tab_in"], 16)
            for t in range(2):
                gla_tile_loads(sp, t, t)
            gla_gates(sp, 0)

        def gla_sp(sp):
            def body(k, t, grp, d, early):
                sp.wait_ge(sem["g_u"], 2 * k + 2)
                gla_tile_loads(sp, k + 2, d)
                gla_gates(sp, k + 1)
            repeat(sp, 2, NT - 2, body, unroll=2)
            gla_gates(sp, NT - 1)
            for n in range(SL_YGLA - RING, SL_YGLA):
                stream_step(sp, n, n % RING)

        def load_exp_ln(act):
            act.add_instruction(mybir.InstLoadActFuncSet(name=nc.get_next_instruction_name(), engine=act.engine,
                                                         act_func_set_id=ACT_SET_EXP_LN))

        def log_a_hi(act, t, grp, d):
            act.wait_ge(g_in[d], 48 * grp + 48)
            if not (isinstance(t, int) and t < 2):
                act.wait_ge(sem["g_E"], 4 * t - 4)
            nc.scalar.activation(la_hi[:, d, :], g_la[:, d, :], ACT.Copy).then_inc(sem["g_la_hi"], 1)

        def gla_first_parts(act):
            act.wait_ge(sem["g_tab_in"], 32)
            nc.scalar.activation(interval[:, :], e_t[:, 0, :], ACT.Copy).then_inc(sem["g_tab"], 1)
            act.wait_ge(sem["g_tab"], 1)
            log_a_hi(act, 0, 0, 0)

        def gla_act(act):
            load_exp_ln(act)

            def gated_hi(t):
                for i in range(2):
                    act.wait_ge(sem["g_og"], 2 * t + i + 1)
                    act.wait_ge(sem["g_tab"], 1)
                    nc.scalar.activation(act_k[:, 4 * i:4 * i + 4, tile_cols(t)],
                                         g_ogb[:, i * HALF:(i + 1) * HALF].rearrange("p (q n) -> p q n", q=4),
                                         ACT.Copy).then_inc(sem["g_hi"], 1)

            def keys(t):
                act.wait_ge(sem["g_kT"], t + 1)
                if not (isinstance(t, int) and t < 1):
                    act.wait_ge(sem["g_u"], 2 * t)
                nc.scalar.activation(g_kdt[:, :], psum[:, kt_bank, :], ACT.Copy,
                                     scale=GLA_DK ** -0.5).then_inc(sem["g_kd"], 1)

            def rstd(t, i):
                act.wait_ge(sem["g_mv"], 4 * t + 2 * i + 2)
                nc.scalar.activation(g_rsb[:, 0, 2 * i:2 * i + 2], g_mvb[:, 2 * i:2 * i + 2, 1],
                                     ACT.Ln, bias=eps_col[:, 0:1]).then_inc(sem["g_lnv"], 1)
                act.wait_ge(sem["g_lnv"], 2 * t + i + 1)
                nc.scalar.activation(g_rsb[:, 1, 2 * i:2 * i + 2], g_rsb[:, 0, 2 * i:2 * i + 2],
                                     ACT.Exp, scale=-0.5).then_inc(sem["g_rstd"], 1)

            def body(k, t, grp, d, early, last=False):
                first = early and d == 0

                def decay(h):
                    e = 4 * t + h
                    act.wait_ge(sem["g_E"], e + 1)
                    if not (first and h < 2):
                        act.wait_ge(sem["g_dec"], e - 1)
                        act.wait_ge(sem["g_kend"], e - 1)
                    nc.scalar.activation(e_t[:, h % 2, :], bank[:, 0:E_BLOCKS * P], ACT.Exp
                                         ).then_inc(sem["g_exp"], 1)

                if early and d == 1:
                    begin_phase(act, 2)
                if not first:
                    keys(t - 1)
                decay(0)
                decay(1)
                if not first:
                    rstd(t - 1, 0)
                    rstd(t - 1, 1)
                decay(2)
                if not last:
                    log_a_hi(act, t + 1, grp + d, 1 - d)
                decay(3)
                if not first:
                    gated_hi(t - 1)
            over_gla_tiles(act, body)
            keys(NT - 1)
            rstd(NT - 1, 0)
            rstd(NT - 1, 1)
            gated_hi(NT - 1)

        def gla_pool(pool):
            def log_a_lo(t, d):
                pool.wait_ge(sem["g_la_hi"], t + 1)
                nc.gpsimd.tensor_tensor(la_lo[:, d, :], g_la[:, d, :], la_hi[:, d, :].bitcast(F32),
                                        ALU.subtract).then_inc(sem["g_la_lo"], 1)

            def gated_lo(t):
                pool.wait_ge(sem["g_hi"], 2 * t + 2)
                pool.wait_ge(sem["g_tab"], 1)
                nc.gpsimd.tensor_tensor(act_lo_k[:, :, tile_cols(t)],
                                        g_ogb[:, :].rearrange("p (q n) -> p q n", q=KT),
                                        act_k[:, :, tile_cols(t)].bitcast(F32),
                                        ALU.subtract).then_inc(sem["g_lo"], 1)

            def body(k, t, grp, d, early, last=False):
                first = early and d == 0
                for h in range(HEADS):
                    e = 4 * t + h
                    b = h % 2
                    pool.wait_ge(sem["g_exp"], e + 1)
                    if not (first and h < 2):
                        pool.wait_ge(sem["g_S"], e - 1)
                    key = g_x[:, d, 2 * h + 1, :]
                    levels = e_t[:, b, P:(NL + 1) * P].rearrange("p (l n) -> p l n", l=NL)
                    nc.gpsimd.tensor_tensor(k_lev[:, b, :, :], levels,
                                            key.unsqueeze(1).to_broadcast((P, NL, P)),
                                            ALU.mult).then_inc(sem["g_klev"], 1)
                    if not first:
                        pool.wait_ge(sem["g_kT"], t)
                    nc.gpsimd.tensor_tensor(k_end[:, h, :], e_t[:, b, 0:P], key, ALU.mult
                                            ).then_inc(sem["g_kend"], 1)
                    if h == HEADS - 2 and not last:
                        log_a_lo(t + 1, 1 - d)
                if not first:
                    gated_lo(t - 1)
            log_a_lo(0, 0)
            over_gla_tiles(pool, body)
            split_slabs(pool, SL_YGLA, SL_YGLA + 2)
            gated_lo(NT - 1)
            split_slabs(pool, SL_YGLA + 2, SL_YGLA + RING)

        def gla_dve(dve):
            nc.vector.memset(g_st[:, :, :], 0.0).then_inc(sem["state_zero"], 1)
            dve.wait_ge(sem["g_tab_in"], 32)

            def gate(t):
                dve.wait_ge(sem["g_gate_in"], 16 * t + 16)
                if not (isinstance(t, int) and t < 1):
                    dve.wait_ge(sem["g_lo"], t)
                for i in range(2):
                    dve.wait_ge(sem["g_onT"], 2 * t + i + 1)
                    nc.vector.tensor_tensor(g_ogb[:, i * HALF:(i + 1) * HALF], psum[:, gate_bank[i], :],
                                            g_gate[:, 4 * i:4 * i + 4, :].rearrange("p q n -> p (q n)"),
                                            ALU.mult).then_inc(sem["g_og"], 1)

            def stats(t, i):
                dve.wait_ge(sem["g_o"], 2 * t + i + 1)
                for h in (2 * i, 2 * i + 1):
                    both = nc.vector.bn_stats(g_bst[:, h, 0:6], psum[:, o_bank[i], head_cols(h)])
                both.then_inc(sem["g_bn"], 1)
                dve.wait_ge(sem["g_tab_in"], 32)
                dve.wait_ge(sem["g_bn"], 2 * t + i + 1)
                for h in (2 * i, 2 * i + 1):
                    nc.vector.bn_aggr(g_mvb[:, h, :], g_bst[:, h, 0:6]).then_inc(sem["g_mv"], 1)

            def normed(t, i):
                dve.wait_ge(sem["g_mv"], 4 * t + 2 * i + 2)
                dve.wait_ge(sem["g_rstd"], 2 * t + i + 1)
                if not (isinstance(t, int) and t < 1):
                    dve.wait_ge(sem["g_onT"], 2 * t)
                for h in (2 * i, 2 * i + 1):
                    nc.vector.tensor_scalar(g_onb[:, h * GLA_DV:(h + 1) * GLA_DV],
                                            psum[:, o_bank[i], head_cols(h)],
                                            g_mvb[:, h, 0:1], g_rsb[:, 1, h:h + 1],
                                            ALU.subtract, ALU.mult).then_inc(sem["g_on"], 1)

            def states(t, d, i):
                dve.wait_ge(sem["g_dec"], 4 * t + 4)
                dve.wait_ge(sem["g_u"], 2 * t + i + 1)
                for h in (2 * i, 2 * i + 1):
                    nc.vector.scalar_tensor_tensor(g_st[:, h, :], g_st[:, h, :], g_deccol[:, d, h:h + 1],
                                                   psum[:, u_bank, head_cols(h)],
                                                   ALU.mult, ALU.add).then_inc(sem["g_state"], 1)

            def body(k, t, grp, d, early, last=False):
                first = early and d == 0

                def queries(h):
                    e, b = 4 * t + h, h % 2
                    dve.wait_ge(sem["g_exp"], e + 1)
                    if not (first and h < 2):
                        dve.wait_ge(sem["g_S"], e - 1)
                    q = g_x[:, d, 2 * h, :]
                    levels = e_t[:, b, P:(NL + 1) * P].rearrange("p (l n) -> p l n", l=NL)
                    nc.vector.tensor_tensor(q_lev[:, b, :, :], levels,
                                            q.unsqueeze(1).to_broadcast((P, NL, P)), ALU.mult)
                    if not early:
                        dve.wait_ge(sem["g_o"], 2 * t - 2)
                    nc.vector.tensor_tensor(q_g[:, d, h, :], e_t[:, b, (NL + 1) * P:], q, ALU.mult
                                            ).then_inc(sem["g_qG"], 1)
                    nc.vector.tensor_copy(g_deccol[:, d, h:h + 1], e_t[:, b, E_BLOCKS * P - 1:]
                                          ).then_inc(sem["g_dec"], 1)

                def scores(h):
                    e = 4 * t + h
                    dve.wait_ge(sem["g_S"], e + 1)
                    if not (first and h == 0):
                        dve.wait_ge(sem["g_P"], e)
                    nc.vector.tensor_tensor(s_masked[:, :], bank[:, 3 * HALF:5 * HALF], masks[:, :],
                                            ALU.mult).then_inc(sem["g_mask"], 1)
                    dve.wait_ge(sem["g_mask"], e + 1)
                    if first and h == 0:
                        begin_phase(dve, 2)
                    if not first:
                        dve.wait_ge(sem["g_o"], 2 * t - 1 + h // 2)
                    nc.vector.tensor_reduce(p_t[:, h, :],
                                            s_masked[:, :].rearrange("p (l n) -> p n l", n=P),
                                            AX.X, ALU.add).then_inc(sem["g_P"], 1)

                queries(0)
                if not first:
                    stats(t - 1, 0)
                queries(1)
                if not first:
                    normed(t - 1, 0)
                    states(t - 1, 1 - d, 0)
                scores(0)
                if not first:
                    stats(t - 1, 1)
                    states(t - 1, 1 - d, 1)
                    normed(t - 1, 1)
                queries(2)
                scores(1)
                queries(3)
                scores(2)
                if not first:
                    gate(t - 1)
                scores(3)
            dve.wait_ge(sem["state_zero"], 1)
            over_gla_tiles(dve, body)
            d = (NT - 1) % 2
            for i in range(2):
                stats(NT - 1, i)
                normed(NT - 1, i)
                states(NT - 1, d, i)
            gate(NT - 1)

        def gla_pe(pe):
            pe.wait_ge(sem["g_tab"], 1)
            pe.wait_ge(sem["state_zero"], 1)
            pe.wait_ge(sem["proj_evac"], N_ROWS)

            def out_transposes(t):
                for i in range(2):
                    if i == 0:
                        pe.wait_ge(sem["g_on"], 4 * t + 4)
                    else:
                        pe.wait_ge(sem["g_state"], 4 * t + 4)
                    for q in range(4):
                        last = nc.tensor.transpose(psum[:, gate_bank[i], q * P:(q + 1) * P],
                                                   g_onb[:, (4 * i + q) * P:(4 * i + q + 1) * P], ident[:, :])
                    last.then_inc(sem["g_onT"], 1)

            def key_transposes(t):
                pe.wait_ge(sem["g_kend"], 4 * t + 4)
                for h in range(HEADS):
                    last = nc.tensor.transpose(psum[:, kt_bank, h * P:(h + 1) * P], k_end[:, h, :], ident[:, :])
                last.then_inc(sem["g_kT"], 1)

            def outputs(t, d, i):
                start = isinstance(t, int) and t < 1
                pe.wait_ge(sem["g_kd"], t + 1)
                pe.wait_ge(sem["g_P"], 4 * t + 2 * i + 2)
                pe.wait_ge(sem["g_qG"], 4 * t + 2 * i + 2)
                if not start:
                    pe.wait_ge(sem["g_state"], 4 * t - 2 + 2 * i)
                    if i == 1:
                        pe.wait_ge(sem["g_og"], 2 * t)
                for h in (2 * i, 2 * i + 1):
                    o = psum[:, o_bank[i], head_cols(h)]
                    nc.tensor.matmul(o, p_t[:, h, :], g_v[:, d, h * GLA_DV:(h + 1) * GLA_DV],
                                     start=True, stop=False)
                    last = nc.tensor.matmul(o, q_g[:, d, h, :], g_st[:, h, :], start=False, stop=True)
                last.then_inc(sem["g_o"], 1)

            def state_inputs(t, d, i):
                if i == 1:
                    pe.wait_ge(sem["g_state"], 4 * t + 2)
                elif not (isinstance(t, int) and t < 1):
                    pe.wait_ge(sem["g_og"], 2 * t)
                for h in (2 * i, 2 * i + 1):
                    last = nc.tensor.matmul(psum[:, u_bank, head_cols(h)], g_kdt[:, h * P:(h + 1) * P],
                                            g_v[:, d, h * GLA_DV:(h + 1) * GLA_DV], start=True, stop=True)
                last.then_inc(sem["g_u"], 1)

            def body(k, t, grp, d, early, last=False):
                first = early and d == 0

                def decay(h):
                    e = 4 * t + h
                    pe.wait_ge(sem["g_la_lo"], t + 1)
                    if not (first and h == 0):
                        pe.wait_ge(sem["g_exp"], e)
                    for c0 in range(0, E_BLOCKS * P, HALF):
                        c1 = min(c0 + HALF, E_BLOCKS * P)
                        nc.tensor.matmul(bank[:, c0:c1], la_hi[:, d, h * P:(h + 1) * P], interval[:, c0:c1],
                                         start=True, stop=False)
                        done = nc.tensor.matmul(bank[:, c0:c1], la_lo[:, d, h * P:(h + 1) * P],
                                                interval[:, c0:c1], start=False, stop=True)
                    done.then_inc(sem["g_E"], 1)

                def scores(h):
                    e, b = 4 * t + h, h % 2
                    pe.wait_ge(sem["g_klev"], e + 1)
                    pe.wait_ge(sem["g_qG"], e + 1)
                    if not (first and h == 0):
                        pe.wait_ge(sem["g_mask"], e)
                    for l in range(NL + 1):
                        o = bank[:, 3 * HALF + l * P:3 * HALF + (l + 1) * P]
                        key = k_lev[:, b, l, :] if l < NL else g_x[:, d, 2 * h + 1, :]
                        query = q_lev[:, b, l, :] if l < NL else g_x[:, d, 2 * h, :]
                        done = nc.tensor.matmul(o, key, query, start=True, stop=True)
                    done.then_inc(sem["g_S"], 1)

                if not first:
                    key_transposes(t - 1)
                decay(0)
                if not first:
                    outputs(t - 1, 1 - d, 0)
                decay(1)
                if not first:
                    state_inputs(t - 1, 1 - d, 0)
                scores(0)
                if not first:
                    outputs(t - 1, 1 - d, 1)
                    state_inputs(t - 1, 1 - d, 1)
                decay(2)
                scores(1)
                decay(3)
                scores(2)
                if not first:
                    out_transposes(t - 1)
                scores(3)
            over_gla_tiles(pe, body)
            key_transposes(NT - 1)
            for i in range(2):
                outputs(NT - 1, (NT - 1) % 2, i)
                state_inputs(NT - 1, (NT - 1) % 2, i)
            out_transposes(NT - 1)
            pe.wait_ge(sem["g_lo"], NT)

        def wait_y_out(dve, grp, slot):
            dve.wait_ge(y_st[(slot + 2) % RING], 16 * grp + (16 if slot >= 2 else 0))

        def ygla_sp(sp):
            begin_phase(sp, 3)

            def gate_load(k, slot):
                if not (isinstance(k, int) and k < 2):
                    sp.wait_ge(sem["y_evac"], k - 1)
                sp.dma_start(y_in[:, slot % 2, :], proj_d[k + ROW_AG, :, :]).then_inc(y_ins[slot], 16)

            def out_store(k, slot):
                sp.wait_ge(sem["y_evac"], k + 1)
                sp.dma_start(gla_d[k, :, :], y_out[:, slot % 2, :]).then_inc(y_st[slot], 16)

            gate_load(0, 0)
            for k in range(KT):
                if k == 2:
                    ret_first_loads(sp)
                if k + 1 < KT:
                    gate_load(k + 1, (k + 1) % RING)
                if k:
                    out_store(k - 1, (k - 1) % RING)
                if k < KT - RING:
                    stream_step(sp, SL_YGLA + k, (SL_YGLA + k) % RING)
            out_store(KT - 1, (KT - 1) % RING)
            for j in range(RING):
                sp.wait_ge(y_st[j], 16 * KT // RING)

        def ygla_dve(dve):
            begin_phase(dve, 3)
            nc.vector.memset(r_st[:, :, :, :].rearrange("p h a n -> p (h a n)"), 0.0
                             ).then_inc(sem["state_zero"], 1)

            def body(k, c, grp, slot, early):
                dve.wait_ge(sem["mm_half"], 2 * k + 2 * SL_YGLA + 2)
                dve.wait_ge(y_ins[slot], 16 * grp + 16)
                if not (early and slot < 2):
                    wait_y_out(dve, grp, slot)
                nc.vector.tensor_tensor(y_out[:, slot % 2, :], pair_view(slot), y_in[:, slot % 2, :], ALU.mult
                                        ).then_inc(sem["y_evac"], 1)
            repeat(dve, 0, KT, body)

        def ygla_pe(pe):
            def body(k, n, grp, j, early):
                if not early:
                    pe.wait_ge(sem["y_evac"], k - RING + 1)
                slab_product(pe, n, j, (j - SL_YGLA) % RING)
            repeat(pe, SL_YGLA, KT, body)

        y_count = [KT, 2 * KT]
        RS = 4 * HEADS

        def ret_step_loads(sp, e, t, h, wait):
            cols = tile_cols(t)
            if wait:
                sp.wait_ge(sem["r_u"], e - 3)
            sp.dma_start(r_x[:, h, 0:4, :], proj_d[ROW_RET + 4 * h:ROW_RET + 4 * h + 4, :, cols]
                         .rearrange("r p n -> p r n")).then_inc(r_in[h], 16)
            sp.dma_start(r_v[:, h, :], val_d[GV_GROUPS + h, t, :, :]).then_inc(r_in[h], 16)
            if wait:
                sp.wait_ge(sem["r_og"], e - 3)
            sp.dma_start(r_x[:, h, 4:8, :], proj_d[ROW_RG + 4 * h:ROW_RG + 4 * h + 4, :, cols]
                         .rearrange("r p n -> p r n")).then_inc(r_gate_in[h], 16)

        def ret_first_loads(sp):
            sp.dma_start(ret_dec[:, :, :].rearrange("p h n -> p (h n)"), ret_dec_in).then_inc(sem["r_tab_in"], 16)
            sp.dma_start(ret_q[:, :, :].rearrange("p h n -> p (h n)"), ret_q_in).then_inc(sem["r_tab_in"], 16)
            sp.dma_start(ret_k[:, :], ret_k_in).then_inc(sem["r_tab_in"], 16)
            sp.dma_start(cossin[:, :, :], rope_d.rearrange("a p n -> p a n")).then_inc(sem["r_tab_in"], 16)
            for h in range(HEADS):
                ret_step_loads(sp, h, 0, h, False)

        def ret_sp(sp, hf):
            lo = hf * RS + HEADS
            for h in range(HEADS):
                ret_step_loads(sp, lo + h, lo // HEADS, h, True)
            first = SL_YRET + hf * 2 * KT
            for n in range(first - RING, first):
                stream_step(sp, n, n % RING)
            repeat(sp, lo + HEADS, RS - 2 * HEADS,
                   lambda k, e, t, h, early: ret_step_loads(sp, e, t, h, True))

        def over_steps(eng, hf, body):
            if hf == 0:
                repeat(eng, 0, RS, body, peel=2)
            else:
                repeat(eng, RS, RS - HEADS, body)
                for h in range(HEADS):
                    body(RS - HEADS + h, 2 * RS - HEADS + h, NT - 1, h, False)

        def in_last_tile(e):
            return isinstance(e, int) and e >= 2 * RS - HEADS

        def tile_before(k, t, h, back):
            return (k - back) // HEADS if isinstance(k, int) else t if h >= back else t - 1

        def ret_pool(pool, hf):
            if hf == 0:
                pool.wait_ge(sem["r_tab_in"], 64)

            def body(k, e, t, h, early):
                b = h % 2
                x4 = r_x[:, h, 0:4, :]
                pool.wait_ge(sem["r_tab_in"], 64)
                pool.wait_ge(r_in[h], 32 * t + 32)
                cos = cossin[:, 0, tile_cols(t)].unsqueeze(1).to_broadcast((P, 4, P))
                sin = cossin[:, 1, tile_cols(t)].unsqueeze(1).to_broadcast((P, 4, P))
                nc.gpsimd.tensor_tensor(r_xcb[:, b, :, :], x4, cos, ALU.mult).then_inc(sem["r_xc"], 1)
                nc.gpsimd.tensor_tensor(r_xsb[:, b, :, :], x4, sin, ALU.mult).then_inc(sem["r_xs"], 1)
                pool.wait_ge(sem["r_xc"], e + 1)
                pool.wait_ge(sem["r_xs"], e + 1)
                if not (hf == 0 and early):
                    pool.wait_ge(sem["r_o"], e - 3)
                xc = r_xcb[:, b, :, :].rearrange("p (a c) n -> p a c n", c=2)
                xs = r_xsb[:, b, :, :].rearrange("p (a c) n -> p a c n", c=2)
                qk = r_qk[:, h, :, :].rearrange("p (a c) n -> p a c n", c=2)
                nc.gpsimd.tensor_tensor(qk[:, :, 0, :], xc[:, :, 0, :], xs[:, :, 1, :], ALU.subtract
                                        ).then_inc(sem["r_rope"], 1)
                nc.gpsimd.tensor_tensor(qk[:, :, 1, :], xs[:, :, 0, :], xc[:, :, 1, :], ALU.add
                                        ).then_inc(sem["r_rope"], 1)
                pool.wait_ge(sem["r_rope"], 2 * e + 2)
                nc.gpsimd.tensor_tensor(r_qdb[:, h, :, :], r_qk[:, h, 0:2, :],
                                        ret_q[:, h, :].unsqueeze(1).to_broadcast((P, 2, P)),
                                        ALU.mult).then_inc(sem["r_qd"], 1)
            def step(k):
                body(k, hf * RS + k, (hf * RS + k) // HEADS, k % HEADS, k < HEADS)

            for k in range(HEADS):
                step(k)
            slab = SL_YRET + hf * 2 * KT
            split_slabs(pool, slab, slab + 2)
            step(HEADS)
            split_slabs(pool, slab + 2, slab + 3)
            step(HEADS + 1)
            split_slabs(pool, slab + 3, slab + RING)
            repeat(pool, hf * RS + HEADS + 2, RS - HEADS - 2, lambda k, e, t, h, early: body(None, e, t, h, False))

        def ret_act(act, hf):
            load_exp_ln(act)

            def rstd(e, b):
                act.wait_ge(sem["r_mv"], e + 1)
                nc.scalar.activation(r_rsb[:, b, 0:1], r_mvb[:, b, 1:2], ACT.Ln, bias=eps_col[:, 0:1]
                                     ).then_inc(sem["r_lnv"], 1)
                act.wait_ge(sem["r_lnv"], e + 1)
                nc.scalar.activation(r_rsb[:, b, 1:2], r_rsb[:, b, 0:1], ACT.Exp, scale=-0.5
                                     ).then_inc(sem["r_rstd"], 1)

            def split_hi(e, g, h):
                act.wait_ge(sem["r_og"], e + 1)
                act.wait_ge(sem["r_tab_in"], 64)
                nc.scalar.activation(act_r[:, 4 * h:4 * h + 4, tile_cols(g)],
                                     r_ogb[:, h % 2, :].rearrange("p (q n) -> p q n", q=4), ACT.Copy
                                     ).then_inc(sem["r_hi"], 1)

            def body(k, e, t, h, early):
                b = h % 2
                if not in_last_tile(e):
                    act.wait_ge(sem["r_kT"], e + 1)
                    if not (hf == 0 and early and h < 2):
                        act.wait_ge(sem["r_u"], e - 1)
                    nc.scalar.activation(r_kdt[:, b, :], psum[:, b, 0:RET_DK], ACT.Copy, scale=ret_k[:, h:h + 1]
                                         ).then_inc(sem["r_kd"], 1)
                if not (early and h < 2):
                    split_hi(e - 2, tile_before(k, t, h, 2) - (0 if isinstance(k, int) else 4 * hf), (h - 2) % 4)
                if not (early and h < 1):
                    rstd(e - 1, 1 - b)
            if hf == 0:
                act.wait_ge(sem["r_tab_in"], 64)
            over_steps(act, hf, body)
            last = hf * RS + RS - 1
            split_hi(last - 1, 3, 2)
            rstd(last, 1)
            split_hi(last, 3, 3)

        def ret_dve(dve, hf):
            if hf == 0:
                dve.wait_ge(sem["state_zero"], 2)
                dve.wait_ge(sem["r_tab_in"], 64)

            def split_lo(e, g, h):
                b = h % 2
                dve.wait_ge(sem["r_hi"], e + 1)
                dve.wait_ge(sem["r_tab_in"], 64)
                dst = act_lo_r[:, 4 * h:4 * h + 4, tile_cols(g)]
                nc.vector.tensor_tensor(dst, r_ogb[:, b, :].rearrange("p (q n) -> p q n", q=4),
                                        act_r[:, 4 * h:4 * h + 4, tile_cols(g)].bitcast(F32),
                                        ALU.subtract).then_inc(sem["r_lo"], 1)

            def gate(e, t, h):
                b = h % 2
                dve.wait_ge(r_gate_in[h], 16 * t + 16)
                dve.wait_ge(sem["r_onT"], e + 1)
                if not (isinstance(e, int) and e < 2):
                    dve.wait_ge(sem["r_lo"], e - 1)
                nc.vector.tensor_tensor(r_ogb[:, b, :], psum[:, 6, :],
                                        r_x[:, h, 4:8, :].rearrange("p q n -> p (q n)"),
                                        ALU.mult).then_inc(sem["r_og"], 1)

            def outputs(e, h, no_on_wait):
                b = h % 2
                o = psum[:, 3 if b == 0 else 7, :]
                dve.wait_ge(sem["r_o"], e + 1)
                nc.vector.bn_stats(r_bst[:, b, 0:6], o).then_inc(sem["r_bn"], 1)
                dve.wait_ge(sem["r_tab_in"], 64)
                dve.wait_ge(sem["r_bn"], e + 1)
                nc.vector.bn_aggr(r_mvb[:, b, :], r_bst[:, b, 0:6]).then_inc(sem["r_mv"], 1)
                dve.wait_ge(sem["r_rstd"], e + 1)
                dve.wait_ge(sem["r_mv"], e + 1)
                if not no_on_wait:
                    dve.wait_ge(sem["r_onT"], e - 1)
                nc.vector.tensor_scalar(r_onb[:, b, :], o, r_mvb[:, b, 0:1], r_rsb[:, b, 1:2],
                                        ALU.subtract, ALU.mult).then_inc(sem["r_on"], 1)
                if in_last_tile(e):
                    return
                dve.wait_ge(sem["r_u"], e + 1)
                gamma_tile = (1.0 - 2.0 ** (-5.0 - h)) ** P
                for a in range(2):
                    nc.vector.scalar_tensor_tensor(r_st[:, h, a, :], r_st[:, h, a, :], gamma_tile,
                                                   psum[:, 4 + a, :], ALU.mult, ALU.add
                                                   ).then_inc(sem["r_state"], 1)

            def body(k, e, t, h, early):
                b = h % 2
                dve.wait_ge(sem["r_S"], e + 1)
                if not (hf == 0 and early and h < 2):
                    dve.wait_ge(sem["r_o"], e - 1)
                nc.vector.tensor_tensor(r_pt[:, b, :], psum[:, 2, 0:P], ret_dec[:, h, :], ALU.mult
                                        ).then_inc(sem["r_P"], 1)
                if not (early and h < 3):
                    split_lo(e - 3, tile_before(k, t, h, 3) - (0 if isinstance(k, int) else 4 * hf), (h - 3) % 4)
                if not (early and h < 2):
                    gate(e - 2, tile_before(k, t, h, 2) + (4 * hf if isinstance(k, int) else 0), (h - 2) % 4)
                if early and h == 1:
                    begin_phase(dve, 4 + 2 * hf)
                if not (early and h < 1):
                    outputs(e - 1, (h - 1) % 4, hf == 0 and early and h - 1 < 2)
            over_steps(dve, hf, body)
            last = hf * RS + RS - 1
            split_lo(last - 2, 3, 1)
            gate(last - 1, last // HEADS, 2)
            outputs(last, 3, False)
            split_lo(last - 1, 3, 2)
            gate(last, last // HEADS, 3)
            split_lo(last, 3, 3)

        def ret_pe(pe, hf):
            pe.wait_ge(sem["y_evac"], y_count[hf])
            if hf == 0:
                pe.wait_ge(sem["state_zero"], 2)

            def output(e, h):
                b = h % 2
                o = psum[:, 3 if b == 0 else 7, :]
                pe.wait_ge(sem["r_P"], e + 1)
                pe.wait_ge(sem["r_qd"], e + 1)
                first_tile = isinstance(e, int) and e < HEADS
                if not first_tile:
                    pe.wait_ge(sem["r_state"], 2 * e - 6)
                last = nc.tensor.matmul(o, r_pt[:, b, :], r_v[:, h, :], start=True, stop=first_tile)
                if not first_tile:
                    for a in range(2):
                        last = nc.tensor.matmul(o, r_qdb[:, h, a, :], r_st[:, h, a, :], start=False, stop=a == 1)
                last.then_inc(sem["r_o"], 1)
                if in_last_tile(e):
                    return
                pe.wait_ge(sem["r_kd"], e + 1)
                if not (isinstance(e, int) and e < 1):
                    pe.wait_ge(sem["r_state"], 2 * e)
                for a in range(2):
                    last = nc.tensor.matmul(psum[:, 4 + a, :], r_kdt[:, b, a * P:(a + 1) * P], r_v[:, h, :],
                                            start=True, stop=True)
                last.then_inc(sem["r_u"], 1)

            def out_transposes(e, h):
                pe.wait_ge(sem["r_on"], e + 1)
                if not (isinstance(e, int) and e < 1):
                    pe.wait_ge(sem["r_og"], e)
                for q in range(4):
                    last = nc.tensor.transpose(psum[:, 6, q * P:(q + 1) * P],
                                               r_onb[:, h % 2, q * P:(q + 1) * P], ident[:, :])
                last.then_inc(sem["r_onT"], 1)

            def body(k, e, t, h, early):
                b = h % 2
                start = hf == 0 and early and h == 0
                pe.wait_ge(r_in[h], 32 * t + 32)
                pe.wait_ge(sem["r_rope"], 2 * e + 2)
                if not in_last_tile(e):
                    if not (hf == 0 and early and h < 2):
                        pe.wait_ge(sem["r_kd"], e - 1)
                    for a in range(2):
                        last = nc.tensor.transpose(psum[:, b, a * P:(a + 1) * P], r_qk[:, h, 2 + a, :], ident[:, :])
                    last.then_inc(sem["r_kT"], 1)
                if not start:
                    pe.wait_ge(sem["r_P"], e)
                for a in range(2):
                    last = nc.tensor.matmul(psum[:, 2, 0:P], r_qk[:, h, 2 + a, :], r_qk[:, h, a, :],
                                            start=a == 0, stop=a == 1)
                last.then_inc(sem["r_S"], 1)
                if not (early and h < 2):
                    out_transposes(e - 2, (h - 2) % 4)
                if not (early and h < 1):
                    output(e - 1, (h - 1) % 4)
            over_steps(pe, hf, body)
            last = hf * RS + RS - 1
            out_transposes(last - 1, 2)
            output(last, 3)
            out_transposes(last, 3)
            pe.wait_ge(sem["r_lo"], last + 1)

        def yret_pe(pe, hf):
            groups = 2 * KT // RING
            def group(g):
                for jj in range(RING):
                    n0 = SL_YRET + hf * 2 * KT + jj
                    kh, b = jj % 2, jj // 2
                    n = g * RING + n0
                    j = n0 % RING
                    pe.wait_ge(sem["slab_ready"], n + 1)
                    if kh == 0 and not (isinstance(g, int) and g == 0):
                        pe.wait_ge(sem["y_evac"], 2 * g + (y_count[hf] + b - 1))
                    for kk in range(KT):
                        sl = slice((kh * KT + kk) * HALF, (kh * KT + kk + 1) * HALF)
                        last = product3(psum[:, b, :], w_hi[:, j, kk * P:(kk + 1) * P],
                                        w_lo[:, j, kk * P:(kk + 1) * P], act_hi[:, sl], act_lo[:, sl],
                                        kh == 0 and kk == 0, kh == 1 and kk == KT - 1)
                        if kk % 4 == 3:
                            last.then_inc(sem["mm_half"], 1)
            group(0)
            with pe.Fori(1, groups) as g:
                group(g)

        def yret_sp(sp, hf):
            begin_phase(sp, 5 + 2 * hf)
            cols = slice(hf * HALF, hf * HALF + HALF)

            def loads(c, s, slot):
                if not (isinstance(c, int) and c < 2):
                    sp.wait_ge(sem["y_evac"], s - 1)
                sp.dma_start(y_in[:, slot % 2, 0:HALF], proj_d[c + ROW_AR, :, cols]).then_inc(y_ins[slot], 16)
                sp.dma_start(y_in[:, slot % 2, HALF:], gla_d[c, :, cols]).then_inc(y_ins[slot], 16)

            def out_store(c, s, slot):
                sp.wait_ge(sem["y_evac"], s + 1)
                sp.dma_start(merged_d[c, :, cols], y_out[:, slot % 2, 0:HALF]).then_inc(y_st[slot], 16)

            lo = y_count[hf]
            loads(0, lo, 0)
            for c in range(KT):
                if c == 2 and hf == 0:
                    for h in range(HEADS):
                        ret_step_loads(sp, RS + h, RS // HEADS, h, False)
                if c == 2 and hf == 1:
                    dense_first_loads(sp, 0, 0, merged_d, x, ln_post_mix)
                if c + 1 < KT:
                    loads(c + 1, lo + c + 1, (c + 1) % RING)
                if c:
                    out_store(c - 1, lo + c - 1, (c - 1) % RING)
                for n in range(SL_YRET + 2 * (hf * KT + c), SL_YRET + 2 * (hf * KT + c) + 2):
                    if c < KT - RING // 2:
                        stream_step(sp, n, n % RING)
            out_store(KT - 1, lo + KT - 1, RING - 1)
            for j in range(RING):
                sp.wait_ge(y_st[j], 16 * (lo + KT) // RING)
            if hf == 1:
                for n in range(SL_MIX - RING, SL_MIX):
                    stream_step(sp, n, n % RING)

        def yret_dve(dve, hf):
            begin_phase(dve, 5 + 2 * hf)

            def body(c, s, grp, slot, early):
                b = slot % 2
                n = 2 * c + (SL_YRET + hf * 2 * KT + 1)
                dve.wait_ge(sem["mm_half"], 2 * n + 2)
                dve.wait_ge(y_ins[slot], 32 * grp - 16 * (KT // RING) + 32)
                if not (early and slot < 2):
                    wait_y_out(dve, grp, slot)
                nc.vector.tensor_tensor(y_out[:, b, 0:HALF], psum[:, b, :], y_in[:, b, 0:HALF], ALU.mult
                                        ).then_inc(sem["y_mul"], 1)
                dve.wait_ge(sem["y_mul"], s - KT + 1)
                nc.vector.tensor_tensor(y_out[:, b, 0:HALF], y_out[:, b, 0:HALF], y_in[:, b, HALF:], ALU.add
                                        ).then_inc(sem["y_evac"], 1)
            repeat(dve, y_count[hf], KT, body)

        def piece(sp, src, k, hf, slot):
            sp.dma_start(d_raw[:, slot, :], src[k, :, hf * HALF:hf * HALF + HALF]).then_inc(d_in[slot], 16)

        def dense_first_loads(sp, job, q0, src, res, ln):
            for k in range(RING):
                if job:
                    sp.wait_ge(sem["d_lo"], q0)
                piece(sp, src, k, 0, (q0 + k) % RING)
            sp.dma_start(d_ln[:, :], ln.to_broadcast((P, D))).then_inc(sem["d_ln_in"], 16)
            residual_rows(sp, res, 0)

        def residual_rows(sp, res, hf):
            sp.dma_start(d_x[:, :, :], res[hf * HALF:hf * HALF + HALF, :].rearrange("(t p) d -> p t d", p=P)
                         ).then_inc(sem["d_x_in"], 16)

        def dense_sp(sp, job, K, n0, q0, src, res, dst):
            loading = N_SLABS - n0 - 2 * RING

            def step(s, q, slot, hf, next_k):
                if next_k is not None:
                    sp.wait_ge(sem["d_lo"], q + 1)
                    piece(sp, src, next_k, hf, slot)
                if hf == 0 or not isinstance(s, int) or s < loading:
                    stream_step(sp, s + n0, (slot + n0 - q0) % RING)

            repeat(sp, q0, K - RING, lambda k, q, grp, slot, early: step(k, q, slot, 0, k + RING))
            for k in range(RING):
                step(K - RING + k, q0 + K - RING + k, (q0 + K + k) % RING, 1, k)
            base = q0 + K
            looped = min(K - RING, loading - K)
            repeat(sp, base, looped, lambda k, q, grp, slot, early: step(k + K, q, slot, 1, k + RING))
            for k in range(looped, K):
                step(K + k, base + k, (base + k) % RING, 1, k + RING if k + RING < K else None)
                if k == K - RING - 1:
                    half_0_done(sp, job, res, dst)
            if looped == K - RING:
                half_0_done(sp, job, res, dst)
            store(sp, job, 1, dst)
            sp.wait_ge(sem["d_stored"], 16 * (4 if job == 0 else 12))
            sp.wait_ge(sem["x1_stored"], 16 * 4)

        def half_0_done(sp, job, res, dst):
            if job:
                store(sp, job, 0, dst)
            sp.wait_ge(sem["d_res"], NT * job + 4)
            residual_rows(sp, res, 1)

        def store(sp, job, hf, dst):
            for tok in range(4):
                t = 4 * hf + tok
                sp.wait_ge(sem["d_res"], NT * job + t + 1)
                sp.dma_start(dst[t * P:(t + 1) * P, :], d_out[:, t, :]).then_inc(sem["d_stored"], 16)

        def dense_pe(pe, job, K, n0, q0, banks_free):
            for hf in range(2):
                def body(k, q, grp, slot, early):
                    j = (slot + n0 - q0) % RING
                    pe.wait_ge(sem["slab_ready"], k + (n0 + hf * K + 1))
                    pe.wait_ge(sem["d_lo"], q + 1)
                    start = isinstance(k, int) and k == 0
                    stop = isinstance(k, int) and k == K - 1
                    for tok in range(4):
                        if start and hf:
                            pe.wait_ge(sem["d_evac"], NT * job + tok + 1)
                        elif start:
                            banks_free(pe, tok)
                        s_hi = d_hib[:, slot, tok * P:(tok + 1) * P]
                        s_lo = d_lob[:, slot, tok * P:(tok + 1) * P]
                        for cc in range(2):
                            last = product3(psum[:, 2 * tok + cc, :], s_hi, s_lo,
                                            w_hi[:, j, cc * HALF:(cc + 1) * HALF],
                                            w_lo[:, j, cc * HALF:(cc + 1) * HALF], start, stop)
                        if tok % 2:
                            last.then_inc(sem["mm_half"], 1)
                repeat(pe, q0 + hf * K, K, body)

        def over_pieces(eng, lo, count, k0, body):
            repeat(eng, lo, count, lambda k, q, grp, slot, early: body(k, k + k0, q, grp, slot, k0 == 0 and early))

        def split_hi_pieces(act, job, n0, q0, k0, count):
            def split(k, s, q, grp, slot, start):
                act.wait_ge(d_in[slot], 16 * grp + 16)
                if not start:
                    act.wait_ge(sem["mm_half"], 2 * s + 2 * (n0 - RING) + 2)
                elif job:
                    act.wait_ge(sem["mm_half"], 2 * SL_UP)
                nc.scalar.activation(d_hib[:, slot, :], d_raw[:, slot, :], ACT.Copy
                                     ).then_inc(sem["d_hi"], 1)
            over_pieces(act, q0 + k0, count, k0, split)

        def split_lo_pieces(dve, q0, k0, count):
            def split(k, s, q, grp, slot, start):
                dve.wait_ge(sem["d_hi"], q + 1)
                nc.vector.tensor_tensor(d_lob[:, slot, :], d_raw[:, slot, :], d_hib[:, slot, :].bitcast(F32),
                                        ALU.subtract).then_inc(sem["d_lo"], 1)
            over_pieces(dve, q0 + k0, count, k0, split)

        def dense_act(act, job, K, n0, q0):
            def tail(hf):
                for tok in range(4):
                    t = 4 * hf + tok
                    act.wait_ge(sem["mm_half"], 2 * (n0 + hf * K + K) - (tok < 2))
                    if job or t:
                        act.wait_ge(sem["d_sq"], NT * job + t)
                    nc.scalar.activation(d_junk[:, :], pair_view(tok), ACT.Square,
                                         accum_out=stat[:, 24 + t:25 + t]).then_inc(sem["d_sq"], 1)
                    act.wait_ge(sem["d_sq"], NT * job + t + 1)
                    nc.scalar.activation(stat[:, 32 + t:33 + t], stat[:, 24 + t:25 + t], ACT.Sqrt, scale=1.0 / D,
                                         bias=eps_col[:, 0:1]).then_inc(sem["d_std"], 1)

            if job == 0:
                split_hi_pieces(act, job, n0, q0, 0, RING)
            split_hi_pieces(act, job, n0, q0, RING, K - 1)
            tail(0)
            split_hi_pieces(act, job, n0, q0, K + RING - 1, K - RING + 1)
            if job == 0:
                norm2_squares(act, 0)
            tail(1)
            if job == 0:
                norm_hi(act, 1, range(KT))
                norm2_squares(act, 1)
                norm_hi(act, 1, range(KT, 2 * KT))

        def dense_dve(dve, job, K, n0, q0):
            def evacuate(hf):
                for tok in range(4):
                    dve.wait_ge(sem["d_sq"], NT * job + 4 * hf + tok + 1)
                    nc.vector.tensor_copy(d_out[:, 4 * hf + tok, :], pair_view(tok)).then_inc(sem["d_evac"], 1)

            def tail(hf):
                dve.wait_ge(sem["d_ln_in"], 16 * job + 16)
                dve.wait_ge(sem["d_x_in"], 16 * (2 * job + hf) + 16)
                for tok in range(4):
                    t = 4 * hf + tok
                    dve.wait_ge(sem["d_std"], NT * job + t + 1)
                    nc.vector.reciprocal(stat[:, 40 + t:41 + t], stat[:, 32 + t:33 + t]).then_inc(sem["d_rstd"], 1)
                    dve.wait_ge(sem["d_rstd"], NT * job + t + 1)
                    direct = job and hf
                    if not direct:
                        dve.wait_ge(sem["d_evac"], NT * job + t + 1)
                    nc.vector.scalar_tensor_tensor(d_out[:, t, :], pair_view(tok) if direct else d_out[:, t, :],
                                                   stat[:, 40 + t:41 + t], d_ln[:, :],
                                                   ALU.mult, ALU.mult).then_inc(sem["d_scaled"], 1)
                    dve.wait_ge(sem["d_scaled"], NT * job + t + 1)
                    nc.vector.tensor_tensor(d_out[:, t, :], d_out[:, t, :], d_x[:, tok, :], ALU.add
                                            ).then_inc(sem["d_res"], 1)

            if job == 0:
                split_lo_pieces(dve, q0, 0, RING)
            split_lo_pieces(dve, q0, RING, K - 1)
            begin_phase(dve, 8 if job == 0 else 10)
            evacuate(0)
            split_lo_pieces(dve, q0, K + RING - 1, 1)
            tail(0)
            split_lo_pieces(dve, q0, K + RING, K - RING)
            if job == 0:
                norm2_scale(dve, 0)
            if job == 0:
                evacuate(1)
                norm_lo(dve, 1, range(KT))
            tail(1)
            if job == 0:
                norm2_scale(dve, 1)
                norm_lo(dve, 1, range(KT, 2 * KT))

        def norm2_squares(act, hf):
            for tok in range(4):
                t = 4 * hf + tok
                act.wait_ge(sem["d_res"], t + 1)
                if hf == 0:
                    act.dma_start(x1_d[t * P:(t + 1) * P, :], d_out[:, t, :]).then_inc(sem["x1_stored"], 16)
                if t:
                    act.wait_ge(sem["n_sq"], t)
                act.wait_ge(sem["d_sq"], 4 + 4 * hf)
                nc.scalar.activation(d_junk[:, :], d_out[:, t, :], ACT.Square,
                                     accum_out=stat[:, t:t + 1]).then_inc(sem["n_sq"], 1)
            act.wait_ge(sem["n_sq"], 4 * hf + 4)
            nc.scalar.activation(stat[:, 8 + 4 * hf:12 + 4 * hf], stat[:, 4 * hf:4 * hf + 4], ACT.Sqrt,
                                 scale=1.0 / D, bias=eps_col[:, 0:1]).then_inc(sem["rms_std"], 1)

        def norm2_scale(dve, hf):
            dve.wait_ge(sem["rms_std"], 2 + hf + 1)
            nc.vector.reciprocal(stat[:, 16 + 4 * hf:20 + 4 * hf], stat[:, 8 + 4 * hf:12 + 4 * hf]
                                 ).then_inc(sem["rms_rstd"], 1)
            dve.wait_ge(sem["rms_rstd"], 2 + hf + 1)
            if hf == 0:
                dve.wait_ge(sem["x1_stored"], 16 * 4)
            else:
                dve.wait_ge(sem["d_res"], NT)
            for tok in range(4):
                t = 4 * hf + tok
                nc.vector.tensor_scalar(d_out[:, t, :] if hf == 0 else d_x[:, tok, :], d_out[:, t, :],
                                        stat[:, 16 + t:17 + t], None, ALU.mult).then_inc(sem["x_scaled"], 1)

        def norm2_transposes(pe, hf):
            for i in range(hf * KT, hf * KT + KT):
                k = i % KT
                pe.wait_ge(sem["x_scaled"], NT + 4 * hf + 4)
                if hf == 0:
                    pe.wait_ge(sem["d_evac"], 4 + i // 2 + 1)
                else:
                    pe.wait_ge(sem["act_lo_done"], 2 * KT + (KT if i < KT + 4 else i - 3))
                for q in range(4):
                    src = d_out[:, q, k * P:(k + 1) * P] if hf == 0 else d_x[:, q, k * P:(k + 1) * P]
                    last = nc.tensor.transpose(psum[:, norm_bank(1, i), q * P:(q + 1) * P], src, ident[:, :])
                last.then_inc(sem["x_transposed"], 1)

        def up_sp(sp):
            def pair(p, s, grp, slot, early):
                for i in range(2):
                    n = 2 * p + (SL_UP + i)
                    stream_step(sp, n, (SL_UP + 2 * slot + i) % RING)
                sp.wait_ge(sem["u_f"], p + 1)
                sp.dma_start(f_d[p, :, :], u_fb[:, slot, :]).then_inc(stored[slot], 16)
            begin_phase(sp, 9)
            repeat(sp, 0, FT - 1, pair)
            for j in range(RING):
                sp.wait_ge(stored[j], 16 * PROJ_STORES + 16)
            dense_first_loads(sp, 1, 2 * KT, f_d, x1_d, ln_post_ffn)
            pair(FT - 1, FT - 1, (FT - 1) // RING, (FT - 1) % RING, False)
            for j in range(RING):
                sp.wait_ge(stored[j], 16 * PROJ_STORES + 16 * len(range(j, FT, RING)))

        def up_act(act):
            begin_phase(act, 9)
            def pair(p, s, grp, b, early):
                for i in range(2):
                    k = 2 * p + i
                    act.wait_ge(sem["mm_half"], 2 * k + 2 * SL_UP + 2)
                    if not early:
                        act.wait_ge(sem["u_f"], p - 1)
                    act.wait_ge(sem["const_in"], 64)
                    nc.scalar.activation(u_conv[:, 2 * b + i, :], pair_view(2 * b + i), ACT.Identity,
                                         scale=col(k, 2), bias=col(k, 3)).then_inc(sem["u_lin"], 1)
                act.wait_ge(sem["u_tap0"], 2 * p + 2)
                nc.scalar.activation(u_conv[:, 2 * b + 1, :], u_conv[:, 2 * b + 1, :], ACT.Gelu_apprx_tanh
                                     ).then_inc(sem["u_gelu"], 1)
            repeat(act, 0, FT - 1, pair, unroll=2)
            split_hi_pieces(act, 1, SL_DOWN, 2 * KT, 0, RING)
            pair(FT - 1, FT - 1, (FT - 1) // 2, (FT - 1) % 2, False)

        def col(k, tap):
            return conv_col[:, 4 * k + tap:4 * k + tap + 1] if isinstance(k, int) else \
                conv_col[:, bass.ds(4 * k + tap, 1)]

        def up_dve(dve):
            begin_phase(dve, 9)
            def pair(p, s, grp, slot, early):
                for i in range(2):
                    k = 2 * p + i
                    b = (2 * slot + i) % RING
                    dve.wait_ge(sem["u_lin"], k + 1)
                    dve.wait_ge(sem["const_in"], 64)
                    nc.vector.scalar_tensor_tensor(u_conv[:, b, 1:], pair_view(b)[:, 0:SEQ - 1], col(k, 1),
                                                   u_conv[:, b, 1:], ALU.mult, ALU.add
                                                   ).then_inc(sem["u_tap1"], 1)
                    dve.wait_ge(sem["u_tap1"], k + 1)
                    dve.wait_ge(sem["const_in"], 64)
                    nc.vector.scalar_tensor_tensor(u_conv[:, b, 2:], pair_view(b)[:, 0:SEQ - 2], col(k, 0),
                                                   u_conv[:, b, 2:], ALU.mult, ALU.add
                                                   ).then_inc(sem["u_tap0"], 1)
                if not early:
                    dve.wait_ge(stored[slot], 16 * PROJ_STORES + 16 * grp)
                dve.wait_ge(sem["u_gelu"], p + 1)
                b = (2 * slot) % RING
                nc.vector.tensor_tensor(u_fb[:, slot, :], u_conv[:, b, :], u_conv[:, b + 1, :], ALU.mult
                                        ).then_inc(sem["u_f"], 1)
            repeat(dve, 0, FT - 1, pair)
            split_lo_pieces(dve, 2 * KT, 0, RING)
            pair(FT - 1, FT - 1, (FT - 1) // RING, (FT - 1) % RING, False)

        def up_pe(pe):
            for k in range(RING):
                pe.wait_ge(sem["slab_ready"], SL_UP + k + 1)
                pe.wait_ge(sem["act_lo_done"], 3 * KT)
                half_product((SL_UP + k) % RING, k, 0)
            norm2_transposes(pe, 1)
            end_phase(pe, "pe")
            pe.wait_ge(sem["act_lo_done"], 4 * KT)
            for k in range(RING):
                half_product((SL_UP + k) % RING, k, 1).then_inc(sem["mm_half"], 2)

            def body(k, n, grp, j, early):
                pe.wait_ge(sem["u_tap0"], k + 1)
                slab_product(pe, n, j, (j - SL_UP) % RING)
            repeat(pe, SL_UP + RING, 2 * FT - RING, body)

        block = ctx.enter_context(nc.Block())
        MIX = dict(job=0, K=KT, n0=SL_MIX, q0=0)
        DOWN = dict(job=1, K=FT, n0=SL_DOWN, q0=2 * KT)

        def mix_banks_free(pe, tok):
            if tok == 0:
                pe.wait_ge(sem["y_evac"], 3 * KT)

        def down_banks_free(pe, tok):
            pe.wait_ge(sem["u_tap0"], 2 * FT - RING + tok + 1)

        @block.sync
        def _(sp):
            sp.dma_start(ident[:, :], ident_in).then_inc(sem["const_in"], 16)
            sp.dma_start(ln_col[:, :, :], ln_cols_in).then_inc(sem["const_in"], 16)
            sp.dma_start(conv_col[:, :], conv_in).then_inc(sem["const_in"], 16)
            sp.dma_start(eps_col[:, :], eps_in).then_inc(sem["const_in"], 16)
            norm_sp(sp)
            stream_prologue(sp)
            sp.sem_inc(sem["sp_phases"], 1)
            begin_phase(sp, 1)
            for phase in (proj_sp, gla_sp, ygla_sp, lambda e: ret_sp(e, 0), lambda e: yret_sp(e, 0),
                          lambda e: ret_sp(e, 1), lambda e: yret_sp(e, 1),
                          lambda e: dense_sp(e, **MIX, src=merged_d, res=x, dst=x1_d), up_sp,
                          lambda e: dense_sp(e, **DOWN, src=f_d, res=x1_d, dst=out)):
                phase(sp)
                sp.sem_inc(sem["sp_phases"], 1)

        @block.tensor
        def _(pe):
            pe.wait_ge(sem["const_in"], 64)
            for phase in (proj_pe, gla_pe, ygla_pe, lambda e: ret_pe(e, 0), lambda e: yret_pe(e, 0),
                          lambda e: ret_pe(e, 1), lambda e: yret_pe(e, 1)):
                phase(pe)
                end_phase(pe, "pe")
            dense_pe(pe, **MIX, banks_free=mix_banks_free)
            norm2_transposes(pe, 0)
            up_pe(pe)
            end_phase(pe, "pe")
            dense_pe(pe, **DOWN, banks_free=down_banks_free)

        @block.scalar
        def _(act):
            for phase in (norm_act, lambda e: (begin_phase(e, 1), proj_act(e)), gla_act, lambda e: None,
                          lambda e: ret_act(e, 0), lambda e: None, lambda e: ret_act(e, 1), lambda e: None,
                          lambda e: dense_act(e, **MIX), up_act, lambda e: dense_act(e, **DOWN)):
                phase(act)
                end_phase(act, "act")

        @block.vector
        def _(dve):
            dve.wait_ge(sem["const_in"], 64)
            for phase in (norm_dve, lambda e: (begin_phase(e, 1), proj_dve(e)), gla_dve, ygla_dve,
                          lambda e: ret_dve(e, 0), lambda e: yret_dve(e, 0), lambda e: ret_dve(e, 1),
                          lambda e: yret_dve(e, 1), lambda e: dense_dve(e, **MIX), up_dve,
                          lambda e: dense_dve(e, **DOWN)):
                phase(dve)
                end_phase(dve, "dve")

        @block.gpsimd
        def _(pool):
            nc.gpsimd.memset(zero_col[:, :], 0.0).then_inc(sem["zero_set"], 1)
            pool.wait_ge(sem["zero_set"], 1)
            split_slabs(pool, 0, SL_YGLA)
            gla_pool(pool)
            split_slabs(pool, SL_YGLA + RING, SL_YRET)
            ret_pool(pool, 0)
            split_slabs(pool, SL_YRET + RING, SL_YRET + 2 * KT)
            ret_pool(pool, 1)
            split_slabs(pool, SL_YRET + 2 * KT + RING, N_SLABS)


def kernel(**inputs):
    import numpy as _np
    import concourse.bacc as _bacc
    from concourse import mybir as _mybir
    from concourse.bass_utils import run_bass_kernel_spmd as _run

    a = {k: _np.asarray(v) for k, v in inputs.items()}

    def slabs(w, cols=None):
        cols = range(0, w.shape[1], P) if cols is None else cols
        return [w[:, c:c + P].reshape(KT, P, P).transpose(1, 0, 2).reshape(P, D) for c in cols]

    w_in, w_up, w_down = a["w_in"][0], a["w_ffn_up"][0], a["w_ffn_down"][0]
    w_ret, w_mix = a["w_ret_out"][0], a["w_mix_out"][0]
    lr = _np.zeros((D, P), _np.float32)
    lr[:, :GLA_RANK] = w_in[:, O_LR:O_LR + GLA_RANK]
    ret = [s for c in range(KT) for kh in range(2)
           for s in slabs(w_ret[kh * D:(kh + 1) * D], [c * P])]
    rows = lambda w: [w[k * P:(k + 1) * P] for k in range(w.shape[0] // P)]
    values = [w_in[2 * i * P:(2 * i + 2) * P, c:c + HALF].reshape(2, P, HALF).transpose(1, 0, 2).reshape(P, D)
              for c in value_columns() for i in range(4)]
    stream = (values + slabs(lr) + slabs(w_in, projection_columns()) + slabs(a["w_gla_out"][0]) + ret + ret
              + rows(w_mix) + rows(w_mix)
              + slabs(w_up, [v for p in range(FT) for v in (p * P, D_FF + p * P)])
              + rows(w_down) + rows(w_down))
    w_stream = _np.stack(stream)
    assert w_stream.shape[0] == N_SLABS
    pair_cols = [v for p in range(FT) for v in (p * P, D_FF + p * P)]
    taps = _np.concatenate([a["conv_w"][0], a["conv_b"]], 0)
    conv = _np.stack([taps[:, c:c + P] for c in pair_cols]).transpose(2, 0, 1).reshape(P, -1)
    ln_cols = _np.stack([a["ln_pre_mix"][0].reshape(KT, P).T, a["ln_pre_ffn"][0].reshape(KT, P).T], 1)
    ret_dec, ret_q, ret_k = retention_tables()
    inv_freq = (10000.0 ** (-_np.arange(0, RET_DK, 2) / RET_DK)).astype(_np.float32).reshape(P, 1)
    feeds = {
        "x": a["x"][0], "positions": a["positions"], "w_stream": w_stream, "w_dec": a["w_gla_decay"][0],
        "b_dec": a["b_gla_decay"], "ln_post_mix": a["ln_post_mix"], "ln_post_ffn": a["ln_post_ffn"],
        "ln_cols_in": ln_cols, "conv_in": conv, "ident_in": _np.eye(P, dtype=_np.float32),
        "interval_in": interval_table(), "masks_in": level_masks(), "ret_dec_in": ret_dec,
        "ret_q_in": ret_q, "ret_k_in": ret_k, "inv_freq_in": inv_freq,
        "eps_in": _np.full((P, 1), EPS, _np.float32),
    }
    nc = _bacc.Bacc("TRN2", target_bir_lowering=False, num_devices=1)
    arrays, args = {}, {}
    for name, v in feeds.items():
        v = _np.ascontiguousarray(v)
        arrays[f"in_{name}"] = v
        args[name] = nc.dram_tensor(f"in_{name}", v.shape, _mybir.dt.from_np(v.dtype), kind="ExternalInput").ap()
    out = nc.dram_tensor("out_0", (SEQ, D), F32, kind="ExternalOutput").ap()
    build(nc, out=out, **args)
    r = _run(nc, [arrays], core_ids=[0])
    return _np.asarray(r.results[0]["out_0"]).reshape(a["x"].shape)
```
